# Optimizing a Trainium2 kernel written in Bass

```python
import math
import jax
import jax.numpy as jnp
from jax import lax
import numpy as np
import jax, jax.numpy as jnp

D_MODEL = 1024
BATCH = 1
SEQ = 512
DEPTH = 1

CHUNK = 64
D_MIX = D_MODEL
HEAD_DIM = 64
D_RWKV = D_MIX // 2
D_SB = D_MIX - D_RWKV
H_RWKV = D_RWKV // HEAD_DIM
H_SB = D_SB // HEAD_DIM
DECAY_LORA = 64
ICLR_LORA = 64
GATE_LORA = 128
VRES_LORA = 32
C_RWKV = 3 * D_RWKV + DECAY_LORA + ICLR_LORA + GATE_LORA
C_IN = C_RWKV + 3 * D_SB
SB_BLOCK = 128
N_EXPERTS = 32
TOP_K = 4
D_FF_EXPERT = D_MODEL
SWIGLU_ALPHA = 1.702
SWIGLU_LIMIT = 7.0
MOE_BLOCK = 128
NORM_EPS = 1e-6
GN_EPS = 1e-5 * HEAD_DIM
L2_EPS = 1e-12


def rms_norm(x, g):
    xf = x.astype(jnp.float32)
    y = xf * lax.rsqrt(jnp.mean(jnp.square(xf), axis=-1, keepdims=True) + NORM_EPS)
    return (y * g.astype(jnp.float32)).astype(x.dtype)

def token_shift(z, mu):
    z_prev = jnp.pad(z[:, :-1], ((0, 0), (1, 0), (0, 0)))
    return z + (z_prev - z) * mu

def split_heads(t, n_heads):
    bsz, seq, _ = t.shape
    return t.reshape(bsz, seq, n_heads, HEAD_DIM)

def rwkv7_recurrence(r, decay, k, v, kk, a):
    bsz, seq, nh, hd = r.shape
    n_chunks = seq // CHUNK

    def to_chunks(t):
        return jnp.transpose(t, (1, 0, 2, 3)).reshape(n_chunks, CHUNK, bsz, nh, hd)

    def step(state, inp):
        r_t, w_t, k_t, v_t, kk_t, a_t = inp
        s_kk = jnp.einsum('bhvk,bhk->bhv', state, kk_t)
        state = (state * w_t[:, :, None, :]
                 - s_kk[..., None] * (kk_t * a_t)[:, :, None, :]
                 + v_t[..., None] * k_t[:, :, None, :])
        return state, jnp.einsum('bhvk,bhk->bhv', state, r_t)

    def chunk_step(state, chunk):
        return lax.scan(step, state, chunk)

    s0 = jnp.zeros((bsz, nh, hd, hd), jnp.float32)
    xs = tuple(to_chunks(t) for t in (r, decay, k, v, kk, a))
    _, y = lax.scan(chunk_step, s0, xs)
    return jnp.transpose(y.reshape(seq, bsz, nh, hd), (1, 0, 2, 3))

def rwkv7_time_mix(z, v_first, mu, decay_w0, decay_up, iclr_a0, iclr_up, gate_up,
                   k_k, k_a, r_k, lnx_w, lnx_b, vres):
    bsz, seq, _ = z.shape
    zs = token_shift(z, mu)
    r = zs[..., :D_RWKV]
    k = zs[..., D_RWKV:2 * D_RWKV]
    v = zs[..., 2 * D_RWKV:3 * D_RWKV]
    o = 3 * D_RWKV
    w_lo = zs[..., o:o + DECAY_LORA]
    a_lo = zs[..., o + DECAY_LORA:o + DECAY_LORA + ICLR_LORA]
    g_lo = zs[..., o + DECAY_LORA + ICLR_LORA:]
    w_pre = (decay_w0 + jnp.tanh(w_lo) @ decay_up).astype(jnp.float32)
    log_decay = -jnp.exp(-jax.nn.softplus(-w_pre) - 0.5)
    a = jax.nn.sigmoid(iclr_a0 + a_lo @ iclr_up)
    g = jax.nn.sigmoid(g_lo) @ gate_up
    if vres is None:
        v_first = v
    else:
        vres_down, vres_up, vres_b = vres
        v = v + (v_first - v) * jax.nn.sigmoid(vres_b + (v @ vres_down) @ vres_up)
    kk = split_heads((k * k_k).astype(jnp.float32), H_RWKV)
    kk = kk / jnp.maximum(jnp.sqrt(jnp.sum(jnp.square(kk), axis=-1, keepdims=True)), L2_EPS)
    k = k * (1.0 + (a - 1.0) * k_a)
    rh = split_heads(r.astype(jnp.float32), H_RWKV)
    kh = split_heads(k.astype(jnp.float32), H_RWKV)
    vh = split_heads(v.astype(jnp.float32), H_RWKV)
    ah = split_heads(a.astype(jnp.float32), H_RWKV)
    wh = split_heads(jnp.exp(log_decay), H_RWKV)
    y = rwkv7_recurrence(rh, wh, kh, vh, kk, ah)
    mean = jnp.mean(y, axis=-1, keepdims=True)
    var = jnp.mean(jnp.square(y - mean), axis=-1, keepdims=True)
    y = ((y - mean) * lax.rsqrt(var + GN_EPS)).reshape(bsz, seq, D_RWKV)
    y = y * lnx_w.astype(jnp.float32) + lnx_b.astype(jnp.float32)
    bonus = jnp.sum(rh * kh * r_k.astype(jnp.float32), axis=-1, keepdims=True) * vh
    out = (y + bonus.reshape(bsz, seq, D_RWKV)) * g.astype(jnp.float32)
    return out.astype(z.dtype), v_first

def stick_breaking_attention(q, k, v, q_norm_g, k_norm_g, out_g):
    bsz, seq, _ = q.shape
    qh = jnp.transpose(rms_norm(split_heads(q, H_SB), q_norm_g).astype(jnp.float32), (0, 2, 1, 3))
    kh = jnp.transpose(rms_norm(split_heads(k, H_SB), k_norm_g).astype(jnp.float32), (0, 2, 1, 3))
    vh = jnp.transpose(split_heads(v, H_SB).astype(jnp.float32), (0, 2, 1, 3))
    scale = 1.0 / math.sqrt(HEAD_DIM)
    blocks = []
    for blk in range(seq // SB_BLOCK):
        t0 = blk * SB_BLOCK
        t1 = t0 + SB_BLOCK
        logits = jnp.einsum('bhqd,bhkd->bhqk', qh[:, :, t0:t1], kh[:, :, :t1]) * scale
        mask = jnp.arange(t1)[None, :] < jnp.arange(t0, t1)[:, None]
        log_keep = jnp.where(mask, jax.nn.log_sigmoid(-logits), 0.0)
        log_between = lax.cumsum(log_keep, axis=3, reverse=True) - log_keep
        weight = jnp.where(mask, jnp.exp(jax.nn.log_sigmoid(logits) + log_between), 0.0)
        blocks.append(jnp.einsum('bhqk,bhkd->bhqd', weight, vh[:, :, :t1]))
    o = jnp.transpose(jnp.concatenate(blocks, axis=2), (0, 2, 1, 3))
    o = rms_norm(o, out_g.reshape(H_SB, HEAD_DIM))
    return o.reshape(bsz, seq, D_SB).astype(q.dtype)

def moe_ffn(h, router_w, router_b, w1, b1, w2, b2):
    bsz, seq, d = h.shape
    n_tok = bsz * seq
    xt = h.reshape(n_tok, d)
    logits = xt.astype(jnp.float32) @ router_w.astype(jnp.float32) + router_b.astype(jnp.float32)
    top_logit, top_idx = lax.top_k(logits, TOP_K)
    top_gate = jax.nn.softmax(top_logit, axis=-1)
    n_assign = n_tok * TOP_K
    flat_e = top_idx.reshape(-1)
    flat_tok = jnp.arange(n_assign, dtype=jnp.int32) // TOP_K
    order = jnp.argsort(flat_e, stable=True)
    e_sorted = flat_e[order]
    counts = jnp.bincount(flat_e, length=N_EXPERTS)
    padded = (counts + MOE_BLOCK - 1) // MOE_BLOCK * MOE_BLOCK
    padded_end = jnp.cumsum(padded)
    padded_start = padded_end - padded
    start = jnp.cumsum(counts) - counts
    dest = padded_start[e_sorted] + jnp.arange(n_assign, dtype=jnp.int32) - start[e_sorted]
    n_rows = n_assign + N_EXPERTS * MOE_BLOCK
    n_blocks = n_rows // MOE_BLOCK
    row_tok = jnp.zeros((n_rows,), jnp.int32).at[dest].set(flat_tok[order])
    row_gate = jnp.zeros((n_rows,), h.dtype).at[dest].set(top_gate.reshape(-1)[order].astype(h.dtype))
    block_expert = jnp.minimum(
        jnp.searchsorted(padded_end, jnp.arange(n_blocks, dtype=jnp.int32) * MOE_BLOCK, side='right'),
        N_EXPERTS - 1)

    def expert_block(args):
        tok, gate, e = args
        xb = xt[tok]
        hid = xb @ w1[e] + b1[e]
        glu = jnp.minimum(hid[:, :D_FF_EXPERT], SWIGLU_LIMIT)
        lin = jnp.clip(hid[:, D_FF_EXPERT:], -SWIGLU_LIMIT, SWIGLU_LIMIT)
        act = glu * jax.nn.sigmoid(SWIGLU_ALPHA * glu) * (lin + 1.0)
        return (act @ w2[e] + b2[e]) * gate[:, None]

    y = lax.map(expert_block, (row_tok.reshape(n_blocks, MOE_BLOCK),
                               row_gate.reshape(n_blocks, MOE_BLOCK), block_expert))
    out = jax.ops.segment_sum(y.reshape(n_rows, d), row_tok, num_segments=n_tok)
    return out.reshape(bsz, seq, d)

def first_inputs(seed: int = 0) -> dict:
    key = jax.random.key(seed)
    ks = iter(jax.random.split(key, 40))

    def normal(shape, scale):
        return jax.random.normal(next(ks), shape, jnp.float32) * scale

    def gain(shape, s=0.02):
        return 1.0 + normal(shape, s)

    L = DEPTH
    LV = max(DEPTH - 1, 0)
    return {
        'x': normal((BATCH, SEQ, D_MODEL), 1.0),
        'c': normal((BATCH, D_MODEL), 1.0),
        'norm1_g': gain((L, D_MODEL)),
        'norm2_g': gain((L, D_MODEL)),
        'ada_w': normal((L, D_MODEL, 6 * D_MODEL), 0.5 * D_MODEL ** -0.5),
        'ada_b': normal((L, 6 * D_MODEL), 0.02),
        'w_in': normal((L, D_MODEL, C_IN), D_MODEL ** -0.5),
        'shift_mu': jax.random.uniform(next(ks), (L, C_RWKV), jnp.float32),
        'decay_w0': jax.random.uniform(next(ks), (L, D_RWKV), jnp.float32, -1.5, 1.5),
        'decay_up': normal((L, DECAY_LORA, D_RWKV), 0.5 * DECAY_LORA ** -0.5),
        'iclr_a0': normal((L, D_RWKV), 0.1),
        'iclr_up': normal((L, ICLR_LORA, D_RWKV), 0.5 * ICLR_LORA ** -0.5),
        'gate_up': normal((L, GATE_LORA, D_RWKV), GATE_LORA ** -0.5),
        'k_k': gain((L, D_RWKV), 0.1),
        'k_a': gain((L, D_RWKV), 0.1),
        'r_k': normal((L, H_RWKV, HEAD_DIM), 0.1),
        'lnx_w': gain((L, D_RWKV)),
        'lnx_b': normal((L, D_RWKV), 0.02),
        'vres_down': normal((LV, D_RWKV, VRES_LORA), D_RWKV ** -0.5),
        'vres_up': normal((LV, VRES_LORA, D_RWKV), 0.5 * VRES_LORA ** -0.5),
        'vres_b': normal((LV, D_RWKV), 0.1),
        'q_norm_g': gain((L, HEAD_DIM)),
        'k_norm_g': gain((L, HEAD_DIM)),
        'sb_out_g': gain((L, D_SB)),
        'w_out': normal((L, D_MIX, D_MODEL), D_MIX ** -0.5),
        'router_w': normal((L, D_MODEL, N_EXPERTS), D_MODEL ** -0.5),
        'router_b': normal((L, N_EXPERTS), 0.01),
        'exp_w1': normal((L, N_EXPERTS, D_MODEL, 2 * D_FF_EXPERT), D_MODEL ** -0.5),
        'exp_b1': normal((L, N_EXPERTS, 2 * D_FF_EXPERT), 0.02),
        'exp_w2': normal((L, N_EXPERTS, D_FF_EXPERT, D_MODEL), D_FF_EXPERT ** -0.5),
        'exp_b2': normal((L, N_EXPERTS, D_MODEL), 0.02),
    }

def first_block(x, c, norm1_g, norm2_g, ada_w, ada_b, w_in, shift_mu, decay_w0, decay_up,
              iclr_a0, iclr_up, gate_up, k_k, k_a, r_k, lnx_w, lnx_b, vres_down, vres_up,
              vres_b, q_norm_g, k_norm_g, sb_out_g, w_out, router_w, router_b,
              exp_w1, exp_b1, exp_w2, exp_b2):
    cond = jax.nn.silu(c)
    v_first = None
    for l in range(DEPTH):
        mod = cond @ ada_w[l] + ada_b[l]
        shift1, scale1, gate1, shift2, scale2, gate2 = jnp.split(mod[:, None, :], 6, axis=-1)
        h = rms_norm(x, norm1_g[l]) * (1.0 + scale1) + shift1
        z = h @ w_in[l]
        vres = None if l == 0 else (vres_down[l - 1], vres_up[l - 1], vres_b[l - 1])
        y_rwkv, v_first = rwkv7_time_mix(
            z[..., :C_RWKV], v_first, shift_mu[l], decay_w0[l], decay_up[l], iclr_a0[l],
            iclr_up[l], gate_up[l], k_k[l], k_a[l], r_k[l], lnx_w[l], lnx_b[l], vres)
        z_sb = z[..., C_RWKV:]
        y_sb = stick_breaking_attention(
            z_sb[..., :D_SB], z_sb[..., D_SB:2 * D_SB], z_sb[..., 2 * D_SB:],
            q_norm_g[l], k_norm_g[l], sb_out_g[l])
        mixed = jnp.concatenate([y_rwkv, y_sb], axis=-1) @ w_out[l]
        x = x + gate1 * mixed
        h2 = rms_norm(x, norm2_g[l]) * (1.0 + scale2) + shift2
        x = x + gate2 * moe_ffn(h2, router_w[l], router_b[l], exp_w1[l], exp_b1[l],
                                exp_w2[l], exp_b2[l])
    return x


CONV_WIDTH_A = D_MODEL // 2
CONV_K = 3
N_HEADS = 8
N_KV_GROUPS = 2
HEADS_PER_GROUP = N_HEADS // N_KV_GROUPS
ATTN_WIDTH = N_HEADS * HEAD_DIM
KV_WIDTH = N_KV_GROUPS * HEAD_DIM
CMP_BLOCK = 32
CMP_STRIDE = 16
SEL_BLOCK = 64
N_SEL = 16
WINDOW = 512
Q_BLOCK = 128
N_NSA_BRANCH = 3
ROPE_THETA = 10000.0
D_FF = 2816
N_MERGE = 2
EPS = 1e-6
NEG = -1e30
FORCE = 1e9

SPLIT_SIZES = [CONV_WIDTH_A, CONV_WIDTH_A, CONV_WIDTH_A, ATTN_WIDTH] + [KV_WIDTH] * 6 + [N_NSA_BRANCH * N_HEADS, N_MERGE * D_MODEL]
IN_COLS = sum(SPLIT_SIZES)


def rmsnorm(x, g):
    x32 = x.astype(jnp.float32)
    y = x32 * lax.rsqrt(jnp.mean(x32 * x32, axis=-1, keepdims=True) + EPS)
    return (y * g.astype(jnp.float32)).astype(x.dtype)

def causal_dwconv(u, w):
    s = u.shape[1]
    up = jnp.pad(u, ((0, 0), (CONV_K - 1, 0), (0, 0)))
    y = w[0] * up[:, 0:s]
    for k in range(1, CONV_K):
        y = y + w[k] * up[:, k:k + s]
    return y

def rope(x, positions):
    half = HEAD_DIM // 2
    inv = ROPE_THETA ** (-jnp.arange(half, dtype=jnp.float32) / half)
    ang = positions.astype(jnp.float32)[..., None] * inv
    cos = jnp.cos(ang)[:, :, None, :]
    sin = jnp.sin(ang)[:, :, None, :]
    x32 = x.astype(jnp.float32)
    x1, x2 = x32[..., :half], x32[..., half:]
    out = jnp.concatenate([x1 * cos - x2 * sin, x2 * cos + x1 * sin], axis=-1)
    return out.astype(x.dtype)

def compress(kv, pe, w1, w2):
    b, s = kv.shape[0], kv.shape[1]
    n_cmp = (s - CMP_BLOCK) // CMP_STRIDE + 1
    idx = np.arange(n_cmp)[:, None] * CMP_STRIDE + np.arange(CMP_BLOCK)[None, :]
    blk = kv[:, idx] + pe[None, None, :, None, :]
    blk = blk.transpose(0, 1, 3, 2, 4).reshape(b, n_cmp, N_KV_GROUPS, CMP_BLOCK * HEAD_DIM)
    return jax.nn.silu(blk @ w1) @ w2

def masked_softmax(s, mask):
    p = jax.nn.softmax(jnp.where(mask, s, NEG), axis=-1)
    return jnp.where(mask, p, 0.0)

def nsa(q, k_cmp, v_cmp, k_sel, v_sel, k_win, v_win, gates):
    b, s = q.shape[0], q.shape[1]
    n_cmp = k_cmp.shape[1]
    n_blk = s // SEL_BLOCK
    n_sel = min(N_SEL, n_blk)
    n_qb = s // Q_BLOCK
    scale = HEAD_DIM ** -0.5
    cmp_end = jnp.arange(n_cmp) * CMP_STRIDE + CMP_BLOCK - 1
    ii = np.arange(n_cmp)[:, None] * CMP_STRIDE
    jj = np.arange(n_blk)[None, :] * SEL_BLOCK
    overlap = jnp.asarray(((ii < jj + SEL_BLOCK) & (ii + CMP_BLOCK > jj)).astype(np.float32))
    ksb = k_sel.reshape(b, n_blk, SEL_BLOCK, N_KV_GROUPS, HEAD_DIM).transpose(0, 3, 1, 2, 4)
    vsb = v_sel.reshape(b, n_blk, SEL_BLOCK, N_KV_GROUPS, HEAD_DIM).transpose(0, 3, 1, 2, 4)
    kwp = jnp.pad(k_win, ((0, 0), (WINDOW, 0), (0, 0), (0, 0)))
    vwp = jnp.pad(v_win, ((0, 0), (WINDOW, 0), (0, 0), (0, 0)))
    b_ix = jnp.arange(b)[:, None, None, None]
    g_ix = jnp.arange(N_KV_GROUPS)[None, :, None, None]
    blk_ids = jnp.arange(n_blk)

    def query_block(qb):
        t0 = qb * Q_BLOCK
        t = t0 + jnp.arange(Q_BLOCK)
        qc = lax.dynamic_slice_in_dim(q, t0, Q_BLOCK, axis=1).reshape(b, Q_BLOCK, N_KV_GROUPS, HEADS_PER_GROUP, HEAD_DIM)
        gc = lax.dynamic_slice_in_dim(gates, t0, Q_BLOCK, axis=1).reshape(b, Q_BLOCK, N_KV_GROUPS, HEADS_PER_GROUP, N_NSA_BRANCH)
        sc = jnp.einsum('bqghd,bkgd->bghqk', qc, k_cmp).astype(jnp.float32) * scale
        p_c = masked_softmax(sc, cmp_end[None, :] <= t[:, None])
        o_c = jnp.einsum('bghqk,bkgd->bqghd', p_c.astype(v_cmp.dtype), v_cmp)
        imp = jnp.einsum('bghqk,kj->bgqj', p_c, overlap)
        cur = t // SEL_BLOCK
        forced = (blk_ids[None, :] == 0) | (blk_ids[None, :] == cur[:, None]) | (blk_ids[None, :] == cur[:, None] - 1)
        valid = blk_ids[None, :] <= cur[:, None]
        imp = jnp.where(forced, FORCE, jnp.where(valid, imp, -FORCE))
        _, sel = lax.top_k(imp, n_sel)
        ks = ksb[b_ix, g_ix, sel].reshape(b, N_KV_GROUPS, Q_BLOCK, n_sel * SEL_BLOCK, HEAD_DIM)
        vs = vsb[b_ix, g_ix, sel].reshape(b, N_KV_GROUPS, Q_BLOCK, n_sel * SEL_BLOCK, HEAD_DIM)
        kpos = (sel[..., None] * SEL_BLOCK + jnp.arange(SEL_BLOCK)).reshape(b, N_KV_GROUPS, Q_BLOCK, n_sel * SEL_BLOCK)
        ss = jnp.einsum('bqghd,bgqkd->bghqk', qc, ks).astype(jnp.float32) * scale
        p_s = masked_softmax(ss, (kpos <= t[None, None, :, None])[:, :, None])
        o_s = jnp.einsum('bghqk,bgqkd->bqghd', p_s.astype(vs.dtype), vs)
        kw = lax.dynamic_slice_in_dim(kwp, t0, WINDOW + Q_BLOCK, axis=1)
        vw = lax.dynamic_slice_in_dim(vwp, t0, WINDOW + Q_BLOCK, axis=1)
        spos = t0 - WINDOW + jnp.arange(WINDOW + Q_BLOCK)
        diff = t[:, None] - spos[None, :]
        mask_w = (diff >= 0) & (diff < WINDOW) & (spos[None, :] >= 0)
        sw = jnp.einsum('bqghd,bkgd->bghqk', qc, kw).astype(jnp.float32) * scale
        p_w = masked_softmax(sw, mask_w)
        o_w = jnp.einsum('bghqk,bkgd->bqghd', p_w.astype(vw.dtype), vw)
        out = gc[..., 0:1] * o_c + gc[..., 1:2] * o_s + gc[..., 2:3] * o_w
        return out.reshape(b, Q_BLOCK, ATTN_WIDTH)

    out = lax.map(query_block, jnp.arange(n_qb))
    return out.transpose(1, 0, 2, 3).reshape(b, s, ATTN_WIDTH)

def second_inputs(seed: int = 0) -> dict:
    key = jax.random.key(seed)
    ks = jax.random.split(key, 24)
    L = DEPTH
    nrm = lambda k, shape, scale: jax.random.normal(k, shape, jnp.float32) * scale
    x = jax.random.normal(ks[0], (BATCH, SEQ, D_MODEL), jnp.float32)
    positions = (jnp.arange(SEQ, dtype=jnp.int32)[None, :] + jax.random.randint(ks[1], (BATCH, 1), 0, 1024, dtype=jnp.int32)).astype(jnp.int32)
    return {
        'x': x,
        'positions': positions,
        'norm1_g': 1.0 + nrm(ks[2], (L, D_MODEL), 0.02),
        'w_in': nrm(ks[3], (L, D_MODEL, IN_COLS), D_MODEL ** -0.5),
        'conv_a_w': nrm(ks[4], (L, CONV_K, CONV_WIDTH_A), CONV_K ** -0.5),
        'w_a_out': nrm(ks[5], (L, CONV_WIDTH_A, D_MODEL), CONV_WIDTH_A ** -0.5),
        'q_norm_g': 1.0 + nrm(ks[6], (L, HEAD_DIM), 0.02),
        'k_norm_g': 1.0 + nrm(ks[7], (L, N_NSA_BRANCH, HEAD_DIM), 0.02),
        'cmp_k_pe': nrm(ks[8], (L, CMP_BLOCK, HEAD_DIM), 0.1),
        'cmp_k_w1': nrm(ks[9], (L, CMP_BLOCK * HEAD_DIM, HEAD_DIM), (CMP_BLOCK * HEAD_DIM) ** -0.5),
        'cmp_k_w2': nrm(ks[10], (L, HEAD_DIM, HEAD_DIM), HEAD_DIM ** -0.5),
        'cmp_v_pe': nrm(ks[11], (L, CMP_BLOCK, HEAD_DIM), 0.1),
        'cmp_v_w1': nrm(ks[12], (L, CMP_BLOCK * HEAD_DIM, HEAD_DIM), (CMP_BLOCK * HEAD_DIM) ** -0.5),
        'cmp_v_w2': nrm(ks[13], (L, HEAD_DIM, HEAD_DIM), HEAD_DIM ** -0.5),
        'w_b_out': nrm(ks[14], (L, ATTN_WIDTH, D_MODEL), ATTN_WIDTH ** -0.5),
        'w_o': nrm(ks[15], (L, D_MODEL, D_MODEL), D_MODEL ** -0.5),
        'norm2_g': 1.0 + nrm(ks[16], (L, D_MODEL), 0.02),
        'w_ffn_in': nrm(ks[17], (L, D_MODEL, 2 * D_FF), D_MODEL ** -0.5),
        'ffn_conv_w': nrm(ks[18], (L, CONV_K, D_FF), CONV_K ** -0.5),
        'ffn_conv_b': nrm(ks[19], (L, D_FF), 0.02),
        'w_ffn_out': nrm(ks[20], (L, D_FF, D_MODEL), D_FF ** -0.5),
    }

def second_block(x, positions, norm1_g, w_in, conv_a_w, w_a_out, q_norm_g, k_norm_g, cmp_k_pe, cmp_k_w1, cmp_k_w2, cmp_v_pe, cmp_v_w1, cmp_v_w2, w_b_out, w_o, norm2_g, w_ffn_in, ffn_conv_w, ffn_conv_b, w_ffn_out):
    b, s, _ = x.shape
    cuts = list(np.cumsum(SPLIT_SIZES)[:-1].tolist())
    for l in range(DEPTH):
        h = rmsnorm(x, norm1_g[l])
        proj = h @ w_in[l]
        a_b, a_c, a_x, q, kc, vc, ksl, vsl, kwn, vwn, g_nsa, g_merge = jnp.split(proj, cuts, axis=-1)
        y_a = a_b * causal_dwconv(a_c * a_x, conv_a_w[l])
        q = rope(rmsnorm(q.reshape(b, s, N_HEADS, HEAD_DIM), q_norm_g[l]), positions)
        kv_shape = (b, s, N_KV_GROUPS, HEAD_DIM)
        k_cmp = rmsnorm(compress(kc.reshape(kv_shape), cmp_k_pe[l], cmp_k_w1[l], cmp_k_w2[l]), k_norm_g[l, 0])
        v_cmp = compress(vc.reshape(kv_shape), cmp_v_pe[l], cmp_v_w1[l], cmp_v_w2[l])
        k_sel = rope(rmsnorm(ksl.reshape(kv_shape), k_norm_g[l, 1]), positions)
        k_win = rope(rmsnorm(kwn.reshape(kv_shape), k_norm_g[l, 2]), positions)
        gates = jax.nn.sigmoid(g_nsa).reshape(b, s, N_HEADS, N_NSA_BRANCH)
        y_b = nsa(q, k_cmp, v_cmp, k_sel, vsl.reshape(kv_shape), k_win, vwn.reshape(kv_shape), gates)
        gm = jax.nn.sigmoid(g_merge)
        mix = gm[..., :D_MODEL] * (y_a @ w_a_out[l]) + gm[..., D_MODEL:] * (y_b @ w_b_out[l])
        x = x + mix @ w_o[l]
        h = rmsnorm(x, norm2_g[l])
        gu = h @ w_ffn_in[l]
        g = causal_dwconv(gu[..., :D_FF], ffn_conv_w[l]) + ffn_conv_b[l]
        x = x + (jax.nn.silu(g) * gu[..., D_FF:]) @ w_ffn_out[l]
    return x


def setup_inputs(seed=0):
    out = dict(first_inputs(seed))
    for name, value in second_inputs(seed + 1).items():
        if name != "x":
            out[name + "_2"] = value
    return out


def reference(
    x, c, norm1_g, norm2_g, ada_w, ada_b, w_in, shift_mu, decay_w0, decay_up, iclr_a0, iclr_up,
    gate_up, k_k, k_a, r_k, lnx_w, lnx_b, vres_down, vres_up, vres_b, q_norm_g, k_norm_g,
    sb_out_g, w_out, router_w, router_b, exp_w1, exp_b1, exp_w2, exp_b2, positions_2, norm1_g_2,
    w_in_2, conv_a_w_2, w_a_out_2, q_norm_g_2, k_norm_g_2, cmp_k_pe_2, cmp_k_w1_2, cmp_k_w2_2,
    cmp_v_pe_2, cmp_v_w1_2, cmp_v_w2_2, w_b_out_2, w_o_2, norm2_g_2, w_ffn_in_2, ffn_conv_w_2,
    ffn_conv_b_2, w_ffn_out_2,
):
    x = first_block(
        x, c, norm1_g, norm2_g, ada_w, ada_b, w_in, shift_mu, decay_w0, decay_up, iclr_a0,
        iclr_up, gate_up, k_k, k_a, r_k, lnx_w, lnx_b, vres_down, vres_up, vres_b, q_norm_g,
        k_norm_g, sb_out_g, w_out, router_w, router_b, exp_w1, exp_b1, exp_w2, exp_b2,
    )
    return second_block(
        x, positions_2, norm1_g_2, w_in_2, conv_a_w_2, w_a_out_2, q_norm_g_2, k_norm_g_2,
        cmp_k_pe_2, cmp_k_w1_2, cmp_k_w2_2, cmp_v_pe_2, cmp_v_w1_2, cmp_v_w2_2, w_b_out_2,
        w_o_2, norm2_g_2, w_ffn_in_2, ffn_conv_w_2, ffn_conv_b_2, w_ffn_out_2,
    )


_drawn_inputs = setup_inputs


def setup_inputs(seed=0):
    import zlib

    import numpy as np

    out = dict(_drawn_inputs(seed))
    spreads = {}
    factors = {'norm1_g': 4.444,
     'decay_up': 2.854,
     'iclr_a0': 3.349,
     'k_k': 15.176,
     'lnx_w': 29.619,
     'lnx_b': 28.436,
     'q_norm_g': 6.024,
     'k_norm_g': 8.0,
     'sb_out_g': 18.217,
     'router_b': 15.018,
     'exp_b1': 8.0,
     'exp_b2': 25.41,
     'norm1_g_2': 3.165,
     'q_norm_g_2': 34.812,
     'k_norm_g_2': 34.208,
     'cmp_k_pe_2': 23.743,
     'cmp_v_pe_2': 33.072,
     'norm2_g_2': 15.36,
     'ffn_conv_b_2': 22.551,
     'norm2_g': 4.672}
    for name, (base, spread) in spreads.items():
        noise = np.random.default_rng([zlib.crc32(name.encode()), seed]).standard_normal(out[name].shape)
        drawn = base * np.exp(spread * noise) if base else spread * noise
        out[name] = jnp.asarray(drawn.astype(out[name].dtype))
    for name, factor in factors.items():
        out[name] = (out[name] * factor).astype(out[name].dtype)
    return out
```

```python
from contextlib import ExitStack

import numpy as np

import concourse.bass as bass
from concourse import mybir

ALU = mybir.AluOpType
ACT = mybir.ActivationFunctionType
AX = mybir.AxisListType
F32 = mybir.dt.float32
I32 = mybir.dt.int32
U32 = mybir.dt.uint32

P = 128
T = 512
D = 1024
KD = D // P
NT = T // P
HD = 64
NH = 8
EXPERTS = 32
TOP_K = 4
FF = 1024
C_RWKV = 1792
NZ = C_RWKV // P
FF2 = 2816
KF = FF2 // P
N_CMP = 31
CMP_BLOCK, CMP_STRIDE = 32, 16
TURN = float(2 * np.pi)
TURN_PARTS = (6.28125, float(np.float32(0.0019350051879882812)), float(np.float32(2 * np.pi - 6.28125 - 0.0019350051879882812)))
ROUNDER = 1.5 * 2.0 ** 23
PI_LOW = 3.1415925
DECAY_K = float(np.exp(-0.5))
NORM_EPS = 1e-6
GN_EPS = 1e-5 * HD
L2_EPS = 1e-12
NEG = -1e30
MAX_CHUNK = 4096
SLOTS = 6

VEC_COLS = dict(c=KD, norm1_g=KD, norm2_g=KD, ada_b=48, shift_mu=NZ, decay_w0=4, iclr_a0=4, k_k=4, k_a=4, r_k=4,
                lnx_w=4, lnx_b=4, sb_out_g=4, q_norm_g=1, k_norm_g=1, norm1_g_2=KD, norm2_g_2=KD,
                conv_a_w_2=12, ffn_conv_w_2=3 * KF, ffn_conv_b_2=KF, cmp_k_pe_2=CMP_BLOCK, cmp_v_pe_2=CMP_BLOCK)
ROW_COLS = dict(router_b=EXPERTS, q_norm_g_2=HD, k_norm_g_2=3 * HD)
CONST_COLS = dict(ident=P, head_ones=P, ones=P, neg_tri=P, neg_ones=P, strict=P, incl=P, sb_mask=P, level=7 * P,
                  iota=P, causal=P, cmp_bias=4 * 32, cmp_mask=4 * 32, inv_freq=32, expert=EXPERTS, eps=4)


def offsets(cols):
    at, out = 0, {}
    for name, n in cols.items():
        out[name] = at
        at += n
    return out, at


VEC_AT, VEC_N = offsets({**VEC_COLS, **ROW_COLS})
CONST_AT, CONST_N = offsets(CONST_COLS)


def constants():
    c = np.zeros((P, CONST_N), np.float32)

    def put(name, value):
        c[:, CONST_AT[name]:CONST_AT[name] + CONST_COLS[name]] = value
    i = np.arange(P)
    row, col = i[:, None], i[None, :]
    put("ident", row == col)
    put("head_ones", row // HD == col // HD)
    put("ones", 1.0)
    put("neg_tri", -1.0 * (row >= col))
    put("neg_ones", -1.0)
    put("strict", row < col)
    put("incl", row <= col)
    put("sb_mask", np.where(row < col, 0.0, NEG))
    for k in range(7):
        s = 2 ** k
        c[:, CONST_AT["level"] + k * P:CONST_AT["level"] + (k + 1) * P] = ((row // s) % 2 == 1) & (col // s == row // s - 1)
    put("iota", col)
    put("causal", np.where(col <= row, 0.0, NEG))
    end = np.arange(32) * CMP_STRIDE + CMP_BLOCK - 1
    ok = np.stack([end[None, :] <= (row + P * q) for q in range(4)], 1)
    put("cmp_bias", np.where(ok, 0.0, NEG).reshape(P, -1))
    put("cmp_mask", ok.reshape(P, -1))
    put("inv_freq", (np.float32(10000.0) ** (-np.arange(32, dtype=np.float32) / np.float32(32)))[None, :])
    put("expert", np.arange(EXPERTS)[None, :])
    put("eps", np.array([[NORM_EPS, GN_EPS, np.pi / 2, 1.0]]))
    return c


class Plan:

    def __init__(self, keys):
        self.at = {k: i for i, k in enumerate(keys)}
        assert len(self.at) == len(keys)

    def bank(self, key):
        return self.at[key] % 4

    def turn(self, key):
        return self.at[key] // 4


def chunk_plan():
    order = [("ada", n) for n in range(4)]
    ada = 4
    for n in range(7):
        order.append(("win", n))
        while ada < 12 and ada < 4 + 2 * (n + 1):
            order.append(("ada", ada))
            ada += 1
    return order


A_B, A_C, A_X, Q2, KC, KV2, G_NSA, G_MERGE = 0, 512, 1024, 1536, 2048, 2304, 2816, 2840


def second_chunks():
    out = [("q2", ("q2", 3)), ("kv2", ("kv2", 3)), ("kc", ("g2", 3)), ("ac", ("ac", 3)), ("ax", ("ax", 3)), ("ab", ("ab", 3)),
           ("wa", ("mg", KD - 1, 3)), ("wb", ("mg", KD - 1, 3))]
    out += [(("mg", j), ("mg", 2 * j + 1, 3)) for j in range(4)]
    out += [(("w_o", j), ("w_o", KD - 1)) for j in range(2)]
    out += [(("fi", j), ("gu", 2 * j + 1, 1)) for j in range(KF // 2)]
    out += [(("fo", j), None) for j in range(6)]
    return out


WIN_CUTS = [0, 512, 1024, 1536, 1792, 2304, 2816, 3328]
WIN_TILES = [range(0, 4), range(4, 8), range(8, 12), range(12, 14), range(14, 18), range(18, 22)]


WIN_LAST = [("z", t[-1]) for t in WIN_TILES] + [("v", NT - 1)]


def program(nc, a, out):
    chunks = chunk_plan()
    slot_of = {c: n % SLOTS for n, c in enumerate(chunks)}
    load_of = {c: n // SLOTS + 1 for n, c in enumerate(chunks)}
    keys = [("z", m) for m in range(22)] + [("v", t) for t in range(NT)]
    keys += [("wag", c, j) for c in range(4) for j in range(3)]
    keys += [("kk", c) for c in range(4)] + [("rk", c) for c in range(4)]
    keys += [("tok", ch, j) for ch in range(NT) for j in range(3)]
    for ch in range(NT):
        keys += [("am", ch, h) for h in range(NH)] + [("yT", ch)]
    keys += [("sbn", i) for i in range(8)]
    keys += [("oT", t) for t in range(NT)]
    keys += [("wo", m) for m in range(KD)]
    keys += [("ht", t, i) for t in range(NT) for i in range(2)] + [("lg", t) for t in range(NT)]
    keys += [("pos", t) for t in range(NT)] + [("cnt",)]
    keys += [("q2", t) for t in range(NT)] + [("kv2", t) for t in range(NT)] + [("kc",), ("vc",)] + [("g2", t) for t in range(NT)]
    keys += [(n, c) for n in ("ac", "ax", "ab") for c in range(4)]
    keys += [("hid", j, g) for j in range(2) for g in range(2)] + [("kvc",), ("kcT",)]
    keys += [("qkT", t) for t in range(NT)] + [("kkT", t) for t in range(NT)]
    for t in range(NT):
        keys += [("cs", t, g) for g in range(2)] + [("cT", t, i) for i in range(2)]
    keys += [("ybT", t) for t in range(NT)]
    keys += [("mg", m, i) for m in range(KD) for i in range(4)]
    keys += [("w_o", m) for m in range(KD)]
    keys += [("gu", m, i) for m in range(KF) for i in range(2)]
    plan = Plan(keys)

    with ExitStack() as ctx:
        def sb(name, shape, dt=F32):
            return ctx.enter_context(nc.sbuf_tensor(name, shape, dt))

        def sem(name):
            return ctx.enter_context(nc.semaphore(name))

        ring = sb("ring", [P, SLOTS * MAX_CHUNK])
        xT = sb("xT", [P, KD, T])
        hT = sb("hT", [P, KD, T])
        cst = sb("cst", [P, CONST_N])
        vec = sb("vec", [P, VEC_N])
        arena = sb("arena", [P, 32 * T])
        cos_sin = sb("cos_sin", [P, 2, NT, 32])
        attn = sb("attn", [P, 320])
        mod = sb("mod", [P, 48])
        gain = sb("gain", [P, KD])
        small = sb("small", [P, 132])
        bank = [ctx.enter_context(nc.psum_tensor(f"bank{i}", [P, T], F32)) for i in range(8)]

        def const(name, n=None):
            at = CONST_AT[name]
            return cst[:, at:at + (n or CONST_COLS[name])]

        def col(name, j=0):
            return vec[:, VEC_AT[name] + j:VEC_AT[name] + j + 1]

        def A(i, n=1):
            return arena[:, i * T:(i + n) * T]

        def R(i, n=1):
            return ring[:, i * T:(i + n) * T]

        ident = const("ident")
        ones = const("ones")
        head_ones = const("head_ones")
        eps = lambda j: cst[:, CONST_AT["eps"] + j:CONST_AT["eps"] + j + 1]

        cst_in, vec_in, x_in, up_in = (sem(n) for n in ("cst_in", "vec_in", "x_in", "up_in"))
        slot_in = [sem(f"slot_in{s}") for s in range(SLOTS)]
        wo_in, rw_in = sem("wo_in"), sem("rw_in")
        ada_used = sem("ada_used")
        evac = [sem(f"evac{i}") for i in range(4)]
        filled = sem("filled")
        sq_ready, ss_done, rs_ready, h_ready = (sem(n) for n in ("sq_ready", "ss_done", "rs_ready", "h_ready"))
        sig_c, cond_ready, acc_ready, mod_mm, z_scaled = (sem(n) for n in ("sig_c", "cond_ready", "acc_ready", "mod_mm", "z_scaled"))
        gates_lo, kk0_ready, kk2_ready, rk_ready, mid_ready, exp_ready = (sem(n) for n in (
            "gates_lo", "kk0_ready", "kk2_ready", "rk_ready", "mid_ready", "exp_ready"))
        prep_done = sem("prep_done")
        t1_mm, t1_sb, xn_mm, x_sb, xt_mm, xt_sb = (sem(n) for n in ("t1_mm", "t1_sb", "xn_mm", "x_sb", "xt_mm", "xt_sb"))
        w_mm, w_sb, u_mm, u_sb, y_mm, y_sb, s_mm, s_sb = (sem(n) for n in (
            "w_mm", "w_sb", "u_mm", "u_sb", "y_mm", "y_sb", "s_mm", "s_sb"))
        var_ready, std_ready, yn_ready = sem("var_ready"), sem("std_ready"), sem("yn_ready")
        mix_ready = sem("mix_ready")
        qk2_ready, qkn_ready = sem("qk2_ready"), sem("qkn_ready")
        l_mm, e_ready, abs_ready, ln_ready, sp_ready, r_mm, r_masked, wt_ready, o_mm, o_sb = (sem(n) for n in (
            "l_mm", "e_ready", "abs_ready", "ln_ready", "sp_ready", "r_mm", "r_masked", "wt_ready", "o_mm", "o_sb"))
        on_ready = sem("on_ready")
        dve_chain, act_chain = sem("dve_chain"), sem("act_chain")
        lg_ready, top_ready, eg_ready, route_ready, npass_ready, pos_out = (sem(n) for n in (
            "lg_ready", "top_ready", "eg_ready", "route_ready", "npass_ready", "pos_out"))
        w1_in = [sem(f"w1_in{k}") for k in range(KD)]
        w2_in = [sem(f"w2_in{k}") for k in range(KD)]
        b1_in, b2_in, w1_free, w2_free, b1_free, b2_free = (sem(n) for n in ("b1_in", "b2_in", "w1_free", "w2_free", "b1_free", "b2_free"))
        oh_ready, ohg_ready, gx_mm, gx_sb, hid_mm, glu_ready, lin_ready, sig_ready, act_ready = (sem(n) for n in (
            "oh_ready", "ohg_ready", "gx_mm", "gx_sb", "hid_mm", "glu_ready", "lin_ready", "sig_ready", "act_ready"))
        aT_mm, aT_sb, ohT_mm, ohT_sb, ye_mm, ye_sb, sc_mm, sc_sb = (sem(n) for n in (
            "aT_mm", "aT_sb", "ohT_mm", "ohT_sb", "ye_mm", "ye_sb", "sc_mm", "sc_sb"))
        moe_chain = sem("moe_chain")
        s2_in = [sem(f"s2_in{s}") for s in range(SLOTS)]
        cw_in, cw_zero, pos_in = sem("cw_in"), sem("cw_zero"), sem("pos_in")
        angles, trig_ready = sem("angles"), sem("trig_ready")
        x2_ready, kc_cp = sem("x2_ready"), sem("kc_cp")
        qn_sq, qn_rt, q_ready, k_ready, kc_sq, kc_rt, kc_ready = (sem(n) for n in (
            "qn_sq", "qn_rt", "q_ready", "k_ready", "kc_sq", "kc_rt", "kc_ready"))
        cs_ready, cp_exp, cp_ready, co_mm, co_sb = (sem(n) for n in ("cs_ready", "cp_exp", "cp_ready", "co_mm", "co_sb"))
        s2_mm, mx_ready, p_ready, pt_mm, pt_sb, o2_mm, yb_ready = (sem(n) for n in (
            "s2_mm", "mx_ready", "p_ready", "pt_mm", "pt_sb", "o2_mm", "yb_ready"))
        ya_ready, mg_ready, conv_ready, silu_ready, fo_mm, fo_sb, out_sent = (sem(n) for n in (
            "ya_ready", "mg_ready", "conv_ready", "silu_ready", "fo_mm", "fo_sb", "out_sent"))

        zs = lambda m, n=1: A(m, n)
        q_sb, k_sb = A(14, 4).rearrange("p (c t) -> p c t", c=4), A(18, 4).rearrange("p (c t) -> p c t", c=4)
        v_sb = A(22, 4).rearrange("p (t n) -> p t n", t=4)
        up_wa, up_g = A(26), A(27)
        acc = [A(28), A(29)]
        rstd = A(30)
        KR = R(16, 8).rearrange("p (c j t) -> p c j t", c=4, j=2)
        ktT = R(24, 4).rearrange("p (c t) -> p c t", c=4)
        btT = R(28, 4).rearrange("p (c t) -> p c t", c=4)
        bonus = R(32, 4).rearrange("p (c t) -> p c t", c=4)
        gT = R(36, 4).rearrange("p (c t) -> p c t", c=4)
        aT = R(40, 4).rearrange("p (c t) -> p c t", c=4)
        kkT = R(44, 4).rearrange("p (c t) -> p c t", c=4)
        sigw = ktT
        nrm = btT
        S1 = ring[:, 0:4 * 4 * 129].rearrange("p (c k t) -> p c k t", c=4, k=4)
        hflat = hT[:, :, :].rearrange("p k t -> p (k t)")
        E1 = hflat[:, 0:4 * 4 * 129].rearrange("p (c k t) -> p c k t", c=4, k=4)
        E2 = R(5, 4).rearrange("p (c k t) -> p c k t", c=4, k=4)
        kt_tok = R(40, 4).rearrange("p (k n) -> p k n", k=4)
        bt_tok = R(44, 4).rearrange("p (k n) -> p k n", k=4)
        v_tok = A(4, 4).rearrange("p (k n) -> p k n", k=4)
        AM = R(0, 8).rearrange("p (h n) -> p h n", h=NH)
        X = R(10, 2).rearrange("p (h n) -> p h n", h=NH)
        XT = R(12, 2).rearrange("p (h n) -> p h n", h=NH)
        T1 = hflat[:, 5 * T:7 * T].rearrange("p (h n) -> p h n", h=NH)
        W_sb = hflat[:, 7 * T:8 * T]
        U_sb = R(9)
        S_sc = up_wa
        yn, ysq = up_g, hflat[:, 0:T]
        mixT = lambda k: A(k) if k < 4 else A(10 + k)
        mids = small[:, 0:16].rearrange("p (c k) -> p c k", c=4)
        nmids = small[:, 16:32].rearrange("p (c k) -> p c k", c=4)
        emid = small[:, 32:48].rearrange("p (c k) -> p c k", c=4)
        dec = small[:, 48:64].rearrange("p (c k) -> p c k", c=4)
        omka = small[:, 64:68]
        omu = small[:, 68:68 + NZ]
        cond = small[:, 84:92]
        sigc = small[:, 92:100]
        hsum = small[:, 100:108]
        hvar = small[:, 108:116]
        hstd = small[:, 116:124]
        hrstd = small[:, 124:132]

        h2_tok = A(0, 8).rearrange("p (t n) -> p t n", t=NT)
        moeT = A(8, 8).rearrange("p (k t) -> p k t", k=KD)
        XG = A(16, 2).rearrange("p (k s) -> p k s", k=KD)
        G = A(18, 2)
        SG = A(20, 2)
        aT2 = SG.rearrange("p (k s) -> p k s", k=KD)
        Y = A(22, 2)
        OH = A(24).rearrange("p (t s) -> p t s", t=NT)
        OHG = A(25).rearrange("p (t s) -> p t s", t=NT)
        OHT = A(26)
        LIN = hflat[:, 6 * T:8 * T]
        B1 = hflat[:, 0:4 * T]
        B2 = hflat[:, 4 * T:6 * T]
        router_w = A(31)[:, 0:KD * EXPERTS].rearrange("p (k n) -> p k n", k=KD)
        route = A(28, 2)
        LG = route[:, 0:128].rearrange("p (t e) -> p t e", t=NT)
        SEL = route[:, 128:256].rearrange("p (t e) -> p t e", t=NT)
        GATE = route[:, 256:384].rearrange("p (t e) -> p t e", t=NT)
        GTMP = route[:, 384:416]
        POS = route[:, 416:416 + 4 * 33].rearrange("p (t e) -> p t e", t=NT)
        TOPV = route[:, 548:580].rearrange("p (t e) -> p t e", t=NT)
        TOPF = route[:, 580:612].rearrange("p (t e) -> p t e", t=NT)
        TOPG = route[:, 612:628].rearrange("p (t e) -> p t e", t=NT)
        GSUM = route[:, 628:632]
        NPF = route[:, 632:636]
        top_idx = sb("top_idx", [P, NT, 8], U32)
        n_pass = sb("n_pass", [P, 1], I32)
        w1_slot = lambda k: ring[:, k * 2 * FF:(k + 1) * 2 * FF]
        w2_slot = lambda k: ring[:, KD * 2 * FF + k * D:KD * 2 * FF + (k + 1) * D]

        q_tok = A(0, 4).rearrange("p (t n) -> p t n", t=NT)
        kv_tok = A(4, 4).rearrange("p (t n) -> p t n", t=NT)
        kcT, vcT = A(8), A(9)
        QT = A(10, 4).rearrange("p (c t) -> p c t", c=4)
        KselT, KwinT = A(14), A(15)
        yaT = A(16, 4).rearrange("p (c t) -> p c t", c=4)
        cmp_w1 = [A(20 + 4 * j, 4).rearrange("p (i n) -> p i n", i=CMP_BLOCK) for j in range(2)]
        scr = A(28)
        scr2 = A(29)
        Pb = [A(30), A(31)]
        PTb = [A(28), A(29)]
        ybT = A(20, 4).rearrange("p (c t) -> p c t", c=4)
        yb_tok = A(0, 4).rearrange("p (t n) -> p t n", t=NT)
        yb_tmp = A(24)
        crow = A(28)
        cPT = A(30, 2).rearrange("p (h q) -> p h q", h=NH)
        u_pos = sb("u_pos", [P, NT], I32)
        mix2 = lambda m: A(m)
        actT = lambda m: A(m)
        nsa_gate = attn[:, 0:96].rearrange("p (t g) -> p t g", t=NT)
        nmax = attn[:, 96:160]
        psum_ = attn[:, 160:224]
        csum = attn[:, 224:232]
        cmx = attn[:, 232:240]
        gs = attn[:, 240:248]
        hbias = attn[:, 248:250]
        cstat = attn[:, 250:254]
        hid = [A(8 + j)[0:HD, 0:64].rearrange("p (g n) -> p g n", g=2) for j in range(2)]
        kcn = A(8)[0:N_CMP, 128:256]
        v_cmp = A(9)[0:N_CMP, 256:384]
        KcT = A(8)[:, 384:384 + N_CMP]
        stats = nmax[:, 0:48].rearrange("p (t h) -> p t h", t=NT)
        cmp_w2 = sb("cmp_w2", [P, 2 * HD])
        trig = A(31)

        def s_bank(u):
            return bank[(2, 3, 6, 7)[u % 4]]

        chunks2 = second_chunks()
        place2, total = {}, [0] * SLOTS
        for n, (name, _) in enumerate(chunks2):
            total[n % SLOTS] += 16 * (2 if name == "kc" or name[0] in ("mg", "fi") else 1)
            place2[name] = (n % SLOTS, total[n % SLOTS])

        def slot2(name, k, width):
            at = place2[name][0] * MAX_CHUNK
            return ring[:, at:at + k * width].rearrange("p (k n) -> p k n", k=k)

        def loaded2(eng, name):
            eng.wait_ge(s2_in[place2[name][0]], place2[name][1])

        def sb_logits(h, kt):
            b = 3 * (h % 2)
            x, lo = ((2 + b, 0), (3 + b, 0), (4 + b, 0), (3 + b, 384))[kt]
            return bank[x][:, lo:lo + T - P * kt]

        def sb_out(h):
            return bank[4 + 3 * (h % 2)][:, 256:512]

        def sb_e(h, kt):
            at = 16 * T + (h % 2) * 1280 + (0, 512, 896, 1152)[kt]
            return ring[:, at:at + T - P * kt]

        def sb_w(h, kt):
            at = 24 * T + (h % 2) * 1280 + (0, 512, 896, 1152)[kt]
            return ring[:, at:at + T - P * kt]
        o_tok = R(32, 4).rearrange("p (t n) -> p t n", t=4)

        block = ctx.enter_context(nc.Block())

        def tile_evacuated(eng, key):
            eng.wait_ge(evac[plan.bank(key)], plan.turn(key) + 1)

        @block.sync
        def _(sp):
            sp.dma_start(cst[:, :], a["consts"]).then_inc(cst_in, 16)
            sp.dma_start(vec[:, :], a["vecs"]).then_inc(vec_in, 16)
            sp.dma_start(xT[:, :, :], a["xT"]).then_inc(x_in, 16)
            sp.dma_start(up_wa[0:64, :], a["decay_up"][0]).then_inc(up_in, 16)
            sp.dma_start(up_wa[64:128, :], a["iclr_up"][0]).then_inc(up_in, 16)
            sp.dma_start(up_g, a["gate_up"][0]).then_inc(up_in, 16)
            sp.dma_start(u_pos[:, :], a["positions"]).then_inc(pos_in, 16)
            ada_w = a["ada_w"][0].rearrange("(k p) n -> p k n", p=P)
            w_in = a["w_in"][0].rearrange("(k p) n -> p k n", p=P)
            for n, (kind, i) in enumerate(chunks):
                if n >= SLOTS:
                    last_kind, last = chunks[n - SLOTS]
                    if last_kind == "ada":
                        sp.wait_ge(ada_used, last + 1)
                    else:
                        sp.wait_ge(filled, plan.at[WIN_LAST[last]] + 1)
                s = n % SLOTS
                lo, hi = (512 * i, 512 * i + 512) if kind == "ada" else (WIN_CUTS[i], WIN_CUTS[i + 1])
                src = (ada_w if kind == "ada" else w_in)[:, :, lo:hi]
                dst = ring[:, s * MAX_CHUNK:s * MAX_CHUNK + KD * (hi - lo)].rearrange("p (k n) -> p k n", k=KD)
                sp.dma_start(dst, src).then_inc(slot_in[s], 16)
            sp.wait_ge(ada_used, 12)
            sp.wait_ge(filled, plan.at["yT", NT - 1] + 1)
            w_out = a["w_out"][0].rearrange("(k p) n -> p k n", p=P)
            sp.dma_start(ring[:, 0:KD * D].rearrange("p (k n) -> p k n", k=KD), w_out).then_inc(wo_in, 16)
            sp.wait_ge(trig_ready, 1)
            sp.dma_start(router_w, a["router_w"][0].rearrange("(k p) e -> p k e", p=P)).then_inc(rw_in, 16)
            w1_d = a["exp_w1"][0].rearrange("e (k p) n -> e k p n", p=P)
            w2_d = a["exp_w2"][0].rearrange("e (k p) n -> e k p n", p=P)
            sp.wait_ge(filled, plan.at["wo", KD - 1] + 1)
            sp.sem_inc(w1_free, KD)
            sp.sem_inc(w2_free, KD)
            sp.wait_ge(npass_ready, 1)
            passes = sp.value_load(n_pass[0:1, 0:1], min_val=1, max_val=4)
            with sp.Fori(0, passes) as j:
                with sp.Fori(0, EXPERTS) as e:
                    it = j * EXPERTS + e
                    sp.wait_ge(lin_ready, it + 1)
                    sp.dma_start(B1, a["exp_b1"][0][bass.ds(e, 1), :].to_broadcast([P, 2 * FF])).then_inc(b1_in, 16)
                    for k in range(KD):
                        sp.wait_ge(w1_free, it * KD + (k + 1))
                        sp.dma_start(w1_slot(k), w1_d[bass.ds(e, 1), k].rearrange("o p n -> p (o n)")).then_inc(w1_in[k], 16)
                    for k in range(KD):
                        sp.wait_ge(w2_free, it * KD + (k + 1))
                        sp.dma_start(w2_slot(k), w2_d[bass.ds(e, 1), k].rearrange("o p n -> p (o n)")).then_inc(w2_in[k], 16)
                    sp.wait_ge(ye_sb, it + 1)
                    sp.dma_start(B2, a["exp_b2"][0][bass.ds(e, 1), :].to_broadcast([P, D])).then_inc(b2_in, 16)
            w_in2 = a["w_in_2"][0].rearrange("(k p) n -> p k n", p=P)
            w_fi = a["w_ffn_in_2"][0].rearrange("(k p) n -> p k n", p=P)
            w_fo = a["w_ffn_out_2"][0].rearrange("(k p) n -> p k n", p=P)
            w_a = a["w_a_out_2"][0].rearrange("(k p) n -> p k n", p=P)
            w_b = a["w_b_out_2"][0].rearrange("(k p) n -> p k n", p=P)
            w_o = a["w_o_2"][0].rearrange("(k p) n -> p k n", p=P)
            sp.wait_ge(w2_free, passes * (EXPERTS * KD) + KD)
            for n, (name, _) in enumerate(chunks2):
                if n >= SLOTS:
                    sp.wait_ge(filled, plan.at[chunks2[n - SLOTS][1]] + 1)
                got = s2_in[n % SLOTS]
                if name == "q2":
                    sp.dma_start(slot2(name, KD, 512), w_in2[:, :, Q2:Q2 + 512]).then_inc(got, 16)
                elif name == "kv2":
                    sp.dma_start(slot2(name, KD, 512), w_in2[:, :, KV2:KV2 + 512]).then_inc(got, 16)
                elif name == "kc":
                    sp.dma_start(slot2(name, KD, 280)[:, :, 0:256], w_in2[:, :, KC:KC + 256]).then_inc(got, 16)
                    sp.dma_start(slot2(name, KD, 280)[:, :, 256:280], w_in2[:, :, G_NSA:G_NSA + 24]).then_inc(got, 16)
                elif name in ("ac", "ax", "ab"):
                    at = {"ac": A_C, "ax": A_X, "ab": A_B}[name]
                    sp.dma_start(slot2(name, KD, 512), w_in2[:, :, at:at + 512]).then_inc(got, 16)
                elif name in ("wa", "wb"):
                    sp.dma_start(slot2(name, 4, D), w_a if name == "wa" else w_b).then_inc(got, 16)
                elif name[0] == "mg":
                    for i in range(2):
                        at = G_MERGE + i * D + name[1] * 256
                        sp.dma_start(slot2(name, KD, 512)[:, :, i * 256:(i + 1) * 256], w_in2[:, :, at:at + 256]).then_inc(got, 16)
                elif name[0] == "w_o":
                    sp.dma_start(slot2(name, 4, D), w_o[:, 4 * name[1]:4 * name[1] + 4, :]).then_inc(got, 16)
                elif name[0] == "fi":
                    for i in range(2):
                        at = i * FF2 + name[1] * 256
                        sp.dma_start(slot2(name, KD, 512)[:, :, i * 256:(i + 1) * 256], w_fi[:, :, at:at + 256]).then_inc(got, 16)
                else:
                    lo, hi = 4 * name[1], min(4 * name[1] + 4, KF)
                    sp.dma_start(slot2(name, hi - lo, D), w_fo[:, lo:hi, :]).then_inc(got, 16)
            o = out.rearrange("(k p) t -> p k t", p=P)
            for m in range(KD):
                sp.wait_ge(fo_sb, m + 1)
                sp.dma_start(o[:, m, :], xT[:, m, :]).then_inc(out_sent, 16)
            sp.wait_ge(out_sent, 16 * KD)

        @block.gpsimd
        def _(pool):
            pool.wait_ge(x2_ready, 1)
            for j, name in enumerate(("cmp_k_w1_2", "cmp_v_w1_2")):
                src = a[name][0].rearrange("(i d) n -> d i n", d=HD)
                for g in range(2):
                    pool.dma_start(cmp_w1[j][g * HD:(g + 1) * HD, :, :], src).then_inc(cw_in, 16)
            for j, name in enumerate(("cmp_k_w2_2", "cmp_v_w2_2")):
                pool.dma_start(cmp_w2[0:HD, j * HD:(j + 1) * HD], a[name][0]).then_inc(cw_in, 16)

        @block.scalar
        def _(act):
            chained = [0]

            def link(ins):
                chained[0] += 1
                ins.then_inc(act_chain, 1)
                act.wait_ge(act_chain, chained[0])

            def take(key, *args, **kw):
                act.wait_ge(filled, plan.at[key] + 1)
                act.activation(args[0], bank[plan.bank(key)][:, :] if len(args) < 3 else args[2], args[1], **kw)\
                   .then_inc(evac[plan.bank(key)], 1)

            def squares(stage):
                for k in range(KD):
                    act.activation(hT[:, k, :], xT[:, k, :], ACT.Square).then_inc(sq_ready, 1)

            def root(stage):
                act.wait_ge(ss_done, stage + 1)
                act.activation(rstd, bank[4][:, :], ACT.Sqrt, scale=1.0 / D, bias=eps(0)).then_inc(rs_ready, 1)

            act.wait_ge(vec_in, 16)
            act.activation(sigc, vec[:, VEC_AT["c"]:VEC_AT["c"] + KD], ACT.Sigmoid).then_inc(sig_c, 1)
            act.wait_ge(x_in, 16)
            act.wait_ge(cst_in, 16)
            act.wait_ge(angles, 1)
            act.activation(cos_sin[:, :, :, :].rearrange("p j t f -> p (j t f)"), trig[:, 0:256], ACT.Sin).then_inc(trig_ready, 1)
            squares(0)
            root(0)

            act.wait_ge(cond_ready, 1)
            for m in range(NZ):
                act.wait_ge(filled, plan.at["z", m] + 1)
                act.activation(zs(m), bank[plan.bank(("z", m))][:, :], ACT.Copy, scale=omu[:, m:m + 1]).then_inc(z_scaled, 1)
            for m in range(NZ, 22):
                take(("z", m), zs(m), ACT.Copy)
            for t in range(NT):
                take(("v", t), v_sb[:, t, :], ACT.Copy)

            tile_evacuated(act, ("z", 12))
            act.activation(zs(12)[0:64], zs(12)[0:64], ACT.Tanh).then_inc(gates_lo, 1)
            tile_evacuated(act, ("z", 13))
            act.activation(zs(13), zs(13), ACT.Sigmoid).then_inc(gates_lo, 1)
            act.wait_ge(ada_used, 12)
            for c in range(4):
                take(("wag", c, 0), sigw[:, c, :], ACT.Sigmoid, bias=col("decay_w0", c))
                take(("wag", c, 1), aT[:, c, :], ACT.Sigmoid, bias=col("iclr_a0", c))
                take(("wag", c, 2), gT[:, c, :], ACT.Copy)
            for c in range(4):
                act.wait_ge(kk0_ready, c + 1)
                act.activation(nrm[:, c, :], kkT[:, c, :], ACT.Square).then_inc(kk2_ready, 1)
            for c in range(4):
                take(("kk", c), nrm[:, c, :], ACT.Sqrt)
            act.wait_ge(mid_ready, 1)
            for c in range(4):
                for k in range(NT):
                    act.activation(E1[:, c, k, :], S1[:, c, k, :], ACT.Exp, scale=-DECAY_K, bias=mids[:, c, k:k + 1])
                    act.activation(E2[:, c, k, :], S1[:, c, k, 1:129], ACT.Exp, scale=DECAY_K, bias=nmids[:, c, k:k + 1]).then_inc(exp_ready, 1)
            act.activation(small[:, 32:48], small[:, 0:16], ACT.Exp, scale=-1.0).then_inc(exp_ready, 1)
            act.wait_ge(prep_done, 4)
            for k in range(NT):
                for j, dst in enumerate((v_tok, kt_tok, bt_tok)):
                    take(("tok", k, j), dst[:, k, :], ACT.Copy)
            for k in range(NT):
                act.wait_ge(w_mm, k + 1)
                act.activation(W_sb, bank[6][:, :], ACT.Copy).then_inc(w_sb, 1)
                act.wait_ge(u_mm, k + 1)
                if k:
                    act.wait_ge(s_mm, k)
                act.activation(U_sb, bank[7][:, :], ACT.Copy, scale=-1.0).then_inc(u_sb, 1)
                act.wait_ge(var_ready, k + 1)
                act.activation(hstd, hvar, ACT.Sqrt, scale=1.0 / HD, bias=eps(1)).then_inc(std_ready, 1)
                act.wait_ge(filled, plan.at["yT", k] + 1)
                src = bank[plan.bank(("yT", k))]
                for c in range(4):
                    ins = act.activation(mixT(c)[:, k * P:(k + 1) * P], src[:, c * P:(c + 1) * P], ACT.Identity,
                                         scale=col("lnx_w", c), bias=col("lnx_b", c))
                ins.then_inc(evac[plan.bank(("yT", k))], 1)

            for i in range(8):
                act.activation(R(40 + i), A(14 + i), ACT.Square).then_inc(qk2_ready, 1)
            for i in range(8):
                take(("sbn", i), R(40 + i), ACT.Sqrt, scale=1.0 / HD, bias=eps(0))
            for h in range(NH):
                act.wait_ge(l_mm, h + 1)
                if h >= 2:
                    act.wait_ge(r_mm, (h - 1) * NT)
                for kt in range(NT):
                    ins = act.activation(sb_e(h, kt), sb_logits(h, kt), ACT.Abs)
                link(ins)
                for kt in range(NT):
                    ins = act.activation(sb_e(h, kt), sb_e(h, kt), ACT.Exp, scale=-1.0)
                link(ins)
                for kt in range(NT):
                    act.activation(sb_e(h, kt), sb_e(h, kt), ACT.Ln, bias=1.0).then_inc(ln_ready, 1)
                act.wait_ge(r_masked, NT * (h + 1))
                if h >= 2:
                    act.wait_ge(o_mm, h - 1)
                for kt in range(NT):
                    act.activation(sb_w(h, kt), sb_logits(h, kt), ACT.Exp).then_inc(wt_ready, 1)
            for t in range(NT):
                act.wait_ge(var_ready, NT + t + 1)
                act.activation(hstd, hvar, ACT.Sqrt, scale=1.0 / HD, bias=eps(0)).then_inc(std_ready, 1)
            for t in range(NT):
                act.wait_ge(filled, plan.at["oT", t] + 1)
                src = bank[plan.bank(("oT", t))]
                for c in range(4):
                    ins = act.activation(mixT(4 + c)[:, t * P:(t + 1) * P], src[:, c * P:(c + 1) * P], ACT.Copy,
                                         scale=col("sb_out_g", c))
                ins.then_inc(evac[plan.bank(("oT", t))], 1)

            for k in range(KD):
                tile_evacuated(act, ("wo", k))
            squares(1)
            root(1)
            for t in range(NT):
                for i in range(2):
                    take(("ht", t, i), h2_tok[:, t, i * T:(i + 1) * T], ACT.Copy)
            act.wait_ge(top_ready, 1)
            act.activation(TOPG, TOPG, ACT.Exp).then_inc(eg_ready, 1)
            act.wait_ge(gx_mm, 1)
            for i in range(2):
                ins = act.activation(XG[:, 4 * i:4 * i + 4, :].rearrange("p k s -> p (k s)"), bank[i][:, :], ACT.Copy)
            ins.then_inc(gx_sb, 1)
            act.sem_inc(aT_sb, 2)
            act.wait_ge(npass_ready, 1)
            passes = act.value_load(n_pass[0:1, 0:1], min_val=1, max_val=4)
            with act.Fori(0, passes) as j:
                with act.Fori(0, EXPERTS) as e:
                    it = j * EXPERTS + e
                    act.wait_ge(w2_free, it * KD + KD)
                    act.wait_ge(glu_ready, it + 1)
                    act.activation(SG, G, ACT.Sigmoid, scale=1.702).then_inc(sig_ready, 1)
                    act.wait_ge(gx_mm, it + 2)
                    for i in range(2):
                        ins = act.activation(XG[:, 4 * i:4 * i + 4, :].rearrange("p k s -> p (k s)"), bank[i][:, :], ACT.Copy)
                    ins.then_inc(gx_sb, 1)
                    act.wait_ge(ohT_mm, it + 2)
                    act.wait_ge(sc_mm, it * KD + KD)
                    act.activation(OHT, bank[4][:, :], ACT.Copy).then_inc(ohT_sb, 1)
                    for i, b in enumerate((5, 2)):
                        act.wait_ge(aT_mm, it * 2 + (i + 3))
                        act.activation(SG[:, i * T:(i + 1) * T], bank[b][:, :], ACT.Copy).then_inc(aT_sb, 1)

            act.wait_ge(x2_ready, 1)
            squares(2)
            root(2)
            for t in range(NT):
                take(("q2", t), q_tok[:, t, :], ACT.Copy)
            for t in range(NT):
                take(("kv2", t), kv_tok[:, t, :], ACT.Copy)
            take(("kc",), kcT, ACT.Copy)
            take(("vc",), vcT, ACT.Copy)
            for t in range(NT):
                act.wait_ge(filled, plan.at["g2", t] + 1)
                b = plan.bank(("g2", t))
                act.activation(nsa_gate[:, t, :], bank[b][:, 0:24], ACT.Sigmoid).then_inc(evac[b], 1)
            act.wait_ge(qn_sq, 1)
            act.activation(nmax[:, 0:48], nmax[:, 0:48], ACT.Sqrt, scale=1.0 / HD, bias=eps(0)).then_inc(qn_rt, 1)
            for c in range(4):
                take(("ac", c), yaT[:, c, :], ACT.Copy)
            for j in range(2):
                for g in range(2):
                    b = plan.bank(("hid", j, g))
                    act.wait_ge(filled, plan.at["hid", j, 1] + 1)
                    if g == 0:
                        link(act.activation(hbias[0:HD, j:j + 1], bank[b][0:HD, 64:65], ACT.Copy))
                    act.activation(hid[j][:, g, 0:N_CMP], bank[b][0:HD, 0:N_CMP], ACT.Silu, bias=hbias[0:HD, j:j + 1]).then_inc(evac[b], 1)
            act.wait_ge(kc_sq, 1)
            act.activation(cstat[0:N_CMP, 0:2], cstat[0:N_CMP, 0:2], ACT.Sqrt, scale=1.0 / HD, bias=eps(0)[0:N_CMP]).then_inc(kc_rt, 1)
            b = plan.bank(("kcT",))
            act.wait_ge(filled, plan.at["kcT",] + 1)
            act.activation(KcT, bank[b][:, 0:N_CMP], ACT.Copy).then_inc(evac[b], 1)
            for t in range(NT):
                b = plan.bank(("qkT", t))
                act.wait_ge(filled, plan.at["qkT", t] + 1)
                act.activation(QT[:, :, t * P:(t + 1) * P], bank[b][:, :].rearrange("p (c q) -> p c q", c=4), ACT.Copy).then_inc(evac[b], 1)
            for t in range(NT):
                b = plan.bank(("kkT", t))
                act.wait_ge(filled, plan.at["kkT", t] + 1)
                act.activation(A(14, 2).rearrange("p (b n) -> p b n", b=2)[:, :, t * P:(t + 1) * P],
                               bank[b][:, 0:256].rearrange("p (b n) -> p b n", b=2), ACT.Copy).then_inc(evac[b], 1)
            for t in range(NT):
                act.wait_ge(cs_ready, t + 1)
                act.activation(crow[:, 0:248], crow[:, 0:248], ACT.Exp).then_inc(cp_exp, 1)
                if t:
                    act.wait_ge(co_mm, t)
                for i in range(2):
                    b = plan.bank(("cT", t, i))
                    act.wait_ge(filled, plan.at["cT", t, i] + 1)
                    act.activation(cPT[0:N_CMP, 4 * i:4 * i + 4, :].rearrange("p h q -> p (h q)"), bank[b][0:N_CMP, :], ACT.Copy)\
                       .then_inc(evac[b], 1)
                act.wait_ge(co_mm, t + 1)
                act.activation(yb_tok[:, t, :], bank[4 + t % 2][:, :], ACT.Copy).then_inc(co_sb, 1)

            def turned(u):
                n = (u // 16 + 1) * P
                act.wait_ge(pt_mm, u + 1)
                if u >= 2:
                    act.wait_ge(o2_mm, u - 1)
                act.activation(PTb[u % 2][:, 0:n], bank[4 + u % 2][:, 0:n], ACT.Copy).then_inc(pt_sb, 1)
            for u in range(64):
                n = (u // 16 + 1) * P
                act.wait_ge(mx_ready, u + 1)
                if u >= 2:
                    act.wait_ge(pt_mm, u - 1)
                act.activation(Pb[u % 2][:, 0:n], s_bank(u)[:, 0:n], ACT.Exp, bias=nmax[:, u:u + 1],
                               accum_out=psum_[:, u:u + 1]).then_inc(p_ready, 1)
                if u:
                    turned(u - 1)
            turned(63)
            for t in range(NT):
                b = plan.bank(("ybT", t))
                act.wait_ge(filled, plan.at["ybT", t] + 1)
                act.activation(ybT[:, :, t * P:(t + 1) * P], bank[b][:, :].rearrange("p (c q) -> p c q", c=4), ACT.Copy).then_inc(evac[b], 1)
            for m in range(KD):
                for i in range(2):
                    if m >= 2:
                        act.wait_ge(mg_ready, m - 1)
                    take(("mg", m, i), A(24 + 2 * (m % 2) + i), ACT.Sigmoid)
            for k in range(KD):
                tile_evacuated(act, ("w_o", k))
            squares(3)
            root(3)
            for m in range(KF):
                if m >= 2:
                    act.wait_ge(conv_ready, m - 1)
                take(("gu", m, 0), A(22 + m % 2), ACT.Copy)
                act.wait_ge(conv_ready, m + 1)
                if m >= 2:
                    tile_evacuated(act, ("gu", m - 2, 1))
                act.activation(A(26 + m % 2), A(24 + m % 2), ACT.Silu).then_inc(silu_ready, 1)

        @block.vector
        def _(dve):
            chained = [0]

            def link(ins):
                chained[0] += 1
                ins.then_inc(dve_chain, 1)
                dve.wait_ge(dve_chain, chained[0])

            counts = {}

            def link_to(ins, signal, n=1):
                counts[signal.name] = counts.get(signal.name, 0) + n
                ins.then_inc(signal, n)
                dve.wait_ge(signal, counts[signal.name])

            def link_evac(ins, key):
                ins.then_inc(evac[plan.bank(key)], 1)
                tile_evacuated(dve, key)

            def row(name):
                return vec[:, VEC_AT[name]:VEC_AT[name] + ROW_COLS[name]]

            def four_k(x):
                return x.rearrange("p (b g d) -> p b g d", b=2, g=2)

            def kk_tok(t):
                return kv_tok[:, t, :].rearrange("p (b v g d) -> p b v g d", b=2, v=2, g=2)[:, :, 0, :, :]

            def conv(dst, src, w, bias, signal=None):
                if bias is None:
                    link(dve.tensor_scalar(dst, src, w[2], None, ALU.mult))
                else:
                    link(dve.tensor_scalar(dst, src, w[2], bias, ALU.mult, ALU.add))
                link(dve.scalar_tensor_tensor(out=dst[:, 1:T], in0=src[:, 0:T - 1], scalar=w[1], in1=dst[:, 1:T], op0=ALU.mult, op1=ALU.add))
                ins = dve.scalar_tensor_tensor(out=dst[:, 2:T], in0=src[:, 0:T - 2], scalar=w[0], in1=dst[:, 2:T], op0=ALU.mult, op1=ALU.add)
                if signal is None:
                    link(ins)
                else:
                    ins.then_inc(signal, 1)

            def gated(m):
                b = plan.bank(("gu", m, 1))
                dve.wait_ge(silu_ready, m + 1)
                dve.wait_ge(filled, plan.at["gu", m, 1] + 1)
                dve.tensor_tensor(actT(m), A(26 + m % 2), bank[b][:, :], ALU.mult).then_inc(evac[b], 1)

            def norm_plain(stage, name):
                dve.wait_ge(rs_ready, stage + 1)
                link(dve.reciprocal(rstd, rstd))
                for k in range(KD):
                    dve.scalar_tensor_tensor(out=hT[:, k, :], in0=xT[:, k, :], scalar=col(name, k), in1=rstd,
                                             op0=ALU.mult, op1=ALU.mult).then_inc(h_ready, 1)

            def norm_scale(stage, scale, shift):
                dve.wait_ge(rs_ready, stage + 1)
                link(dve.reciprocal(rstd, rstd))
                for k in range(KD):
                    ins = dve.tensor_tensor(hT[:, k, :], xT[:, k, :], rstd, ALU.mult)
                link(ins)
                for k in range(KD):
                    dve.tensor_scalar(hT[:, k, :], hT[:, k, :], scale(k), shift(k), ALU.mult, ALU.add).then_inc(h_ready, 1)

            dve.wait_ge(vec_in, 16)
            dve.wait_ge(pos_in, 16)
            dve.wait_ge(cst_in, 16)
            link(dve.tensor_copy(small[:, 120:124], u_pos[:, :]))
            ang, turns = trig[:, 128:256], trig[:, 256:384]
            for t in range(NT):
                ins = dve.tensor_scalar(ang[:, t * 32:(t + 1) * 32], const("inv_freq"), small[:, 120 + t:121 + t], None, ALU.mult)
            link(ins)
            link(dve.tensor_scalar(turns, ang, 1.0 / TURN, ROUNDER, ALU.mult, ALU.add))
            link(dve.tensor_scalar(turns, turns, ROUNDER, None, ALU.subtract))
            for part in TURN_PARTS:
                link(dve.scalar_tensor_tensor(out=ang, in0=turns, scalar=-part, in1=ang, op0=ALU.mult, op1=ALU.add))
            link(dve.tensor_scalar(ang, ang, PI_LOW, -PI_LOW, ALU.min, ALU.max))
            link(dve.tensor_scalar(trig[:, 0:128], ang, TURN / 4, None, ALU.add))
            link(dve.tensor_scalar(turns, trig[:, 0:128], TURN / 2, -TURN, ALU.is_gt, ALU.mult))
            link(dve.tensor_tensor(trig[:, 0:128], trig[:, 0:128], turns, ALU.add))
            dve.tensor_scalar(trig[:, 0:128], trig[:, 0:128], PI_LOW, -PI_LOW, ALU.min, ALU.max).then_inc(angles, 1)
            dve.tensor_scalar(omka, vec[:, VEC_AT["k_a"]:VEC_AT["k_a"] + 4], -1.0, 1.0, ALU.mult, ALU.add)
            dve.tensor_scalar(omu, vec[:, VEC_AT["shift_mu"]:VEC_AT["shift_mu"] + NZ], -1.0, 1.0, ALU.mult, ALU.add)
            dve.wait_ge(sig_c, 1)
            dve.tensor_tensor(cond, sigc, vec[:, VEC_AT["c"]:VEC_AT["c"] + KD], ALU.mult).then_inc(cond_ready, 1)
            dve.wait_ge(cond_ready, 1)

            def ada(n):
                s = slot_of["ada", n]
                dve.wait_ge(slot_in[s], 16 * load_of["ada", n])
                if n >= 2:
                    dve.wait_ge(mod_mm, n - 1)
                w = ring[:, s * MAX_CHUNK:(s + 1) * MAX_CHUNK].rearrange("p (k n) -> p k n", k=KD)
                link(dve.tensor_scalar(acc[n % 2], w[:, 0, :], cond[:, 0:1], None, ALU.mult))
                for k in range(1, KD - 1):
                    link(dve.scalar_tensor_tensor(out=acc[n % 2], in0=w[:, k, :], scalar=cond[:, k:k + 1], in1=acc[n % 2],
                                                  op0=ALU.mult, op1=ALU.add))
                k = KD - 1
                dve.scalar_tensor_tensor(out=acc[n % 2], in0=w[:, k, :], scalar=cond[:, k:k + 1], in1=acc[n % 2],
                                         op0=ALU.mult, op1=ALU.add).then_inc(ada_used, 1)

            def modulation(lo, hi, chunks_done):
                dve.wait_ge(mod_mm, chunks_done)
                link(dve.tensor_tensor(mod[:, lo:hi], bank[5][:, lo:hi], vec[:, VEC_AT["ada_b"] + lo:VEC_AT["ada_b"] + hi], ALU.add))

            for n in range(4):
                ada(n)
            modulation(0, 16, 4)
            link(dve.scalar_tensor_tensor(out=gain[:, :], in0=mod[:, 8:16], scalar=1.0,
                                          in1=vec[:, VEC_AT["norm1_g"]:VEC_AT["norm1_g"] + KD], op0=ALU.add, op1=ALU.mult))
            norm_scale(0, lambda k: gain[:, k:k + 1], lambda k: mod[:, k:k + 1])
            later = 4
            for m in range(NZ):
                b = plan.bank(("z", m))
                dve.wait_ge(z_scaled, m + 1)
                dve.scalar_tensor_tensor(out=zs(m)[:, 1:T], in0=bank[b][:, 0:T - 1], scalar=col("shift_mu", m),
                                         in1=zs(m)[:, 1:T], op0=ALU.mult, op1=ALU.add).then_inc(evac[b], 1)
                if m % 2 == 1 and later < 12:
                    ada(later)
                    later += 1
            while later < 12:
                ada(later)
                later += 1
            modulation(16, 48, 12)

            dve.wait_ge(filled, plan.at["v", NT - 1] + 1)
            for c in range(4):
                dve.tensor_scalar(kkT[:, c, :], zs(4 + c), col("k_k", c), None, ALU.mult).then_inc(kk0_ready, 1)
            link(dve.memset(S1[:, :, :, 0:1], 0.0))
            for c in range(4):
                tile_evacuated(dve, ("wag", c, 0))
                for k in range(NT):
                    s = sigw[:, c, k * P:(k + 1) * P]
                    ins = dve.tensor_tensor_scan(S1[:, c, k, 1:129], ones, s, 0.0, ALU.mult, ALU.add)
            link(ins)
            dve.tensor_scalar(mids, S1[:, :, :, 64], DECAY_K, None, ALU.mult)
            dve.tensor_scalar(nmids, S1[:, :, :, 64], -DECAY_K, None, ALU.mult).then_inc(mid_ready, 1)
            for c in range(4):
                tile_evacuated(dve, ("wag", c, 1))
                t = KR[:, c, 0, :]
                link(dve.tensor_scalar(t, aT[:, c, :], col("k_a", c), omka[:, c:c + 1], ALU.mult, ALU.add))
                link(dve.tensor_tensor(zs(4 + c), zs(4 + c), t, ALU.mult))
                dve.scalar_tensor_tensor(out=KR[:, c, 1, :], in0=zs(c), scalar=col("r_k", c), in1=zs(4 + c),
                                         op0=ALU.mult, op1=ALU.mult).then_inc(rk_ready, 1)
            for c in range(4):
                b = plan.bank(("rk", c))
                dve.wait_ge(filled, plan.at["rk", c] + 1)
                dve.tensor_tensor(bonus[:, c, :], bank[b][:, :], zs(8 + c), ALU.mult).then_inc(evac[b], 1)
                tile_evacuated(dve, ("kk", c))
                link(dve.tensor_scalar(nrm[:, c, :], nrm[:, c, :], L2_EPS, None, ALU.max))
                link(dve.reciprocal(nrm[:, c, :], nrm[:, c, :]))
                link(dve.tensor_tensor(kkT[:, c, :], kkT[:, c, :], nrm[:, c, :], ALU.mult))
                dve.wait_ge(exp_ready, 4 * (c + 1))
                four = lambda x: x.rearrange("p (k t) -> p k t", k=NT)
                dve.tensor_tensor(four(KR[:, c, 0, :]), four(kkT[:, c, :]), E1[:, c, :, 0:128], ALU.mult)
                dve.tensor_tensor(four(KR[:, c, 1, :]), four(zs(c)), E1[:, c, :, 1:129], ALU.mult)
                dve.tensor_tensor(four(ktT[:, c, :]), four(zs(4 + c)), E2[:, c, :, :], ALU.mult)
                link(dve.tensor_tensor(aT[:, c, :], aT[:, c, :], kkT[:, c, :], ALU.mult))
                dve.tensor_tensor(four(btT[:, c, :]), four(aT[:, c, :]), E2[:, c, :, :], ALU.mult).then_inc(prep_done, 1)
            dve.wait_ge(exp_ready, 17)
            link(dve.tensor_tensor(dec[:, :, 0:3], E1[:, :, 0:3, 128], emid[:, :, 1:4], ALU.mult))
            link(dve.tensor_copy(dec[:, :, 3], E1[:, :, 3, 128]))
            tile_evacuated(dve, ("wag", 3, 2))
            dve.memset(S_sc, 0.0).then_inc(s_sb, 1)

            both = [const("strict"), const("incl")]
            mask2 = cst[:, CONST_AT["strict"]:CONST_AT["strict"] + 2 * P]
            q = 0
            for k in range(NT):
                for h in range(NH):
                    b = plan.bank(("am", k, h))
                    dve.wait_ge(filled, plan.at["am", k, h] + 1)
                    dve.tensor_tensor(AM[:, h, :].rearrange("p (j n) -> p j n", j=2),
                                      bank[b][:, :].rearrange("p (j n) -> p j n", j=2),
                                      mask2[:, None, :].to_broadcast([P, 2, 2 * P]), ALU.mult).then_inc(evac[b], 1)
                dve.tensor_copy(X[:, :, :], ident[:, None, :].to_broadcast([P, NH, P])).then_inc(x_sb, 1)
                dve.tensor_copy(XT[:, :, :], ident[:, None, :].to_broadcast([P, NH, P])).then_inc(xt_sb, 1)
                for lv in range(7):
                    mask = const("level")[:, lv * P:(lv + 1) * P]
                    for g in range(2):
                        hs = slice(4 * g, 4 * g + 4)
                        dve.wait_ge(t1_mm, (k * 7 + lv) * 2 + g + 1)
                        dve.tensor_tensor(T1[:, hs, :], bank[4 + g][:, :].rearrange("p (h n) -> p h n", h=4),
                                          mask[:, None, :].to_broadcast([P, 4, P]), ALU.mult).then_inc(t1_sb, 1)
                    for g in range(2):
                        hs = slice(4 * g, 4 * g + 4)
                        if lv < 6:
                            dve.wait_ge(xn_mm, (k * 6 + lv) * 2 + g + 1)
                            dve.tensor_tensor(X[:, hs, :], X[:, hs, :], bank[6 + g][:, :].rearrange("p (h n) -> p h n", h=4),
                                              ALU.subtract).then_inc(x_sb, 1)
                        dve.wait_ge(xt_mm, (k * 7 + lv) * 2 + g + 1)
                        dve.tensor_tensor(XT[:, hs, :], XT[:, hs, :], bank[4 + g][:, :].rearrange("p (h n) -> p h n", h=4),
                                          ALU.subtract).then_inc(xt_sb, 1)
                dve.wait_ge(s_mm, k + 1)
                Sv = S_sc.rearrange("p (c n) -> p c n", c=4)
                Pv = bank[5][:, :].rearrange("p (c n) -> p c n", c=4)
                for half in range(2):
                    ps = slice(HD * half, HD * half + HD)
                    ins = dve.tensor_tensor(Sv[ps, :, ps], Sv[ps, :, ps], Pv[ps, :, ps], ALU.add)
                link(ins)
                for half in range(2):
                    ps = slice(HD * half, HD * half + HD)
                    ins = dve.tensor_tensor(Sv[ps, :, ps], Sv[ps, :, ps], dec[ps, :, k:k + 1].to_broadcast([HD, 4, HD]), ALU.mult)
                ins.then_inc(s_sb, 1)
                dve.wait_ge(y_mm, k + 1)
                heads = lambda x: x.rearrange("p (h d) -> p h d", h=NH)
                yv = heads(bank[4][:, :])
                link(dve.tensor_reduce(hsum, yv, AX.X, ALU.add))
                link(dve.tensor_scalar(hsum, hsum, 1.0 / HD, None, ALU.mult))
                if k:
                    tile_evacuated(dve, ("yT", k - 1))
                link(dve.tensor_tensor(heads(yn), yv, hsum[:, :, None].to_broadcast([P, NH, HD]), ALU.subtract))
                link(dve.tensor_tensor(ysq, yn, yn, ALU.mult))
                dve.tensor_reduce(hvar, heads(ysq), AX.X, ALU.add).then_inc(var_ready, 1)
                dve.wait_ge(std_ready, k + 1)
                link(dve.reciprocal(hrstd, hstd))
                dve.tensor_tensor(heads(yn), heads(yn), hrstd[:, :, None].to_broadcast([P, NH, HD]), ALU.mult).then_inc(yn_ready, 1)
            for k in range(NT):
                tile_evacuated(dve, ("yT", k))
            for c in range(4):
                link(dve.tensor_tensor(mixT(c), mixT(c), bonus[:, c, :], ALU.add))
                dve.tensor_tensor(mixT(c), mixT(c), gT[:, c, :], ALU.mult).then_inc(mix_ready, 1)

            for i in range(8):
                tile_evacuated(dve, ("sbn", i))
                link(dve.reciprocal(R(40 + i), R(40 + i)))
                g = col("q_norm_g") if i < 4 else col("k_norm_g")
                if i < 4:
                    link(dve.tensor_scalar(R(40 + i), R(40 + i), HD ** -0.5, None, ALU.mult))
                dve.scalar_tensor_tensor(out=A(14 + i), in0=A(14 + i), scalar=g, in1=R(40 + i), op0=ALU.mult, op1=ALU.mult)\
                   .then_inc(qkn_ready, 1)
            for h in range(NH):
                for kt in range(NT):
                    e = sb_e(h, kt)
                    dve.wait_ge(ln_ready, h * NT + kt + 1)
                    link(dve.scalar_tensor_tensor(out=e, in0=sb_logits(h, kt), scalar=0.0, in1=e, op0=ALU.max, op1=ALU.add))
                    dve.tensor_tensor(e[:, 0:P], e[:, 0:P], const("strict"), ALU.mult).then_inc(sp_ready, 1)
                for kt in range(NT):
                    dve.wait_ge(r_mm, NT * (h + 1))
                for kt in range(NT):
                    diag = sb_logits(h, kt)[:, 0:P]
                    dve.tensor_tensor(diag, diag, const("sb_mask"), ALU.add).then_inc(r_masked, 1)
                dve.wait_ge(o_mm, h + 1)
                dve.tensor_copy(o_tok[:, :, h * HD:(h + 1) * HD], sb_out(h).rearrange("p (t d) -> p t d", t=4)).then_inc(o_sb, 1)
            dve.wait_ge(o_sb, NH)
            for t in range(NT):
                heads = lambda x: x.rearrange("p (h d) -> p h d", h=NH)
                link(dve.tensor_tensor(ysq, o_tok[:, t, :], o_tok[:, t, :], ALU.mult))
                dve.tensor_reduce(hvar, heads(ysq), AX.X, ALU.add).then_inc(var_ready, 1)
                dve.wait_ge(std_ready, NT + t + 1)
                link(dve.reciprocal(hrstd, hstd))
                dve.tensor_tensor(heads(o_tok[:, t, :]), heads(o_tok[:, t, :]), hrstd[:, :, None].to_broadcast([P, NH, HD]), ALU.mult)\
                   .then_inc(on_ready, 1)
            for m in range(KD):
                b = plan.bank(("wo", m))
                dve.wait_ge(filled, plan.at["wo", m] + 1)
                dve.scalar_tensor_tensor(out=xT[:, m, :], in0=bank[b][:, :], scalar=mod[:, 16 + m:17 + m], in1=xT[:, m, :],
                                         op0=ALU.mult, op1=ALU.add).then_inc(evac[b], 1)

            link(dve.scalar_tensor_tensor(out=gain[:, :], in0=mod[:, 32:40], scalar=1.0,
                                          in1=vec[:, VEC_AT["norm2_g"]:VEC_AT["norm2_g"] + KD], op0=ALU.add, op1=ALU.mult))
            norm_scale(1, lambda k: gain[:, k:k + 1], lambda k: mod[:, 24 + k:25 + k])
            for t in range(NT):
                b = plan.bank(("lg", t))
                dve.wait_ge(filled, plan.at["lg", t] + 1)
                link_evac(dve.tensor_tensor(LG[:, t, :], bank[b][:, 0:EXPERTS], row("router_b"), ALU.add), ("lg", t))
            for t in range(NT):
                link(dve.max(TOPV[:, t, :], LG[:, t, :]))
                ins = dve.max_index(top_idx[:, t, :], TOPV[:, t, :], LG[:, t, :])
            link(ins)
            dve.tensor_copy(TOPF, top_idx[:, :, :])
            dve.tensor_tensor(TOPG, TOPV[:, :, 0:TOP_K], TOPV[:, :, 0:1].to_broadcast([P, NT, TOP_K]), ALU.subtract).then_inc(top_ready, 1)
            dve.wait_ge(eg_ready, 1)
            link(dve.tensor_reduce(GSUM, TOPG, AX.X, ALU.add))
            link(dve.reciprocal(GSUM, GSUM))
            link(dve.tensor_tensor(TOPG, TOPG, GSUM[:, :, None].to_broadcast([P, NT, TOP_K]), ALU.mult))
            for t in range(NT):
                link(dve.tensor_scalar(SEL[:, t, :], const("expert"), TOPF[:, t, 0:1], None, ALU.is_equal))
                link(dve.tensor_scalar(GATE[:, t, :], const("expert"), TOPF[:, t, 0:1], TOPG[:, t, 0:1], ALU.is_equal, ALU.mult))
                for r in range(1, TOP_K):
                    link(dve.scalar_tensor_tensor(out=SEL[:, t, :], in0=const("expert"), scalar=TOPF[:, t, r:r + 1], in1=SEL[:, t, :],
                                                  op0=ALU.is_equal, op1=ALU.add))
                    link(dve.tensor_scalar(GTMP, const("expert"), TOPF[:, t, r:r + 1], TOPG[:, t, r:r + 1], ALU.is_equal, ALU.mult))
                    link(dve.tensor_tensor(GATE[:, t, :], GATE[:, t, :], GTMP, ALU.add))
            link_to(dve.memset(moeT[:, :, :], 0.0), route_ready)
            for t in range(NT):
                b = plan.bank(("pos", t))
                dve.wait_ge(filled, plan.at["pos", t] + 1)
                link_evac(dve.scalar_tensor_tensor(out=POS[:, t, 0:EXPERTS], in0=bank[b][:, 0:EXPERTS], scalar=1.0, in1=SEL[:, t, :],
                                                   op0=ALU.add, op1=ALU.mult), ("pos", t))
            link(dve.tensor_scalar(POS[:, :, 0:EXPERTS], POS[:, :, 0:EXPERTS], -1.0, None, ALU.add))
            link(dve.tensor_scalar(POS[:, :, EXPERTS:EXPERTS + 1], POS[:, :, 0:1], -float(P), None, ALU.add))
            b = plan.bank(("cnt",))
            dve.wait_ge(filled, plan.at["cnt",] + 1)
            link_evac(dve.tensor_reduce(NPF[:, 0:1], bank[b][:, 0:EXPERTS], AX.X, ALU.max), ("cnt",))
            link(dve.tensor_scalar(NPF[:, 1:2], NPF[:, 0:1], 128.5, 1.0, ALU.is_gt, ALU.add))
            link(dve.scalar_tensor_tensor(out=NPF[:, 1:2], in0=NPF[:, 0:1], scalar=256.5, in1=NPF[:, 1:2], op0=ALU.is_gt, op1=ALU.add))
            link(dve.scalar_tensor_tensor(out=NPF[:, 1:2], in0=NPF[:, 0:1], scalar=384.5, in1=NPF[:, 1:2], op0=ALU.is_gt, op1=ALU.add))
            dve.tensor_copy(n_pass[:, :], NPF[:, 1:2]).then_inc(npass_ready, 1)
            dve.memset(Y, 0.0).then_inc(ye_sb, 1)
            dve.memset(OHT, 0.0).then_inc(ohT_sb, 1)
            dve.sem_inc(lin_ready, 1)

            def slot_map(dst, e, gates):
                for t in range(NT):
                    at = POS[:, t, bass.ds(e, 1)]
                    if gates:
                        ins = dve.tensor_scalar(dst[:, t, :], const("iota"), at, GATE[:, t, bass.ds(e, 1)], ALU.is_equal, ALU.mult)
                    else:
                        ins = dve.tensor_scalar(dst[:, t, :], const("iota"), at, None, ALU.is_equal)
                return ins
            slot_map(OH, 0, False).then_inc(oh_ready, 1)
            dve.wait_ge(npass_ready, 1)
            passes = dve.value_load(n_pass[0:1, 0:1], min_val=1, max_val=4)
            LINKS = 3
            with dve.Fori(0, passes) as j:
                with dve.Fori(0, EXPERTS) as e:
                    it = j * EXPERTS + e
                    dve.wait_ge(gx_mm, it + 1)
                    slot_map(OH, e + 1, False).then_inc(oh_ready, 1)
                    dve.wait_ge(ohT_mm, it + 1)
                    slot_map(OHG, e, True).then_inc(ohg_ready, 1)
                    dve.wait_ge(w1_free, it * KD + 2 * KD)
                    dve.wait_ge(b1_in, it * 16 + 16)
                    dve.wait_ge(aT_mm, it * 2 + 2)
                    for i in range(2):
                        ins = dve.tensor_tensor(G[:, i * T:(i + 1) * T], bank[i][:, :], B1[:, i * T:(i + 1) * T], ALU.add)
                    ins.then_inc(moe_chain, 1)
                    dve.wait_ge(moe_chain, it * LINKS + 1)
                    dve.tensor_scalar(G, G, 7.0, None, ALU.min).then_inc(glu_ready, 1)
                    for i in range(2):
                        ins = dve.tensor_tensor(LIN[:, i * T:(i + 1) * T], bank[2 + i][:, :], B1[:, (2 + i) * T:(3 + i) * T], ALU.add)
                    ins.then_inc(lin_ready, 1)
                    dve.wait_ge(lin_ready, it + 2)
                    dve.tensor_scalar(LIN, LIN, 7.0, -7.0, ALU.min, ALU.max).then_inc(moe_chain, 1)
                    dve.wait_ge(moe_chain, it * LINKS + 2)
                    dve.scalar_tensor_tensor(out=LIN, in0=LIN, scalar=1.0, in1=G, op0=ALU.add, op1=ALU.mult).then_inc(moe_chain, 1)
                    dve.wait_ge(moe_chain, it * LINKS + 3)
                    dve.wait_ge(sig_ready, it + 1)
                    dve.tensor_tensor(G, LIN, SG, ALU.mult).then_inc(act_ready, 1)
                    for m in range(KD):
                        dve.wait_ge(sc_mm, it * KD + (m + 1))
                        dve.tensor_tensor(moeT[:, m, :], moeT[:, m, :], bank[6 + m % 2][:, :], ALU.add).then_inc(sc_sb, 1)
                    dve.wait_ge(w2_free, it * KD + 2 * KD)
                    dve.wait_ge(b2_in, it * 16 + 16)
                    for i in range(2):
                        ins = dve.tensor_tensor(Y[:, i * T:(i + 1) * T], bank[6 + i][:, :], B2[:, i * T:(i + 1) * T], ALU.add)
                    ins.then_inc(ye_sb, 1)
                dve.wait_ge(oh_ready, j * EXPERTS + EXPERTS + 1)
                dve.tensor_scalar(POS, POS, -float(P), None, ALU.add).then_inc(pos_out, 1)
                dve.wait_ge(pos_out, j + 1)
            for m in range(KD):
                dve.wait_ge(sc_mm, passes * (EXPERTS * KD) + (m + 1))
                ins = dve.tensor_tensor(moeT[:, m, :], moeT[:, m, :], bank[6 + m % 2][:, :], ALU.add)
                ins.then_inc(sc_sb, 1)
            dve.wait_ge(sc_sb, passes * (EXPERTS * KD) + KD)
            for m in range(KD):
                ins = dve.scalar_tensor_tensor(out=xT[:, m, :], in0=moeT[:, m, :], scalar=mod[:, 40 + m:41 + m], in1=xT[:, m, :],
                                               op0=ALU.mult, op1=ALU.add)
            link_to(ins, x2_ready)

            norm_plain(2, "norm1_g_2")
            for t in range(NT):
                tile_evacuated(dve, ("q2", t))
                tile_evacuated(dve, ("kv2", t))
                link(dve.tensor_tensor(scr, q_tok[:, t, :], q_tok[:, t, :], ALU.mult))
                dve.tensor_reduce(stats[:, t, 0:8], scr.rearrange("p (h d) -> p h d", h=8), AX.X, ALU.add)
                link(dve.tensor_tensor(four_k(scr2[:, 0:256]), kk_tok(t), kk_tok(t), ALU.mult))
                ins = dve.tensor_reduce(stats[:, t, 8:12], scr2[:, 0:256].rearrange("p (h d) -> p h d", h=4), AX.X, ALU.add)
            ins.then_inc(qn_sq, 1)
            dve.wait_ge(qn_rt, 1)
            link(dve.reciprocal(nmax[:, 0:48], nmax[:, 0:48]))
            link(dve.tensor_scalar(stats[:, :, 0:8], stats[:, :, 0:8], HD ** -0.5, None, ALU.mult))

            def rotate(n, x1, x2, o1, o2, t):
                shape = list(x1.shape)
                cos = cos_sin[:, 0, t, :]
                sin = cos_sin[:, 1, t, :]
                if len(shape) == 4:
                    cs = [c[:, None, None, :].to_broadcast(shape) for c in (cos, sin)]
                else:
                    cs = [c[:, None, :].to_broadcast(shape) for c in (cos, sin)]
                w = n * 32
                tmp = [scr[:, 0:w], scr[:, 256:256 + w], scr2[:, 0:w], scr2[:, 256:256 + w]]
                if len(shape) == 4:
                    tmp = [x.rearrange("p (a b d) -> p a b d", a=shape[1], b=shape[2]) for x in tmp]
                else:
                    tmp = [x.rearrange("p (a d) -> p a d", a=shape[1]) for x in tmp]
                dve.tensor_tensor(tmp[0], x1, cs[0], ALU.mult)
                dve.tensor_tensor(tmp[1], x2, cs[1], ALU.mult)
                dve.tensor_tensor(tmp[2], x2, cs[0], ALU.mult)
                link(dve.tensor_tensor(tmp[3], x1, cs[1], ALU.mult))
                dve.tensor_tensor(o1, tmp[0], tmp[1], ALU.subtract)
                return dve.tensor_tensor(o2, tmp[2], tmp[3], ALU.add)
            for t in range(NT):
                q = q_tok[:, t, :].rearrange("p (h d) -> p h d", h=8)
                link(dve.tensor_tensor(q, q, stats[:, t, 0:8, None].to_broadcast([P, 8, HD]), ALU.mult))
                link(dve.tensor_tensor(q, q, row("q_norm_g_2")[:, None, :].to_broadcast([P, 8, HD]), ALU.mult))
                src = q_tok[:, t, :].rearrange("p (j c d) -> p j c d", j=2, c=4)
                dst = q_tok[:, t, :].rearrange("p (c j d) -> p j c d", j=2, c=4)
                link_to(rotate(8, src[:, :, :, 0:32], src[:, :, :, 32:64], dst[:, :, :, 0:32], dst[:, :, :, 32:64], t), q_ready)
                k = kk_tok(t)
                link(dve.tensor_tensor(k, k, stats[:, t, 8:12].rearrange("p (b g) -> p b g", b=2)[:, :, :, None].to_broadcast([P, 2, 2, HD]), ALU.mult))
                g = row("k_norm_g_2")[:, HD:3 * HD].rearrange("p (b d) -> p b d", b=2)[:, :, None, :].to_broadcast([P, 2, 2, HD])
                link(dve.tensor_tensor(k, k, g, ALU.mult))
                link_to(rotate(4, k[:, :, :, 0:32], k[:, :, :, 32:64], k[:, :, :, 0:32], k[:, :, :, 32:64], t), k_ready)
            for c in range(4):
                tile_evacuated(dve, ("ac", c))
                dve.wait_ge(filled, plan.at["ax", c] + 1)
                link_evac(dve.tensor_tensor(yaT[:, c, :], bank[plan.bank(("ax", c))][:, :], yaT[:, c, :], ALU.mult), ("ax", c))
            for c in range(4):
                conv(scr, yaT[:, c, :], [col("conv_a_w_2", 4 * j + c) for j in range(3)], None)
                dve.wait_ge(filled, plan.at["ab", c] + 1)
                link_evac(dve.tensor_tensor(yaT[:, c, :], bank[plan.bank(("ab", c))][:, :], scr, ALU.mult), ("ab", c))
            b = plan.bank(("kvc",))
            dve.wait_ge(filled, plan.at["kvc",] + 1)
            dve.tensor_copy(v_cmp, bank[b][0:N_CMP, 128:256])
            link_evac(dve.tensor_copy(kcn, bank[b][0:N_CMP, 0:128]), ("kvc",))
            pair = lambda x: x.rearrange("p (g d) -> p g d", g=2)
            link(dve.tensor_tensor(scr[0:N_CMP, 0:P], kcn, kcn, ALU.mult))
            dve.tensor_reduce(cstat[0:N_CMP, 0:2], pair(scr[0:N_CMP, 0:P]), AX.X, ALU.add).then_inc(kc_sq, 1)
            dve.wait_ge(kc_rt, 1)
            link(dve.reciprocal(cstat[0:N_CMP, 0:2], cstat[0:N_CMP, 0:2]))
            link(dve.tensor_tensor(pair(kcn), pair(kcn), cstat[0:N_CMP, 0:2, None].to_broadcast([N_CMP, 2, HD]), ALU.mult))
            dve.tensor_tensor(pair(kcn), pair(kcn), row("k_norm_g_2")[0:N_CMP, None, 0:HD].to_broadcast([N_CMP, 2, HD]), ALU.mult)\
               .then_inc(kc_ready, 1)
            hk = lambda x: x.rearrange("p (h n) -> p h n", h=NH)
            sc = crow[:, 0:248]
            gate3 = lambda t, j: nsa_gate[:, t, :].rearrange("p (h j) -> p h j", j=3)[:, :, j]
            for t in range(NT):
                bias = const("cmp_bias")[:, t * 32:t * 32 + N_CMP]
                ok = const("cmp_mask")[:, t * 32:t * 32 + N_CMP]
                if t:
                    dve.wait_ge(filled, plan.at["cT", t - 1, 1] + 1)
                for g in range(2):
                    b = plan.bank(("cs", t, g))
                    dve.wait_ge(filled, plan.at["cs", t, g] + 1)
                    src = bank[b][:, 0:128].rearrange("p (h n) -> p h n", h=4)[:, :, 0:N_CMP]
                    link_evac(dve.tensor_tensor(hk(sc)[:, 4 * g:4 * g + 4, :], src, bias[:, None, :].to_broadcast([P, 4, N_CMP]), ALU.add), ("cs", t, g))
                link(dve.tensor_reduce(cmx, hk(sc), AX.X, ALU.max))
                dve.tensor_tensor(hk(sc), hk(sc), cmx[:, :, None].to_broadcast([P, NH, N_CMP]), ALU.subtract).then_inc(cs_ready, 1)
                dve.wait_ge(cp_exp, t + 1)
                link(dve.tensor_reduce(csum, hk(sc), AX.X, ALU.add))
                link(dve.reciprocal(csum, csum))
                link(dve.tensor_tensor(gs, csum, gate3(t, 0), ALU.mult))
                link(dve.tensor_tensor(hk(sc), hk(sc), gs[:, :, None].to_broadcast([P, NH, N_CMP]), ALU.mult))
                dve.tensor_tensor(hk(sc), hk(sc), ok[:, None, :].to_broadcast([P, NH, N_CMP]), ALU.mult).then_inc(cp_ready, 1)
            def combine(t):
                dve.wait_ge(p_ready, 16 * (t + 1))
                sums = psum_[:, 16 * t:16 * t + 16]
                link(dve.reciprocal(sums, sums))
                dve.wait_ge(o2_mm, 16 * (t + 1))
                dve.wait_ge(co_sb, t + 1)
                for j in range(2):
                    link(dve.tensor_tensor(gs, sums.rearrange("p (h j) -> p h j", j=2)[:, :, j], gate3(t, 1 + j), ALU.mult))
                    link(dve.tensor_tensor(hk(yb_tmp), hk(bank[j][:, :]), gs[:, :, None].to_broadcast([P, NH, HD]), ALU.mult))
                    ins = dve.tensor_tensor(yb_tok[:, t, :], yb_tok[:, t, :], yb_tmp, ALU.add)
                    if j == 0:
                        link(ins)
                link_to(ins, yb_ready)

            for u in range(64):
                t = u // 16
                s = s_bank(u)
                dve.wait_ge(s2_mm, u + 1)
                link(dve.tensor_tensor(s[:, t * P:(t + 1) * P], s[:, t * P:(t + 1) * P], const("causal"), ALU.add))
                dve.tensor_reduce(nmax[:, u:u + 1], s[:, 0:(t + 1) * P], AX.X, ALU.max, negate=True).then_inc(mx_ready, 1)
                if t and u % 16 == 1:
                    combine(t - 1)
            combine(NT - 1)
            for m in range(KD):
                for i in range(2):
                    tile_evacuated(dve, ("mg", m, i))
                for i in range(2):
                    g = A(24 + 2 * (m % 2) + i)
                    dve.wait_ge(filled, plan.at["mg", m, 2 + i] + 1)
                    link_evac(dve.tensor_tensor(g, g, bank[plan.bank(("mg", m, 2 + i))][:, :], ALU.mult), ("mg", m, 2 + i))
                dve.tensor_tensor(mix2(m), A(24 + 2 * (m % 2)), A(25 + 2 * (m % 2)), ALU.add).then_inc(mg_ready, 1)
            for m in range(KD):
                b = plan.bank(("w_o", m))
                dve.wait_ge(filled, plan.at["w_o", m] + 1)
                dve.tensor_tensor(xT[:, m, :], xT[:, m, :], bank[b][:, :], ALU.add).then_inc(evac[b], 1)
            norm_plain(3, "norm2_g_2")
            for m in range(KF):
                tile_evacuated(dve, ("gu", m, 0))
                if m >= 2:
                    dve.wait_ge(silu_ready, m - 1)
                conv(A(24 + m % 2), A(22 + m % 2), [col("ffn_conv_w_2", KF * j + m) for j in range(3)], col("ffn_conv_b_2", m), conv_ready)
                if m:
                    gated(m - 1)
            gated(KF - 1)
            for m in range(KD):
                dve.wait_ge(fo_mm, m + 1)
                dve.tensor_tensor(xT[:, m, :], xT[:, m, :], bank[m][:, :], ALU.add).then_inc(fo_sb, 1)

        @block.tensor
        def _(pe):
            mm = pe.matmul

            def turn(key, parts, rows=P):
                b = plan.bank(key)
                pe.wait_ge(evac[b], plan.turn(key))
                for c, x in enumerate(parts):
                    ins = pe.transpose(bank[b][0:rows, c * P:(c + 1) * P], x, ident)
                ins.then_inc(filled, 1)

            def fill(key, parts, cols=T):
                b = plan.bank(key)
                if plan.turn(key):
                    pe.wait_ge(evac[b], plan.turn(key))
                dst = bank[b][:, 0:cols]
                for i, (l, r) in enumerate(parts):
                    ins = mm(dst, l, r, start=(i == 0), stop=(i == len(parts) - 1))
                ins.then_inc(filled, 1)

            def mean_square(stage):
                for k in range(KD):
                    pe.wait_ge(sq_ready, stage * KD + k + 1)
                    ins = mm(bank[4][:, :], ones, hT[:, k, :], start=(k == 0), stop=(k == KD - 1))
                ins.then_inc(ss_done, 1)

            def sum_mod(n):
                pe.wait_ge(ada_used, n + 1)
                for j in range(4):
                    ins = mm(bank[5][:, 4 * n + j:4 * n + j + 1], acc[n % 2][:, j * P:(j + 1) * P], ones[:, 0:1], start=True, stop=True)
                ins.then_inc(mod_mm, 1)

            pe.wait_ge(cst_in, 16)
            mean_square(0)
            for n in range(4):
                sum_mod(n)
            later = 4
            for i in range(7):
                s = slot_of["win", i]
                width = WIN_CUTS[i + 1] - WIN_CUTS[i]
                w = ring[:, s * MAX_CHUNK:s * MAX_CHUNK + KD * width].rearrange("p (k n) -> p k n", k=KD)
                pe.wait_ge(slot_in[s], 16 * load_of["win", i])
                pe.wait_ge(h_ready, KD)
                if i < 6:
                    for j, m in enumerate(WIN_TILES[i]):
                        fill(("z", m), [(w[:, k, j * P:(j + 1) * P], hT[:, k, :]) for k in range(KD)])
                        if m >= 2 and m % 2 == 0 and later < 12 and m < NZ:
                            sum_mod(later)
                            later += 1
                else:
                    for t in range(NT):
                        fill(("v", t), [(hT[:, k, t * P:(t + 1) * P], w[:, k, :]) for k in range(KD)])
            while later < 12:
                sum_mod(later)
                later += 1

            pe.wait_ge(up_in, 48)
            pe.wait_ge(gates_lo, 2)
            for c in range(4):
                cs = slice(c * P, (c + 1) * P)
                fill(("wag", c, 0), [(up_wa[0:64, cs], zs(12)[0:64, :])])
                fill(("wag", c, 1), [(up_wa[64:128, cs], zs(12)[64:128, :])])
                fill(("wag", c, 2), [(up_g[:, cs], zs(13))])
            for c in range(4):
                pe.wait_ge(kk2_ready, c + 1)
                fill(("kk", c), [(head_ones, nrm[:, c, :])])
            for c in range(4):
                pe.wait_ge(rk_ready, c + 1)
                fill(("rk", c), [(head_ones, KR[:, c, 1, :])])
            pe.wait_ge(prep_done, 4)
            for k in range(NT):
                ks = slice(k * P, (k + 1) * P)
                for j, src in enumerate((lambda c: zs(8 + c)[:, ks], lambda c: ktT[:, c, ks], lambda c: btT[:, c, ks])):
                    key = ("tok", k, j)
                    b = plan.bank(key)
                    pe.wait_ge(evac[b], plan.turn(key))
                    for c in range(4):
                        ins = pe.transpose(bank[b][:, c * P:(c + 1) * P], src(c), ident)
                    ins.then_inc(filled, 1)
            for k in range(NT):
                ks = slice(k * P, (k + 1) * P)
                for h in range(NH):
                    hp, c = slice(HD * (h % 2), HD * (h % 2) + HD), h // 2
                    key = ("am", k, h)
                    b = plan.bank(key)
                    pe.wait_ge(evac[b], plan.turn(key))
                    rhs = KR[hp, c, :, ks]
                    mm(bank[b][:, 0:256], ktT[hp, c, ks], rhs, start=True, stop=True)
                    mm(bank[b][:, 256:512], btT[hp, c, ks], rhs, start=True, stop=True).then_inc(filled, 1)
                for h in range(NH):
                    tile_evacuated(pe, ("am", k, h))
                for lv in range(7):
                    for g in range(2):
                        done = 1 if lv == 0 else 1 + (lv - 1) * 2 + g + 1
                        pe.wait_ge(x_sb, k * 13 + done)
                        pe.wait_ge(xt_sb, k * 15 + done)
                        for h in range(4 * g, 4 * g + 4):
                            ins = mm(bank[4 + g][:, (h % 4) * P:(h % 4 + 1) * P], AM[:, h, 2 * P:3 * P], X[:, h, :], start=True, stop=True)
                        ins.then_inc(t1_mm, 1)
                    for g in range(2):
                        pe.wait_ge(t1_sb, (k * 7 + lv) * 2 + g + 1)
                        if lv < 6:
                            for h in range(4 * g, 4 * g + 4):
                                ins = mm(bank[6 + g][:, (h % 4) * P:(h % 4 + 1) * P], XT[:, h, :], T1[:, h, :], start=True, stop=True)
                            ins.then_inc(xn_mm, 1)
                        for h in range(4 * g, 4 * g + 4):
                            ins = mm(bank[4 + g][:, (h % 4) * P:(h % 4 + 1) * P], T1[:, h, :], XT[:, h, :], start=True, stop=True)
                        ins.then_inc(xt_mm, 1)
                pe.wait_ge(s_sb, k + 1)
                tile_evacuated(pe, ("tok", k, 2))
                for c in range(4):
                    cs = slice(c * P, (c + 1) * P)
                    mm(bank[6][:, cs], KR[:, c, 0, ks], S_sc[:, cs], start=True, stop=True)
                    for h in (2 * c, 2 * c + 1):
                        hs = slice(h * HD, (h + 1) * HD)
                        ins = mm(bank[6][:, hs], AM[:, h, 0:P], v_tok[:, k, hs], start=False, stop=True, skip_group_check=True)
                ins.then_inc(w_mm, 1)
                pe.wait_ge(w_sb, k + 1)
                pe.wait_ge(xt_sb, (k + 1) * 15)
                for h in range(NH):
                    hs = slice(h * HD, (h + 1) * HD)
                    ins = mm(bank[7][:, hs], XT[:, h, :], W_sb[:, hs], start=True, stop=True)
                ins.then_inc(u_mm, 1)
                pe.wait_ge(u_sb, k + 1)
                for c in range(4):
                    cs = slice(c * P, (c + 1) * P)
                    mm(bank[4][:, cs], KR[:, c, 1, ks], S_sc[:, cs], start=True, stop=True)
                    for h in (2 * c, 2 * c + 1):
                        hs = slice(h * HD, (h + 1) * HD)
                        mm(bank[4][:, hs], AM[:, h, P:2 * P], v_tok[:, k, hs], start=False, stop=True, skip_group_check=True)
                        ins = mm(bank[4][:, hs], AM[:, h, 3 * P:4 * P], U_sb[:, hs], start=False, stop=True, skip_group_check=True)
                ins.then_inc(y_mm, 1)
                for c in range(4):
                    cs = slice(c * P, (c + 1) * P)
                    mm(bank[5][:, cs], kt_tok[:, k, cs], v_tok[:, k, cs], start=True, stop=False)
                    ins = mm(bank[5][:, cs], bt_tok[:, k, cs], U_sb[:, cs], start=False, stop=True)
                ins.then_inc(s_mm, 1)
                pe.wait_ge(yn_ready, k + 1)
                key = ("yT", k)
                b = plan.bank(key)
                pe.wait_ge(evac[b], plan.turn(key))
                for c in range(4):
                    ins = pe.transpose(bank[b][:, c * P:(c + 1) * P], yn[:, c * P:(c + 1) * P], ident)
                ins.then_inc(filled, 1)

            for i in range(8):
                pe.wait_ge(qk2_ready, i + 1)
                fill(("sbn", i), [(head_ones, R(40 + i))])
            pe.wait_ge(qkn_ready, 8)

            def logits(h):
                hp, c = slice(HD * (h % 2), HD * (h % 2) + HD), h // 2
                if h >= 2:
                    pe.wait_ge(wt_ready, NT * (h - 1))
                    pe.wait_ge(o_sb, h - 1)
                for kt in (0, 1, 3, 2):
                    ins = mm(sb_logits(h, kt), k_sb[hp, c, kt * P:(kt + 1) * P], q_sb[hp, c, kt * P:T], start=(kt != 3), stop=True,
                       skip_group_check=True)
                ins.then_inc(l_mm, 1)

            def sums(h):
                for kt in range(NT - 1, -1, -1):
                    pe.wait_ge(sp_ready, h * NT + NT)
                    dst = sb_logits(h, kt)
                    ins = mm(dst, const("neg_tri"), sb_e(h, kt), start=False, stop=True, skip_group_check=True)
                    for k2 in range(kt + 1, NT):
                        ins = mm(dst[:, (k2 - kt) * P:], const("neg_ones"), sb_e(h, k2), start=False, stop=True, skip_group_check=True)
                    ins.then_inc(r_mm, 1)

            def values(h):
                hs = slice(h * HD, (h + 1) * HD)
                pe.wait_ge(wt_ready, NT * (h + 1))
                for t in range(NT):
                    for kt in range(t + 1):
                        ins = mm(sb_out(h)[:, t * HD:(t + 1) * HD], sb_w(h, kt)[:, (t - kt) * P:(t - kt + 1) * P], v_sb[:, kt, hs],
                                 start=(kt == 0), stop=(kt == t), skip_group_check=True)
                ins.then_inc(o_mm, 1)

            for i in range(8):
                tile_evacuated(pe, ("sbn", i))
            pe.wait_ge(s_sb, NT + 1)
            pe.wait_ge(yn_ready, NT)
            logits(0)
            for h in range(NH):
                if h + 1 < NH:
                    logits(h + 1)
                sums(h)
                values(h)
            for t in range(NT):
                key = ("oT", t)
                b = plan.bank(key)
                pe.wait_ge(on_ready, t + 1)
                pe.wait_ge(evac[b], plan.turn(key))
                for c in range(4):
                    ins = pe.transpose(bank[b][:, c * P:(c + 1) * P], o_tok[:, t, c * P:(c + 1) * P], ident)
                ins.then_inc(filled, 1)
            pe.wait_ge(wo_in, 16)
            pe.wait_ge(mix_ready, 4)
            for t in range(NT):
                tile_evacuated(pe, ("oT", t))
            w = ring[:, 0:KD * D].rearrange("p (k n) -> p k n", k=KD)
            for m in range(KD):
                fill(("wo", m), [(w[:, k, m * P:(m + 1) * P], mixT(k)) for k in range(KD)])

            mean_square(1)
            pe.wait_ge(h_ready, 2 * KD)
            for t in range(NT):
                ts = slice(t * P, (t + 1) * P)
                for i in range(2):
                    turn(("ht", t, i), [hT[:, 4 * i + c, ts] for c in range(4)])
            pe.wait_ge(rw_in, 16)
            for t in range(NT):
                ts = slice(t * P, (t + 1) * P)
                fill(("lg", t), [(hT[:, k, ts], router_w[:, k, :]) for k in range(KD)], cols=EXPERTS)
            pe.wait_ge(route_ready, 1)
            for t in range(NT):
                fill(("pos", t), [(ones, SEL[:, i, :]) for i in range(t)] + [(const("strict"), SEL[:, t, :])], cols=EXPERTS)
            fill(("cnt",), [(ones, SEL[:, t, :]) for t in range(NT)], cols=EXPERTS)
            for i in range(2):
                for t in range(NT):
                    tile_evacuated(pe, ("ht", t, i))
            for t in range(NT):
                tile_evacuated(pe, ("pos", t))
            tile_evacuated(pe, ("cnt",))

            def gather():
                for c in range(KD):
                    for t in range(NT):
                        ins = mm(bank[c // 4][:, (c % 4) * P:(c % 4 + 1) * P], h2_tok[:, t, c * P:(c + 1) * P], OH[:, t, :],
                                 start=(t == 0), stop=(t == NT - 1))
                ins.then_inc(gx_mm, 1)

            def scatter(it):
                pe.wait_ge(ye_sb, it + 1)
                pe.wait_ge(ohT_sb, it + 1)
                for m in range(KD):
                    if m >= 2:
                        pe.wait_ge(sc_sb, it * KD + (m - 1))
                    mm(bank[6 + m % 2][:, :], Y[:, m * P:(m + 1) * P], OHT, start=True, stop=True).then_inc(sc_mm, 1)
            pe.wait_ge(oh_ready, 1)
            gather()
            pe.sem_inc(ohT_mm, 1)
            pe.sem_inc(aT_mm, 2)
            pe.wait_ge(npass_ready, 1)
            passes = pe.value_load(n_pass[0:1, 0:1], min_val=1, max_val=4)
            with pe.Fori(0, passes) as j:
                with pe.Fori(0, EXPERTS) as e:
                    it = j * EXPERTS + e
                    pe.wait_ge(gx_sb, it + 1)
                    pe.wait_ge(lin_ready, it + 1)
                    pe.wait_ge(aT_sb, it * 2 + 2)
                    for k in range(KD):
                        pe.wait_ge(w1_in[k], it * 16 + 16)
                        for n in range(4):
                            ins = mm(bank[n][:, :], XG[:, k, :], w1_slot(k)[:, n * T:(n + 1) * T], start=(k == 0), stop=(k == KD - 1))
                        ins.then_inc(w1_free, 1)
                    scatter(it)
                    pe.wait_ge(oh_ready, it + 2)
                    pe.wait_ge(glu_ready, it + 1)
                    gather()
                    pe.wait_ge(ohg_ready, it + 1)
                    pe.wait_ge(ohT_sb, it + 1)
                    for t in range(NT):
                        ins = pe.transpose(bank[4][:, t * P:(t + 1) * P], OHG[:, t, :], ident)
                    ins.then_inc(ohT_mm, 1)
                    pe.wait_ge(act_ready, it + 1)
                    for i, b in enumerate((5, 2)):
                        for c in range(4):
                            ins = pe.transpose(bank[b][:, c * P:(c + 1) * P], G[:, (4 * i + c) * P:(4 * i + c + 1) * P], ident)
                        ins.then_inc(aT_mm, 1)
                    pe.wait_ge(sc_sb, it * KD + KD)
                    for k in range(KD):
                        if k % 4 == 0:
                            pe.wait_ge(aT_sb, it * 2 + (k // 4 + 3))
                        pe.wait_ge(w2_in[k], it * 16 + 16)
                        for n in range(2):
                            ins = mm(bank[6 + n][:, :], aT2[:, k, :], w2_slot(k)[:, n * T:(n + 1) * T], start=(k == 0), stop=(k == KD - 1))
                        ins.then_inc(w2_free, 1)
            scatter(passes * EXPERTS)

            pe.wait_ge(x2_ready, 1)
            mean_square(2)
            pe.wait_ge(h_ready, 3 * KD)
            loaded2(pe, "q2")
            w = slot2("q2", KD, 512)
            for t in range(NT):
                fill(("q2", t), [(hT[:, k, t * P:(t + 1) * P], w[:, k, :]) for k in range(KD)])
            loaded2(pe, "kv2")
            w = slot2("kv2", KD, 512)
            for t in range(NT):
                fill(("kv2", t), [(hT[:, k, t * P:(t + 1) * P], w[:, k, :]) for k in range(KD)])
            loaded2(pe, "kc")
            w = slot2("kc", KD, 280)
            fill(("kc",), [(w[:, k, 0:P], hT[:, k, :]) for k in range(KD)])
            fill(("vc",), [(w[:, k, P:2 * P], hT[:, k, :]) for k in range(KD)])
            for t in range(NT):
                fill(("g2", t), [(hT[:, k, t * P:(t + 1) * P], w[:, k, 256:280]) for k in range(KD)], cols=24)
            for name in ("ac", "ax", "ab"):
                loaded2(pe, name)
                w = slot2(name, KD, 512)
                for c in range(4):
                    fill((name, c), [(w[:, k, c * P:(c + 1) * P], hT[:, k, :]) for k in range(KD)])
            pe.wait_ge(cw_in, 16 * 6)
            tile_evacuated(pe, ("kc",))
            tile_evacuated(pe, ("vc",))
            for j, (src, pe_name) in enumerate(((kcT, "cmp_k_pe_2"), (vcT, "cmp_v_pe_2"))):
                for g in range(2):
                    key = ("hid", j, g)
                    b = plan.bank(key)
                    pe.wait_ge(evac[b], plan.turn(key))
                    gp = slice(g * HD, (g + 1) * HD)
                    for i in range(CMP_BLOCK):
                        ins = mm(bank[b][0:HD, 0:N_CMP], cmp_w1[j][gp, i, :], src[gp, i:i + CMP_STRIDE * (N_CMP - 1) + 1:CMP_STRIDE],
                                 start=(i == 0), stop=(i == CMP_BLOCK - 1))
                    if g == 0:
                        for i in range(CMP_BLOCK):
                            at = VEC_AT[pe_name] + i
                            ins = mm(bank[b][0:HD, 64:65], cmp_w1[j][0:HD, i, :], vec[0:HD, at:at + 1], start=(i == 0), stop=(i == CMP_BLOCK - 1))
                    ins.then_inc(filled, 1)
            key = ("kvc",)
            b = plan.bank(key)
            pe.wait_ge(evac[b], plan.turn(key))
            for j in range(2):
                for g in range(2):
                    tile_evacuated(pe, ("hid", j, g))
                    ins = mm(bank[b][0:N_CMP, j * P + g * HD:j * P + (g + 1) * HD], hid[j][:, g, 0:N_CMP], cmp_w2[0:HD, j * HD:(j + 1) * HD],
                             start=True, stop=True)
            ins.then_inc(filled, 1)
            key = ("kcT",)
            b = plan.bank(key)
            pe.wait_ge(evac[b], plan.turn(key))
            pe.wait_ge(kc_ready, 1)
            pe.transpose(bank[b][:, 0:N_CMP], kcn, ident[0:N_CMP, 0:N_CMP]).then_inc(filled, 1)
            for t in range(NT):
                pe.wait_ge(q_ready, t + 1)
                turn(("qkT", t), [q_tok[:, t, c * P:(c + 1) * P] for c in range(4)])
            for t in range(NT):
                pe.wait_ge(k_ready, t + 1)
                turn(("kkT", t), [kv_tok[:, t, 2 * b * P:(2 * b + 1) * P] for b in range(2)])
            tile_evacuated(pe, ("kcT",))
            for t in range(NT):
                tile_evacuated(pe, ("qkT", t))
                tile_evacuated(pe, ("kkT", t))

            def head(h):
                return h % 4, slice(HD * (h // 4), HD * (h // 4) + HD)
            for t in range(NT):
                ts = slice(t * P, (t + 1) * P)
                for g in range(2):
                    key = ("cs", t, g)
                    b = plan.bank(key)
                    pe.wait_ge(evac[b], plan.turn(key))
                    for h in range(4 * g, 4 * g + 4):
                        c, hp = head(h)
                        ins = mm(bank[b][:, c * 32:c * 32 + N_CMP], QT[hp, c, ts], KcT[hp, :], start=True, stop=True)
                    ins.then_inc(filled, 1)
                pe.wait_ge(cp_ready, t + 1)
                for i in range(2):
                    turn(("cT", t, i), [crow[:, (4 * i + c) * N_CMP:(4 * i + c + 1) * N_CMP] for c in range(4)], rows=N_CMP)
                for i in range(2):
                    tile_evacuated(pe, ("cT", t, i))
                if t >= 2:
                    pe.wait_ge(co_sb, t - 1)
                for h in range(NH):
                    ins = mm(bank[4 + t % 2][:, h * HD:(h + 1) * HD], cPT[0:N_CMP, h, :], v_cmp[:, (h // 4) * HD:(h // 4 + 1) * HD],
                             start=True, stop=True)
                ins.then_inc(co_mm, 1)
            pe.wait_ge(co_sb, NT)

            def scores(u):
                t, h, j = u // 16, u % 16 // 2, u % 2
                c, hp = head(h)
                if u >= 4:
                    pe.wait_ge(p_ready, u - 3)
                mm(s_bank(u)[:, 0:(t + 1) * P], QT[hp, c, t * P:(t + 1) * P], (KselT, KwinT)[j][hp, 0:(t + 1) * P], start=True, stop=True)\
                    .then_inc(s2_mm, 1)

            def turn_weights(u):
                t = u // 16
                pe.wait_ge(p_ready, u + 1)
                if u >= 2:
                    pe.wait_ge(pt_sb, u - 1)
                for k in range(t + 1):
                    ins = pe.transpose(bank[4 + u % 2][:, k * P:(k + 1) * P], Pb[u % 2][:, k * P:(k + 1) * P], ident)
                ins.then_inc(pt_mm, 1)

            def weigh(u):
                t, h, j = u // 16, u % 16 // 2, u % 2
                if u % 16 < 2 and t:
                    pe.wait_ge(yb_ready, t)
                pe.wait_ge(pt_sb, u + 1)
                v = (2 * j + 1) * P + (h // 4) * HD
                for k in range(t + 1):
                    ins = mm(bank[j][:, h * HD:(h + 1) * HD], PTb[u % 2][:, k * P:(k + 1) * P], kv_tok[:, k, v:v + HD],
                             start=(k == 0), stop=(k == t))
                ins.then_inc(o2_mm, 1)
            scores(0)
            scores(1)
            for u in range(64):
                if u + 2 < 64:
                    scores(u + 2)
                if u:
                    weigh(u - 1)
                turn_weights(u)
            weigh(63)
            pe.wait_ge(yb_ready, NT)
            for t in range(NT):
                turn(("ybT", t), [yb_tok[:, t, c * P:(c + 1) * P] for c in range(4)])
            for t in range(NT):
                tile_evacuated(pe, ("ybT", t))
            for name in ("wa", "wb"):
                loaded2(pe, name)
            wa, wb = slot2("wa", 4, D), slot2("wb", 4, D)
            for m in range(KD):
                if m % 2 == 0:
                    loaded2(pe, ("mg", m // 2))
                w = slot2(("mg", m // 2), KD, 512)
                at = (m % 2) * P
                fill(("mg", m, 0), [(w[:, k, at:at + P], hT[:, k, :]) for k in range(KD)])
                fill(("mg", m, 1), [(w[:, k, 256 + at:256 + at + P], hT[:, k, :]) for k in range(KD)])
                fill(("mg", m, 2), [(wa[:, k, m * P:(m + 1) * P], yaT[:, k, :]) for k in range(4)])
                fill(("mg", m, 3), [(wb[:, k, m * P:(m + 1) * P], ybT[:, k, :]) for k in range(4)])
            for j in range(2):
                loaded2(pe, ("w_o", j))
            pe.wait_ge(mg_ready, KD)
            for m in range(KD):
                fill(("w_o", m), [(slot2(("w_o", k // 4), 4, D)[:, k % 4, m * P:(m + 1) * P], mix2(k)) for k in range(KD)])
            mean_square(3)
            for m in range(KF):
                if m % 2 == 0:
                    loaded2(pe, ("fi", m // 2))
                pe.wait_ge(h_ready, 4 * KD)
                w = slot2(("fi", m // 2), KD, 512)
                at = (m % 2) * P
                for i in range(2):
                    fill(("gu", m, i), [(w[:, k, 256 * i + at:256 * i + at + P], hT[:, k, :]) for k in range(KD)])
            for m in range(KF):
                tile_evacuated(pe, ("gu", m, 1))
            for k in range(KF):
                if k % 4 == 0:
                    loaded2(pe, ("fo", k // 4))
                w = slot2(("fo", k // 4), min(4, KF - 4 * (k // 4)), D)
                for m in range(KD):
                    ins = mm(bank[m][:, :], w[:, k % 4, m * P:(m + 1) * P], actT(k), start=(k == 0), stop=(k == KF - 1))
                    if k == KF - 1:
                        ins.then_inc(fo_mm, 1)


def kernel(**inputs):
    import concourse.bacc as _bacc
    from concourse.bass_utils import run_bass_kernel_spmd as _run

    def cols(x):
        return np.asarray(x).reshape(-1, P).T

    def twice(x):
        return np.concatenate([x, x], 0)

    i = inputs
    v = dict(c=cols(i["c"]), norm1_g=cols(i["norm1_g"]), norm2_g=cols(i["norm2_g"]), ada_b=cols(i["ada_b"]),
             shift_mu=cols(i["shift_mu"]), decay_w0=cols(i["decay_w0"]), iclr_a0=cols(i["iclr_a0"]), k_k=cols(i["k_k"]),
             k_a=cols(i["k_a"]), r_k=cols(i["r_k"]), lnx_w=cols(i["lnx_w"]), lnx_b=cols(i["lnx_b"]),
             sb_out_g=cols(i["sb_out_g"]), q_norm_g=twice(i["q_norm_g"].T), k_norm_g=twice(i["k_norm_g"].T),
             norm1_g_2=cols(i["norm1_g_2"]), norm2_g_2=cols(i["norm2_g_2"]), conv_a_w_2=cols(i["conv_a_w_2"]),
             ffn_conv_w_2=cols(i["ffn_conv_w_2"]), ffn_conv_b_2=cols(i["ffn_conv_b_2"]),
             cmp_k_pe_2=twice(i["cmp_k_pe_2"][0].T), cmp_v_pe_2=twice(i["cmp_v_pe_2"][0].T))
    for name in ROW_COLS:
        v[name] = np.tile(np.asarray(i[name]).reshape(1, -1), (P, 1))
    vecs = np.ascontiguousarray(np.concatenate([v[n] for n in VEC_AT], 1))
    arrays = dict(vecs=vecs, consts=constants(),
                  xT=np.ascontiguousarray(i["x"][0].T.reshape(KD, P, T).transpose(1, 0, 2)))
    arrays["positions"] = np.ascontiguousarray(np.asarray(i["positions_2"]).reshape(NT, P).T)
    for name in ("decay_up", "iclr_up", "gate_up", "ada_w", "w_in", "w_out", "router_w", "exp_w1", "exp_b1", "exp_w2", "exp_b2",
                 "w_in_2", "w_a_out_2", "w_b_out_2", "w_o_2", "w_ffn_in_2", "w_ffn_out_2", "cmp_k_w1_2", "cmp_k_w2_2",
                 "cmp_v_w1_2", "cmp_v_w2_2"):
        arrays[name] = np.ascontiguousarray(i[name])
    nc = _bacc.Bacc("TRN2", target_bir_lowering=False, num_devices=1)
    a = {n: nc.dram_tensor(f"in_{n}", x.shape, mybir.dt.from_np(x.dtype), kind="ExternalInput").ap() for n, x in arrays.items()}
    out = nc.dram_tensor("out_0_dram", (D, T), F32, kind="ExternalOutput").ap()
    program(nc, a, out)
    r = _run(nc, [{f"in_{n}": x for n, x in arrays.items()}], core_ids=[0])
    return np.ascontiguousarray(r.results[0]["out_0_dram"].T)[None]
```

```python
from contextlib import ExitStack

import numpy as np

import concourse.bass as bass
from concourse import mybir

ALU = mybir.AluOpType
ACT = mybir.ActivationFunctionType
AX = mybir.AxisListType
F32 = mybir.dt.float32
I32 = mybir.dt.int32
U32 = mybir.dt.uint32
BF16 = mybir.dt.bfloat16

P = 128
T = 512
D = 1024
KD = D // P
NT = T // P
HD = 64
NH = 8
EXPERTS = 32
TOP_K = 4
FF = 1024
C_RWKV = 1792
NZ = C_RWKV // P
FF2 = 2816
KF = FF2 // P
N_CMP = 31
CMP_BLOCK, CMP_STRIDE = 32, 16
TURN = float(2 * np.pi)
TURN_PARTS = (6.28125, float(np.float32(0.0019350051879882812)), float(np.float32(2 * np.pi - 6.28125 - 0.0019350051879882812)))
ROUNDER = 1.5 * 2.0 ** 23
PI_LOW = 3.1415925
DECAY_K = float(np.exp(-0.5))
NORM_EPS = 1e-6
GN_EPS = 1e-5 * HD
L2_EPS = 1e-12
NEG = -1e30
MAX_CHUNK = 4096
SLOTS = 6

VEC_COLS = dict(c=KD, norm1_g=KD, norm2_g=KD, ada_b=48, shift_mu=NZ, decay_w0=4, iclr_a0=4, k_k=4, k_a=4, r_k=4,
                lnx_w=4, lnx_b=4, sb_out_g=4, q_norm_g=1, k_norm_g=1, norm1_g_2=KD, norm2_g_2=KD,
                conv_a_w_2=12, ffn_conv_w_2=3 * KF, ffn_conv_b_2=KF, cmp_k_pe_2=CMP_BLOCK, cmp_v_pe_2=CMP_BLOCK)
ROW_COLS = dict(router_b=EXPERTS, q_norm_g_2=HD, k_norm_g_2=3 * HD)
CONST_COLS = dict(ident=P, head_ones=P, ones=P, neg_tri=P, neg_ones=P, strict=P, incl=P, sb_mask=P, level=7 * P,
                  iota=P, causal=P, cmp_bias=4 * 32, cmp_mask=4 * 32, inv_freq=32, expert=EXPERTS, token=2 * NT, eps=4)


def offsets(cols):
    at, out = 0, {}
    for name, n in cols.items():
        out[name] = at
        at += n
    return out, at


VEC_AT, VEC_N = offsets({**VEC_COLS, **ROW_COLS})
CONST_AT, CONST_N = offsets(CONST_COLS)


def constants():
    c = np.zeros((P, CONST_N), np.float32)

    def put(name, value):
        c[:, CONST_AT[name]:CONST_AT[name] + CONST_COLS[name]] = value
    i = np.arange(P)
    row, col = i[:, None], i[None, :]
    put("ident", row == col)
    put("head_ones", row // HD == col // HD)
    put("ones", 1.0)
    put("neg_tri", -1.0 * (row >= col))
    put("neg_ones", -1.0)
    put("strict", row < col)
    put("incl", row <= col)
    put("sb_mask", np.where(row < col, 0.0, NEG))
    for k in range(7):
        s = 2 ** k
        c[:, CONST_AT["level"] + k * P:CONST_AT["level"] + (k + 1) * P] = ((row // s) % 2 == 1) & (col // s == row // s - 1)
    put("iota", col)
    put("causal", np.where(col <= row, 0.0, NEG))
    end = np.arange(32) * CMP_STRIDE + CMP_BLOCK - 1
    ok = np.stack([end[None, :] <= (row + P * q) for q in range(4)], 1)
    put("cmp_bias", np.where(ok, 0.0, NEG).reshape(P, -1))
    put("cmp_mask", ok.reshape(P, -1))
    put("inv_freq", (np.float32(10000.0) ** (-np.arange(32, dtype=np.float32) / np.float32(32)))[None, :])
    put("expert", np.arange(EXPERTS)[None, :])
    put("token", np.concatenate([np.concatenate([i[:, None], np.full((P, 1), t * P)], 1) for t in range(NT)], 1))
    put("eps", np.array([[NORM_EPS, GN_EPS, np.pi / 2, 1.0]]))
    return c


class Plan:

    def __init__(self, keys):
        self.at = {k: i for i, k in enumerate(keys)}
        assert len(self.at) == len(keys)

    def bank(self, key):
        return self.at[key] % 4

    def turn(self, key):
        return self.at[key] // 4


def chunk_plan():
    order = [("ada", n) for n in range(4)]
    ada = 4
    for n in range(7):
        order.append(("win", n))
        while ada < 12 and ada < 4 + 2 * (n + 1):
            order.append(("ada", ada))
            ada += 1
    return order


A_B, A_C, A_X, Q2, KC, KV2, G_NSA, G_MERGE = 0, 512, 1024, 1536, 2048, 2304, 2816, 2840


def second_chunks():
    out = [("q2", ("q2", 3)), ("kv2", ("kv2", 3)), ("kc", ("g2", 3)), ("ac", ("ac", 3)), ("ax", ("ax", 3)), ("ab", ("ab", 3)),
           ("wa", ("mg", KD - 1, 3)), ("wb", ("mg", KD - 1, 3))]
    out += [(("mg", j), ("mg", 2 * j + 1, 3)) for j in range(4)]
    out += [(("w_o", j), ("w_o", KD - 1)) for j in range(2)]
    out += [(("fi", j), ("gu", 2 * j + 1, 1)) for j in range(KF // 2)]
    out += [(("fo", j), None) for j in range(6)]
    return out


WIN_CUTS = [0, 512, 1024, 1536, 1792, 2304, 2816, 3328]
WIN_TILES = [range(0, 4), range(4, 8), range(8, 12), range(12, 14), range(14, 18), range(18, 22)]


WIN_LAST = [("z", t[-1]) for t in WIN_TILES] + [("v", NT - 1)]


def program(nc, a, out):
    chunks = chunk_plan()
    slot_of = {c: n % SLOTS for n, c in enumerate(chunks)}
    load_of = {c: n // SLOTS + 1 for n, c in enumerate(chunks)}
    keys = [("z", m) for m in range(22)] + [("v", t) for t in range(NT)]
    keys += [("wag", c, j) for c in range(4) for j in range(3)]
    keys += [("kk", c) for c in range(4)] + [("rk", c) for c in range(4)]
    keys += [("tok", ch, j) for ch in range(NT) for j in range(3)]
    for ch in range(NT):
        keys += [("am", ch, h) for h in range(NH)] + [("yT", ch - 1)] * (ch > 0) + [("sbn", 2 * ch), ("sbn", 2 * ch + 1)]
    keys += [("yT", NT - 1)]
    keys += [("oT", t) for t in range(NT)]
    keys += [("wo", m) for m in range(KD)]
    keys += [("ht", t, i) for t in range(NT) for i in range(2)] + [("lg", t) for t in range(NT)]
    keys += [("pos", t) for t in range(NT)] + [("cnt",), ("gateT",)]
    keys += [("q2", t) for t in range(NT)] + [("kv2", t) for t in range(NT)] + [("kc",), ("vc",)] + [("g2", t) for t in range(NT)]
    keys += [(n, c) for n in ("ac", "ax", "ab") for c in range(4)]
    keys += [("hid", j, g) for j in range(2) for g in range(2)] + [("kvc",), ("kcT",)]
    keys += [("qkT", t) for t in range(NT)] + [("kkT", t) for t in range(NT)]
    for t in range(NT):
        keys += [("cs", t, g) for g in range(2)] + [("cT", t, i) for i in range(2)]
    keys += [("ybT", t) for t in range(NT)]
    keys += [("mg", m, i) for m in range(KD) for i in range(4)]
    keys += [("w_o", m) for m in range(KD)]
    keys += [("gu", m, i) for m in range(KF) for i in range(2)]
    plan = Plan(keys)

    with ExitStack() as ctx:
        def sb(name, shape, dt=F32):
            return ctx.enter_context(nc.sbuf_tensor(name, shape, dt))

        def sem(name):
            return ctx.enter_context(nc.semaphore(name))

        ring = sb("ring", [P, SLOTS * MAX_CHUNK])
        xT = sb("xT", [P, KD, T])
        hT = sb("hT", [P, KD, T])
        cst = sb("cst", [P, CONST_N])
        vec = sb("vec", [P, VEC_N])
        arena = sb("arena", [P, 32 * T])
        cos_sin = sb("cos_sin", [P, 2, NT, 32])
        attn = sb("attn", [P, 320])
        mod = sb("mod", [P, 48])
        gain = sb("gain", [P, KD])
        small = sb("small", [P, 132])
        bank = [ctx.enter_context(nc.psum_tensor(f"bank{i}", [P, T], F32)) for i in range(8)]

        def const(name, n=None):
            at = CONST_AT[name]
            return cst[:, at:at + (n or CONST_COLS[name])]

        def col(name, j=0):
            return vec[:, VEC_AT[name] + j:VEC_AT[name] + j + 1]

        def A(i, n=1):
            return arena[:, i * T:(i + n) * T]

        def R(i, n=1):
            return ring[:, i * T:(i + n) * T]

        ident = const("ident")
        ones = const("ones")
        head_ones = const("head_ones")
        eps = lambda j: cst[:, CONST_AT["eps"] + j:CONST_AT["eps"] + j + 1]

        cst_in, vec_in, x_in, up_in = (sem(n) for n in ("cst_in", "vec_in", "x_in", "up_in"))
        slot_in = [sem(f"slot_in{s}") for s in range(SLOTS)]
        wo_in, rw_in = sem("wo_in"), sem("rw_in")
        ada_used = sem("ada_used")
        evac = [sem(f"evac{i}") for i in range(4)]
        filled = sem("filled")
        sq_ready, ss_done, rs_ready, h_ready = (sem(n) for n in ("sq_ready", "ss_done", "rs_ready", "h_ready"))
        sig_c, cond_ready, mod_mm, z_scaled = (sem(n) for n in ("sig_c", "cond_ready", "mod_mm", "z_scaled"))
        gates_lo, kk0_ready, kk2_ready, rk_ready, mid_ready, exp_ready = (sem(n) for n in (
            "gates_lo", "kk0_ready", "kk2_ready", "rk_ready", "mid_ready", "exp_ready"))
        prep_done = sem("prep_done")
        t1_mm, t1_sb, xn_mm, x_sb, xt_mm, xt_sb = (sem(n) for n in ("t1_mm", "t1_sb", "xn_mm", "x_sb", "xt_mm", "xt_sb"))
        w_mm, w_sb, u_mm, u_sb, y_mm, s_mm, s_sb = (sem(n) for n in (
            "w_mm", "w_sb", "u_mm", "u_sb", "y_mm", "s_mm", "s_sb"))
        var_ready, std_ready, yn_ready = sem("var_ready"), sem("std_ready"), sem("yn_ready")
        mix_ready = sem("mix_ready")
        qk2_ready, qkn_ready = sem("qk2_ready"), sem("qkn_ready")
        l_mm, ln_ready, sp_ready, r_mm, r_masked, wt_ready, o_mm, o_sb = (sem(n) for n in (
            "l_mm", "ln_ready", "sp_ready", "r_mm", "r_masked", "wt_ready", "o_mm", "o_sb"))
        on_ready = sem("on_ready")
        dve_chain, act_chain = sem("dve_chain"), sem("act_chain")
        top_ready, eg_ready, route_ready, npass_ready = (sem(n) for n in (
            "top_ready", "eg_ready", "route_ready", "npass_ready"))
        w1_in = [sem(f"w1_in{k}") for k in range(KD)]
        w2_in = [sem(f"w2_in{k}") for k in range(KD)]
        h2_out, rows_in, y_out, b2_in, idx_used, y_free = (sem(n) for n in ("h2_out", "rows_in", "y_out", "b2_in", "idx_used", "y_free"))
        b1_in, w1_free, w2_free = (sem(n) for n in ("b1_in", "w1_free", "w2_free"))
        oh_ready, idx_mm, idx_f, idx_sb, gx_mm, gx_sb, glu_ready, lin_ready, sig_ready, act_ready = (sem(n) for n in (
            "oh_ready", "idx_mm", "idx_f", "idx_sb", "gx_mm", "gx_sb", "glu_ready", "lin_ready", "sig_ready", "act_ready"))
        aT_mm, aT_sb, ye_sb = (sem(n) for n in ("aT_mm", "aT_sb", "ye_sb"))
        rows_ready, mix_mm, sum_ready, sum_chain, choice_chain, passed = (sem(n) for n in (
            "rows_ready", "mix_mm", "sum_ready", "sum_chain", "choice_chain", "passed"))
        yr_in = [sem(f"yr_in{t}") for t in range(NT)]
        moe_chain, pool_turn = sem("moe_chain"), sem("pool_turn")
        s2_in = [sem(f"s2_in{s}") for s in range(SLOTS)]
        cw_in, pos_in = sem("cw_in"), sem("pos_in")
        angles, trig_ready = sem("angles"), sem("trig_ready")
        x2_ready = sem("x2_ready")
        qn_sq, qn_rt, q_ready, k_ready, kc_sq, kc_rt, kc_ready = (sem(n) for n in (
            "qn_sq", "qn_rt", "q_ready", "k_ready", "kc_sq", "kc_rt", "kc_ready"))
        cs_ready, cp_exp, cp_ready, co_mm, co_sb = (sem(n) for n in ("cs_ready", "cp_exp", "cp_ready", "co_mm", "co_sb"))
        s2_mm, mx_ready, p_ready, pt_mm, pt_sb, o2_mm, yb_ready = (sem(n) for n in (
            "s2_mm", "mx_ready", "p_ready", "pt_mm", "pt_sb", "o2_mm", "yb_ready"))
        mg_ready, conv_ready, silu_ready, fo_mm, fo_sb, out_sent = (sem(n) for n in (
            "mg_ready", "conv_ready", "silu_ready", "fo_mm", "fo_sb", "out_sent"))

        zs = lambda m, n=1: A(m, n)
        q_sb, k_sb = A(14, 4).rearrange("p (c t) -> p c t", c=4), A(18, 4).rearrange("p (c t) -> p c t", c=4)
        v_sb = A(22, 4).rearrange("p (t n) -> p t n", t=4)
        up_wa, up_g = A(26), A(27)
        acc = [A(28), A(29)]
        rstd = A(30)
        KR = R(16, 8).rearrange("p (c j t) -> p c j t", c=4, j=2)
        ktT = R(24, 4).rearrange("p (c t) -> p c t", c=4)
        btT = R(28, 4).rearrange("p (c t) -> p c t", c=4)
        bonus = R(32, 4).rearrange("p (c t) -> p c t", c=4)
        gT = R(36, 4).rearrange("p (c t) -> p c t", c=4)
        aT = R(40, 4).rearrange("p (c t) -> p c t", c=4)
        kkT = R(44, 4).rearrange("p (c t) -> p c t", c=4)
        sigw = ktT
        nrm = btT
        S1 = ring[:, 0:4 * 4 * 129].rearrange("p (c k t) -> p c k t", c=4, k=4)
        hflat = hT[:, :, :].rearrange("p k t -> p (k t)")
        E1 = hflat[:, 0:4 * 4 * 129].rearrange("p (c k t) -> p c k t", c=4, k=4)
        E2 = R(5, 4).rearrange("p (c k t) -> p c k t", c=4, k=4)
        kt_tok = R(40, 4).rearrange("p (k n) -> p k n", k=4)
        bt_tok = R(44, 4).rearrange("p (k n) -> p k n", k=4)
        v_tok = A(4, 4).rearrange("p (k n) -> p k n", k=4)
        AM = R(0, 8).rearrange("p (h n) -> p h n", h=NH)
        X = R(10, 2).rearrange("p (h n) -> p h n", h=NH)
        XT = R(12, 2).rearrange("p (h n) -> p h n", h=NH)
        T1 = hflat[:, 5 * T:7 * T].rearrange("p (h n) -> p h n", h=NH)
        W_sb = hflat[:, 7 * T:8 * T]
        U_sb = R(9)
        S_sc = up_wa
        qk_sq = lambda i: hflat[:, (1 + i % 4) * T:(2 + i % 4) * T]
        yn, ysq = up_g, hflat[:, 0:T]
        mixT = lambda k: A(k) if k < 4 else A(10 + k)
        mids = small[:, 0:16].rearrange("p (c k) -> p c k", c=4)
        nmids = small[:, 16:32].rearrange("p (c k) -> p c k", c=4)
        emid = small[:, 32:48].rearrange("p (c k) -> p c k", c=4)
        dec = small[:, 48:64].rearrange("p (c k) -> p c k", c=4)
        omka = small[:, 64:68]
        omu = small[:, 68:68 + NZ]
        cond = small[:, 84:92]
        sigc = small[:, 92:100]
        hsum = small[:, 100:108]
        hvar = small[:, 108:116]
        hstd = small[:, 116:124]
        hrstd = small[:, 124:132]

        h2_tok = A(0, 8).rearrange("p (t n) -> p t n", t=NT)
        h2_d = nc.dram_tensor("h2_rows", (T, D), F32).ap()
        y_d = nc.dram_tensor("expert_rows", (EXPERTS * P, D), F32).ap()
        XR = A(0, 2)
        h2_tok = A(0, 8).rearrange("p (t n) -> p t n", t=NT)
        XG = A(2, 2).rearrange("p (k s) -> p k s", k=KD)
        G = A(4, 2)
        SG = A(6, 2)
        LIN = A(8, 2)
        aT2 = A(10, 2)
        aT2k = aT2.rearrange("p (k s) -> p k s", k=KD)
        Y = A(12, 2)
        OH = A(22).bitcast(BF16)[:, 0:T].rearrange("p (t s) -> p t s", t=NT)
        token = small[:, 4:4 + NT].bitcast(BF16).rearrange("p (t i) -> p t i", t=NT)
        picks = A(27).rearrange("p (i e) -> p i e", e=EXPERTS)
        GATE_T = A(26)[0:EXPERTS, :]
        B1 = hflat[:, 0:4 * T]
        B2 = hflat[0:EXPERTS, 4 * T:6 * T]
        YR = [A(i, 2) for i in (14, 16, 18, 20, 0, 2, 4, 6, 8, 10, 12, 22, 24, 30, 14, 16)]
        router_w = A(31)[:, 0:KD * EXPERTS].rearrange("p (k n) -> p k n", k=KD)
        route = A(28, 2)
        LG = route[:, 0:128].rearrange("p (t e) -> p t e", t=NT)
        SEL = route[:, 128:256].rearrange("p (t e) -> p t e", t=NT)
        GATE = route[:, 256:384].rearrange("p (t e) -> p t e", t=NT)
        GTMP = route[:, 384:416]
        POS = route[:, 416:416 + 4 * 34].rearrange("p (t e) -> p t e", t=NT)
        TOPV = route[:, 552:584].rearrange("p (t e) -> p t e", t=NT)
        TOPF = route[:, 584:616].rearrange("p (t e) -> p t e", t=NT)
        TOPG = route[:, 616:632].rearrange("p (t e) -> p t e", t=NT)
        GSUM = route[:, 632:636]
        NPF = route[:, 636:640]
        LOOKS = EXPERTS + 2
        TURNS = EXPERTS + 1
        top_idx = sb("top_idx", [P, NT, 8], U32)
        n_pass = sb("n_pass", [P, 1], I32)
        slot_token = small[:, 2:3].bitcast(U32)
        slot_f = small[:, 0:1]
        choice_at = small[:, 48:64]
        choice_in = small[:, 64:80]
        choice_gate = small[:, 80:96]
        choice_row = small[:, 16:32].bitcast(U32)
        w1_slot = lambda k: ring[:, k * 2 * FF:(k + 1) * 2 * FF]
        w2_slot = lambda k: ring[:, KD * 2 * FF + k * D:KD * 2 * FF + (k + 1) * D]

        q_tok = A(0, 4).rearrange("p (t n) -> p t n", t=NT)
        kv_tok = A(4, 4).rearrange("p (t n) -> p t n", t=NT)
        kcT, vcT = A(8), A(9)
        QT = A(10, 4).rearrange("p (c t) -> p c t", c=4)
        KselT, KwinT = A(14), A(15)
        yaT = A(16, 4).rearrange("p (c t) -> p c t", c=4)
        cmp_w1 = [A(20 + 4 * j, 4).rearrange("p (i n) -> p i n", i=CMP_BLOCK) for j in range(2)]
        scr = A(28)
        scr2 = A(29)
        Pb = [A(30), A(31)]
        PTb = [A(28), A(29)]
        ybT = A(20, 4).rearrange("p (c t) -> p c t", c=4)
        yb_tok = A(0, 4).rearrange("p (t n) -> p t n", t=NT)
        yb_tmp = A(24)
        crow = A(28)
        cPT = A(30, 2).rearrange("p (h q) -> p h q", h=NH)
        u_pos = sb("u_pos", [P, NT], I32)
        mix2 = lambda m: A(m)
        actT = lambda m: A(m)
        nsa_gate = attn[:, 0:96].rearrange("p (t g) -> p t g", t=NT)
        nmax = attn[:, 96:160]
        psum_ = attn[:, 160:224]
        csum = attn[:, 224:232]
        cmx = attn[:, 232:240]
        gs = attn[:, 240:248]
        hbias = attn[:, 248:250]
        cstat = attn[:, 250:254]
        hid = [A(8 + j)[0:HD, 0:64].rearrange("p (g n) -> p g n", g=2) for j in range(2)]
        kcn = A(8)[0:N_CMP, 128:256]
        v_cmp = A(9)[0:N_CMP, 256:384]
        KcT = A(8)[:, 384:384 + N_CMP]
        stats = nmax[:, 0:48].rearrange("p (t h) -> p t h", t=NT)
        cmp_w2 = sb("cmp_w2", [P, 2 * HD])
        trig = A(31)

        def s_bank(u):
            return bank[(2, 3, 6, 7)[u % 4]]

        chunks2 = second_chunks()
        place2, total = {}, [0] * SLOTS
        last_in = {}
        before = {}
        for n, (name, reader) in enumerate(chunks2):
            s = n % SLOTS if n < 12 else (n + 2) % SLOTS
            before[name] = last_in.get(s)
            last_in[s] = reader
            total[s] += 16 * (2 if name == "kc" or name[0] in ("mg", "fi") else 1)
            place2[name] = (s, total[s])

        def slot2(name, k, width):
            at = place2[name][0] * MAX_CHUNK
            return ring[:, at:at + k * width].rearrange("p (k n) -> p k n", k=k)

        def loaded2(eng, name):
            eng.wait_ge(s2_in[place2[name][0]], place2[name][1])

        def sb_logits(h, kt):
            b = 3 * (h % 2)
            x, lo = ((2 + b, 0), (3 + b, 0), (4 + b, 0), (3 + b, 384))[kt]
            return bank[x][:, lo:lo + T - P * kt]

        def sb_out(h):
            return bank[h % 2][:, 0:256]

        def sb_e(h, kt):
            at = 16 * T + (h % 2) * 1280 + (0, 512, 896, 1152)[kt]
            return ring[:, at:at + T - P * kt]

        def sb_w(h, kt):
            at = 24 * T + (h % 2) * 1280 + (0, 512, 896, 1152)[kt]
            return ring[:, at:at + T - P * kt]
        o_tok = R(32, 4).rearrange("p (t n) -> p t n", t=4)

        block = ctx.enter_context(nc.Block())

        def tile_evacuated(eng, key):
            eng.wait_ge(evac[plan.bank(key)], plan.turn(key) + 1)

        @block.sync
        def _(sp):
            sp.dma_start(cst[:, :], a["consts"]).then_inc(cst_in, 16)
            sp.dma_start(vec[:, :], a["vecs"]).then_inc(vec_in, 16)
            sp.dma_start(xT[:, :, :], a["xT"]).then_inc(x_in, 16)
            sp.dma_start(up_wa[0:64, :], a["decay_up"][0]).then_inc(up_in, 16)
            sp.dma_start(up_wa[64:128, :], a["iclr_up"][0]).then_inc(up_in, 16)
            sp.dma_start(up_g, a["gate_up"][0]).then_inc(up_in, 16)
            sp.dma_start(u_pos[:, :], a["positions"]).then_inc(pos_in, 16)
            ada_w = a["ada_w"][0].rearrange("(k p) n -> p k n", p=P)
            w_in = a["w_in"][0].rearrange("(k p) n -> p k n", p=P)
            for n, (kind, i) in enumerate(chunks):
                if n >= SLOTS:
                    last_kind, last = chunks[n - SLOTS]
                    if last_kind == "ada":
                        sp.wait_ge(ada_used, last + 1)
                    else:
                        sp.wait_ge(filled, plan.at[WIN_LAST[last]] + 1)
                s = n % SLOTS
                lo, hi = (512 * i, 512 * i + 512) if kind == "ada" else (WIN_CUTS[i], WIN_CUTS[i + 1])
                src = (ada_w if kind == "ada" else w_in)[:, :, lo:hi]
                dst = ring[:, s * MAX_CHUNK:s * MAX_CHUNK + KD * (hi - lo)].rearrange("p (k n) -> p k n", k=KD)
                sp.dma_start(dst, src).then_inc(slot_in[s], 16)
            sp.wait_ge(ada_used, 12)
            sp.wait_ge(filled, plan.at["yT", NT - 1] + 1)
            w_out = a["w_out"][0].rearrange("(k p) n -> p k n", p=P)
            sp.dma_start(ring[:, 0:KD * D].rearrange("p (k n) -> p k n", k=KD), w_out).then_inc(wo_in, 16)
            sp.wait_ge(trig_ready, 1)
            sp.dma_start(router_w, a["router_w"][0].rearrange("(k p) e -> p k e", p=P)).then_inc(rw_in, 16)
            w1_d = a["exp_w1"][0].rearrange("e (k p) n -> e k p n", p=P)
            w2_d = a["exp_w2"][0].rearrange("e (k p) n -> e k p n", p=P)
            sp.wait_ge(filled, plan.at["wo", KD - 1] + 1)
            sp.sem_inc(w1_free, KD)
            sp.sem_inc(w2_free, KD)
            sp.wait_ge(lin_ready, 1)
            sp.dma_start(B2, a["exp_b2"][0]).then_inc(b2_in, 16)
            sp.wait_ge(npass_ready, 1)
            passes = sp.value_load(n_pass[0:1, 0:1], min_val=1, max_val=4)
            def load_w1(it, e):
                for k in range(KD):
                    sp.wait_ge(w1_free, it * KD + (k + 1))
                    sp.dma_start(w1_slot(k), w1_d[bass.ds(e, 1), k].rearrange("o p n -> p (o n)")).then_inc(w1_in[k], 16)
                sp.wait_ge(lin_ready, it + 1)
                sp.dma_start(B1, a["exp_b1"][0][bass.ds(e, 1), :].to_broadcast([P, 2 * FF])).then_inc(b1_in, 16)

            def load_w2(it, e):
                for k in range(KD):
                    sp.wait_ge(w2_free, it * KD + (k + 1))
                    sp.dma_start(w2_slot(k), w2_d[bass.ds(e, 1), k].rearrange("o p n -> p (o n)")).then_inc(w2_in[k], 16)
            sp.wait_ge(rows_in, 16)
            with sp.Fori(0, passes) as j:
                load_w1(j * EXPERTS, 0)
                with sp.Fori(0, EXPERTS - 1) as e:
                    it = j * EXPERTS + e
                    load_w1(it + 1, e + 1)
                    load_w2(it, e)
                load_w2(j * EXPERTS + (EXPERTS - 1), EXPERTS - 1)
            w_in2 = a["w_in_2"][0].rearrange("(k p) n -> p k n", p=P)
            w_fi = a["w_ffn_in_2"][0].rearrange("(k p) n -> p k n", p=P)
            w_fo = a["w_ffn_out_2"][0].rearrange("(k p) n -> p k n", p=P)
            w_a = a["w_a_out_2"][0].rearrange("(k p) n -> p k n", p=P)
            w_b = a["w_b_out_2"][0].rearrange("(k p) n -> p k n", p=P)
            w_o = a["w_o_2"][0].rearrange("(k p) n -> p k n", p=P)
            sp.wait_ge(yr_in[NT - 1], passes * (16 * TOP_K))
            for name, _ in chunks2:
                if before[name]:
                    sp.wait_ge(filled, plan.at[before[name]] + 1)
                got = s2_in[place2[name][0]]
                if name == "q2":
                    sp.dma_start(slot2(name, KD, 512), w_in2[:, :, Q2:Q2 + 512]).then_inc(got, 16)
                elif name == "kv2":
                    sp.dma_start(slot2(name, KD, 512), w_in2[:, :, KV2:KV2 + 512]).then_inc(got, 16)
                elif name == "kc":
                    sp.dma_start(slot2(name, KD, 280)[:, :, 0:256], w_in2[:, :, KC:KC + 256]).then_inc(got, 16)
                    sp.dma_start(slot2(name, KD, 280)[:, :, 256:280], w_in2[:, :, G_NSA:G_NSA + 24]).then_inc(got, 16)
                elif name in ("ac", "ax", "ab"):
                    at = {"ac": A_C, "ax": A_X, "ab": A_B}[name]
                    sp.dma_start(slot2(name, KD, 512), w_in2[:, :, at:at + 512]).then_inc(got, 16)
                elif name in ("wa", "wb"):
                    sp.dma_start(slot2(name, 4, D), w_a if name == "wa" else w_b).then_inc(got, 16)
                elif name[0] == "mg":
                    for i in range(2):
                        at = G_MERGE + i * D + name[1] * 256
                        sp.dma_start(slot2(name, KD, 512)[:, :, i * 256:(i + 1) * 256], w_in2[:, :, at:at + 256]).then_inc(got, 16)
                elif name[0] == "w_o":
                    sp.dma_start(slot2(name, 4, D), w_o[:, 4 * name[1]:4 * name[1] + 4, :]).then_inc(got, 16)
                elif name[0] == "fi":
                    for i in range(2):
                        at = i * FF2 + name[1] * 256
                        sp.dma_start(slot2(name, KD, 512)[:, :, i * 256:(i + 1) * 256], w_fi[:, :, at:at + 256]).then_inc(got, 16)
                else:
                    lo, hi = 4 * name[1], min(4 * name[1] + 4, KF)
                    sp.dma_start(slot2(name, hi - lo, D), w_fo[:, lo:hi, :]).then_inc(got, 16)
            o = out.rearrange("(k p) t -> p k t", p=P)
            for m in range(KD):
                sp.wait_ge(fo_sb, m + 1)
                sp.dma_start(o[:, m, :], xT[:, m, :]).then_inc(out_sent, 16)
            sp.wait_ge(out_sent, 16 * KD)

        @block.gpsimd
        def _(pool):
            pool.sem_inc(idx_used, 1)
            pool.sem_inc(y_free, 1)
            pool.wait_ge(h2_out, 16)
            pool.wait_ge(npass_ready, 1)
            passes = pool.value_load(n_pass[0:1, 0:1], min_val=1, max_val=4)

            def gather(j, n):
                pool.wait_ge(idx_sb, j * LOOKS + (n + 1))
                pool.wait_ge(gx_mm, j * TURNS + (n + 1))
                pool.sem_inc(pool_turn, 1)
                pool.indirect_dma_start(XR, None, h2_d, bass.IndirectOffsetOnAxis(ap=slot_token[:, 0:1], axis=0)).then_inc(rows_in, 16)
                pool.wait_ge(rows_in, j * (16 * LOOKS) + n * 16 + 16)
                pool.sem_inc(idx_used, 1)

            def store(j, e):
                pool.wait_ge(ye_sb, j * EXPERTS + (e + 2))
                pool.sem_inc(pool_turn, 1)
                pool.dma_start(y_rows[bass.ds(e, 1)].rearrange("a s n -> s (a n)"), Y).then_inc(y_out, 16)
                pool.wait_ge(y_out, j * (16 * EXPERTS) + e * 16 + 16)
                pool.sem_inc(y_free, 1)
            y_rows = y_d.rearrange("(e s) n -> e s n", s=P)
            with pool.Fori(0, passes) as j:
                for n in range(3):
                    gather(j, n)
                with pool.Fori(0, EXPERTS - 1) as e:
                    gather(j, e + 3)
                    store(j, e)
                store(j, EXPERTS - 1)
                pool.wait_ge(rows_ready, j + 1)
                pool.sem_inc(pool_turn, 1)
                for i in range(NT * TOP_K):
                    if i == 14:
                        pool.wait_ge(sum_ready, j * NT + 1)
                        pool.wait_ge(mix_mm, j * (NT - 1 + KD) + 1)
                        pool.sem_inc(pool_turn, 1)
                    pool.indirect_dma_start(YR[i], None, y_d, bass.IndirectOffsetOnAxis(ap=choice_row[:, i:i + 1], axis=0))\
                        .then_inc(yr_in[i // TOP_K], 16)
                pool.wait_ge(passed, j + 1)
            pool.wait_ge(x2_ready, 1)
            for j, name in enumerate(("cmp_k_w1_2", "cmp_v_w1_2")):
                src = a[name][0].rearrange("(i d) n -> d i n", d=HD)
                for g in range(2):
                    pool.dma_start(cmp_w1[j][g * HD:(g + 1) * HD, :, :], src).then_inc(cw_in, 16)
            for j, name in enumerate(("cmp_k_w2_2", "cmp_v_w2_2")):
                pool.dma_start(cmp_w2[0:HD, j * HD:(j + 1) * HD], a[name][0]).then_inc(cw_in, 16)

        @block.scalar
        def _(act):
            chained = [0]

            def link(ins):
                chained[0] += 1
                ins.then_inc(act_chain, 1)
                act.wait_ge(act_chain, chained[0])

            def take(key, *args, **kw):
                act.wait_ge(filled, plan.at[key] + 1)
                act.activation(args[0], bank[plan.bank(key)][:, :] if len(args) < 3 else args[2], args[1], **kw)\
                   .then_inc(evac[plan.bank(key)], 1)

            def squares(stage):
                for k in range(KD):
                    act.activation(hT[:, k, :], xT[:, k, :], ACT.Square).then_inc(sq_ready, 1)

            def root(stage):
                act.wait_ge(ss_done, stage + 1)
                act.activation(rstd, bank[4][:, :], ACT.Sqrt, scale=1.0 / D, bias=eps(0)).then_inc(rs_ready, 1)

            act.wait_ge(vec_in, 16)
            act.activation(sigc, vec[:, VEC_AT["c"]:VEC_AT["c"] + KD], ACT.Sigmoid).then_inc(sig_c, 1)
            act.wait_ge(x_in, 16)
            act.wait_ge(cst_in, 16)
            act.wait_ge(angles, 1)
            act.activation(cos_sin[:, :, :, :].rearrange("p j t f -> p (j t f)"), trig[:, 0:256], ACT.Sin).then_inc(trig_ready, 1)
            squares(0)
            root(0)

            act.wait_ge(cond_ready, 1)
            for m in range(NZ):
                act.wait_ge(filled, plan.at["z", m] + 1)
                act.activation(zs(m), bank[plan.bank(("z", m))][:, :], ACT.Copy, scale=omu[:, m:m + 1]).then_inc(z_scaled, 1)
            for m in range(NZ, 22):
                take(("z", m), zs(m), ACT.Copy)
            for t in range(NT):
                take(("v", t), v_sb[:, t, :], ACT.Copy)

            tile_evacuated(act, ("z", 12))
            act.activation(zs(12)[0:64], zs(12)[0:64], ACT.Tanh).then_inc(gates_lo, 1)
            tile_evacuated(act, ("z", 13))
            act.activation(zs(13), zs(13), ACT.Sigmoid).then_inc(gates_lo, 1)
            act.wait_ge(ada_used, 12)
            for c in range(4):
                take(("wag", c, 0), sigw[:, c, :], ACT.Sigmoid, bias=col("decay_w0", c))
                take(("wag", c, 1), aT[:, c, :], ACT.Sigmoid, bias=col("iclr_a0", c))
                take(("wag", c, 2), gT[:, c, :], ACT.Copy)
            for c in range(4):
                act.wait_ge(kk0_ready, c + 1)
                act.activation(nrm[:, c, :], kkT[:, c, :], ACT.Square).then_inc(kk2_ready, 1)
            for c in range(4):
                take(("kk", c), nrm[:, c, :], ACT.Sqrt)
            act.wait_ge(mid_ready, 1)
            for c in range(4):
                for k in range(NT):
                    act.activation(E1[:, c, k, :], S1[:, c, k, :], ACT.Exp, scale=-DECAY_K, bias=mids[:, c, k:k + 1])
                    act.activation(E2[:, c, k, :], S1[:, c, k, 1:129], ACT.Exp, scale=DECAY_K, bias=nmids[:, c, k:k + 1]).then_inc(exp_ready, 1)
            act.activation(small[:, 32:48], small[:, 0:16], ACT.Exp, scale=-1.0).then_inc(exp_ready, 1)
            act.wait_ge(prep_done, 4)
            for k in range(NT):
                for j, dst in enumerate((v_tok, kt_tok, bt_tok)):
                    take(("tok", k, j), dst[:, k, :], ACT.Copy)

            def qk_squares(k):
                for i in (2 * k, 2 * k + 1):
                    if i >= 4:
                        act.wait_ge(qkn_ready, i - 3)
                    act.activation(qk_sq(i), A(14 + i), ACT.Square).then_inc(qk2_ready, 1)
            act.wait_ge(s_sb, 1)
            qk_squares(0)
            for k in range(NT):
                for i in (2 * k, 2 * k + 1):
                    take(("sbn", i), qk_sq(i), ACT.Sqrt, scale=1.0 / HD, bias=eps(0))
                act.wait_ge(w_mm, k + 1)
                act.activation(W_sb, bank[6][:, :], ACT.Copy).then_inc(w_sb, 1)
                act.wait_ge(u_mm, k + 1)
                if k:
                    act.wait_ge(s_mm, k)
                act.activation(U_sb, bank[7][:, :], ACT.Copy, scale=-1.0).then_inc(u_sb, 1)
                act.wait_ge(var_ready, k + 1)
                act.activation(hstd, hvar, ACT.Sqrt, scale=1.0 / HD, bias=eps(1)).then_inc(std_ready, 1)
                if k < NT - 1:
                    qk_squares(k + 1)
                act.wait_ge(filled, plan.at["yT", k] + 1)
                src = bank[plan.bank(("yT", k))]
                for c in range(4):
                    ins = act.activation(mixT(c)[:, k * P:(k + 1) * P], src[:, c * P:(c + 1) * P], ACT.Identity,
                                         scale=col("lnx_w", c), bias=col("lnx_b", c))
                ins.then_inc(evac[plan.bank(("yT", k))], 1)

            def softplus(h):
                act.wait_ge(l_mm, h + 1)
                if h >= 2:
                    act.wait_ge(r_mm, (h - 1) * NT)
                for kt in range(NT):
                    ins = act.activation(sb_e(h, kt), sb_logits(h, kt), ACT.Abs)
                link(ins)
                for kt in range(NT):
                    ins = act.activation(sb_e(h, kt), sb_e(h, kt), ACT.Exp, scale=-1.0)
                link(ins)
                for kt in range(NT):
                    act.activation(sb_e(h, kt), sb_e(h, kt), ACT.Ln, bias=1.0).then_inc(ln_ready, 1)
            softplus(0)
            for h in range(NH):
                if h + 1 < NH:
                    softplus(h + 1)
                act.wait_ge(r_masked, NT * (h + 1))
                if h >= 2:
                    act.wait_ge(o_mm, h - 1)
                for kt in range(NT):
                    act.activation(sb_w(h, kt), sb_logits(h, kt), ACT.Exp).then_inc(wt_ready, 1)
            for t in range(NT):
                act.wait_ge(var_ready, NT + t + 1)
                act.activation(hstd, hvar, ACT.Sqrt, scale=1.0 / HD, bias=eps(0)).then_inc(std_ready, 1)
            for t in range(NT):
                act.wait_ge(filled, plan.at["oT", t] + 1)
                src = bank[plan.bank(("oT", t))]
                for c in range(4):
                    ins = act.activation(mixT(4 + c)[:, t * P:(t + 1) * P], src[:, c * P:(c + 1) * P], ACT.Copy,
                                         scale=col("sb_out_g", c))
                ins.then_inc(evac[plan.bank(("oT", t))], 1)

            for k in range(KD):
                tile_evacuated(act, ("wo", k))
            squares(1)
            root(1)
            for t in range(NT):
                for i in range(2):
                    take(("ht", t, i), h2_tok[:, t, i * T:(i + 1) * T], ACT.Copy)
            for t in range(NT):
                for i in range(2):
                    tile_evacuated(act, ("ht", t, i))
            act.dma_start(h2_d.rearrange("(t p) n -> p t n", p=P), h2_tok).then_inc(h2_out, 16)
            act.wait_ge(top_ready, 1)
            act.activation(TOPG, TOPG, ACT.Exp).then_inc(eg_ready, 1)
            b = plan.bank(("gateT",))
            act.wait_ge(filled, plan.at["gateT",] + 1)
            act.activation(GATE_T, bank[b][0:EXPERTS, :], ACT.Copy).then_inc(evac[b], 1)
            act.sem_inc(aT_sb, 1)
            act.wait_ge(npass_ready, 1)
            passes = act.value_load(n_pass[0:1, 0:1], min_val=1, max_val=4)

            def take_turned(j, n):
                act.wait_ge(gx_mm, j * TURNS + (n + 2))
                for i in range(2):
                    ins = act.activation(XG[:, 4 * i:4 * i + 4, :].rearrange("p k s -> p (k s)"), bank[4 + i][:, :], ACT.Copy)
                ins.then_inc(gx_sb, 1)

            def expert(j, e):
                it = j * EXPERTS + e
                act.wait_ge(glu_ready, it + 1)
                act.activation(SG, G, ACT.Sigmoid, scale=1.702).then_inc(sig_ready, 1)
                take_turned(j, e + 1)
                act.wait_ge(aT_mm, it + 2)
                for i in range(2):
                    ins = act.activation(aT2[:, i * T:(i + 1) * T], bank[4 + i][:, :], ACT.Copy)
                ins.then_inc(aT_sb, 1)
            with act.Fori(0, passes) as j:
                take_turned(j, 0)
                expert(j, 0)
                with act.Fori(0, EXPERTS - 1) as e:
                    expert(j, e + 1)

            act.wait_ge(x2_ready, 1)
            squares(2)
            root(2)
            for t in range(NT):
                take(("q2", t), q_tok[:, t, :], ACT.Copy)
            for t in range(NT):
                take(("kv2", t), kv_tok[:, t, :], ACT.Copy)
            take(("kc",), kcT, ACT.Copy)
            take(("vc",), vcT, ACT.Copy)
            for t in range(NT):
                act.wait_ge(filled, plan.at["g2", t] + 1)
                b = plan.bank(("g2", t))
                act.activation(nsa_gate[:, t, :], bank[b][:, 0:24], ACT.Sigmoid).then_inc(evac[b], 1)
            act.wait_ge(qn_sq, 1)
            act.activation(nmax[:, 0:48], nmax[:, 0:48], ACT.Sqrt, scale=1.0 / HD, bias=eps(0)).then_inc(qn_rt, 1)
            for c in range(4):
                take(("ac", c), yaT[:, c, :], ACT.Copy)
            for j in range(2):
                for g in range(2):
                    b = plan.bank(("hid", j, g))
                    act.wait_ge(filled, plan.at["hid", j, 1] + 1)
                    if g == 0:
                        link(act.activation(hbias[0:HD, j:j + 1], bank[b][0:HD, 64:65], ACT.Copy))
                    act.activation(hid[j][:, g, 0:N_CMP], bank[b][0:HD, 0:N_CMP], ACT.Silu, bias=hbias[0:HD, j:j + 1]).then_inc(evac[b], 1)
            act.wait_ge(kc_sq, 1)
            act.activation(cstat[0:N_CMP, 0:2], cstat[0:N_CMP, 0:2], ACT.Sqrt, scale=1.0 / HD, bias=eps(0)[0:N_CMP]).then_inc(kc_rt, 1)
            b = plan.bank(("kcT",))
            act.wait_ge(filled, plan.at["kcT",] + 1)
            act.activation(KcT, bank[b][:, 0:N_CMP], ACT.Copy).then_inc(evac[b], 1)
            for t in range(NT):
                b = plan.bank(("qkT", t))
                act.wait_ge(filled, plan.at["qkT", t] + 1)
                act.activation(QT[:, :, t * P:(t + 1) * P], bank[b][:, :].rearrange("p (c q) -> p c q", c=4), ACT.Copy).then_inc(evac[b], 1)
            for t in range(NT):
                b = plan.bank(("kkT", t))
                act.wait_ge(filled, plan.at["kkT", t] + 1)
                act.activation(A(14, 2).rearrange("p (b n) -> p b n", b=2)[:, :, t * P:(t + 1) * P],
                               bank[b][:, 0:256].rearrange("p (b n) -> p b n", b=2), ACT.Copy).then_inc(evac[b], 1)
            for t in range(NT):
                act.wait_ge(cs_ready, t + 1)
                act.activation(crow[:, 0:248], crow[:, 0:248], ACT.Exp).then_inc(cp_exp, 1)
                if t:
                    act.wait_ge(co_mm, t)
                for i in range(2):
                    b = plan.bank(("cT", t, i))
                    act.wait_ge(filled, plan.at["cT", t, i] + 1)
                    act.activation(cPT[0:N_CMP, 4 * i:4 * i + 4, :].rearrange("p h q -> p (h q)"), bank[b][0:N_CMP, :], ACT.Copy)\
                       .then_inc(evac[b], 1)
                act.wait_ge(co_mm, t + 1)
                act.activation(yb_tok[:, t, :], bank[4 + t % 2][:, :], ACT.Copy).then_inc(co_sb, 1)

            def turned(u):
                n = (u // 16 + 1) * P
                act.wait_ge(pt_mm, u + 1)
                if u >= 2:
                    act.wait_ge(o2_mm, u - 1)
                act.activation(PTb[u % 2][:, 0:n], bank[4 + u % 2][:, 0:n], ACT.Copy).then_inc(pt_sb, 1)
            for u in range(64):
                n = (u // 16 + 1) * P
                act.wait_ge(mx_ready, u + 1)
                if u >= 2:
                    act.wait_ge(pt_mm, u - 1)
                act.activation(Pb[u % 2][:, 0:n], s_bank(u)[:, 0:n], ACT.Exp, bias=nmax[:, u:u + 1],
                               accum_out=psum_[:, u:u + 1]).then_inc(p_ready, 1)
                if u:
                    turned(u - 1)
            turned(63)
            for t in range(NT):
                b = plan.bank(("ybT", t))
                act.wait_ge(filled, plan.at["ybT", t] + 1)
                act.activation(ybT[:, :, t * P:(t + 1) * P], bank[b][:, :].rearrange("p (c q) -> p c q", c=4), ACT.Copy).then_inc(evac[b], 1)
            for m in range(KD):
                for i in range(2):
                    if m >= 2:
                        act.wait_ge(mg_ready, m - 1)
                    take(("mg", m, i), A(24 + 2 * (m % 2) + i), ACT.Sigmoid)
            for k in range(KD):
                tile_evacuated(act, ("w_o", k))
            squares(3)
            root(3)
            for m in range(KF):
                if m >= 2:
                    act.wait_ge(conv_ready, m - 1)
                take(("gu", m, 0), A(22 + m % 2), ACT.Copy)
                act.wait_ge(conv_ready, m + 1)
                if m >= 2:
                    tile_evacuated(act, ("gu", m - 2, 1))
                act.activation(A(26 + m % 2), A(24 + m % 2), ACT.Silu).then_inc(silu_ready, 1)

        @block.vector
        def _(dve):
            chained = [0]

            def link(ins):
                chained[0] += 1
                ins.then_inc(dve_chain, 1)
                dve.wait_ge(dve_chain, chained[0])

            counts = {}

            def link_to(ins, signal, n=1):
                counts[signal.name] = counts.get(signal.name, 0) + n
                ins.then_inc(signal, n)
                dve.wait_ge(signal, counts[signal.name])

            def link_evac(ins, key):
                ins.then_inc(evac[plan.bank(key)], 1)
                tile_evacuated(dve, key)

            def row(name):
                return vec[:, VEC_AT[name]:VEC_AT[name] + ROW_COLS[name]]

            def four_k(x):
                return x.rearrange("p (b g d) -> p b g d", b=2, g=2)

            def kk_tok(t):
                return kv_tok[:, t, :].rearrange("p (b v g d) -> p b v g d", b=2, v=2, g=2)[:, :, 0, :, :]

            def conv(dst, src, w, bias, signal=None):
                if bias is None:
                    link(dve.tensor_scalar(dst, src, w[2], None, ALU.mult))
                else:
                    link(dve.tensor_scalar(dst, src, w[2], bias, ALU.mult, ALU.add))
                link(dve.scalar_tensor_tensor(out=dst[:, 1:T], in0=src[:, 0:T - 1], scalar=w[1], in1=dst[:, 1:T], op0=ALU.mult, op1=ALU.add))
                ins = dve.scalar_tensor_tensor(out=dst[:, 2:T], in0=src[:, 0:T - 2], scalar=w[0], in1=dst[:, 2:T], op0=ALU.mult, op1=ALU.add)
                if signal is None:
                    link(ins)
                else:
                    ins.then_inc(signal, 1)

            def gated(m):
                b = plan.bank(("gu", m, 1))
                dve.wait_ge(silu_ready, m + 1)
                dve.wait_ge(filled, plan.at["gu", m, 1] + 1)
                dve.tensor_tensor(actT(m), A(26 + m % 2), bank[b][:, :], ALU.mult).then_inc(evac[b], 1)

            def norm_plain(stage, name):
                dve.wait_ge(rs_ready, stage + 1)
                link(dve.reciprocal(rstd, rstd))
                for k in range(KD):
                    dve.scalar_tensor_tensor(out=hT[:, k, :], in0=xT[:, k, :], scalar=col(name, k), in1=rstd,
                                             op0=ALU.mult, op1=ALU.mult).then_inc(h_ready, 1)

            def norm_scale(stage, scale, shift):
                dve.wait_ge(rs_ready, stage + 1)
                link(dve.reciprocal(rstd, rstd))
                for k in range(KD):
                    ins = dve.tensor_tensor(hT[:, k, :], xT[:, k, :], rstd, ALU.mult)
                link(ins)
                for k in range(KD):
                    dve.tensor_scalar(hT[:, k, :], hT[:, k, :], scale(k), shift(k), ALU.mult, ALU.add).then_inc(h_ready, 1)

            dve.wait_ge(vec_in, 16)
            dve.wait_ge(pos_in, 16)
            dve.wait_ge(cst_in, 16)
            link(dve.tensor_copy(small[:, 120:124], u_pos[:, :]))
            ang, turns = trig[:, 128:256], trig[:, 256:384]
            for t in range(NT):
                ins = dve.tensor_scalar(ang[:, t * 32:(t + 1) * 32], const("inv_freq"), small[:, 120 + t:121 + t], None, ALU.mult)
            link(ins)
            link(dve.tensor_scalar(turns, ang, 1.0 / TURN, ROUNDER, ALU.mult, ALU.add))
            link(dve.tensor_scalar(turns, turns, ROUNDER, None, ALU.subtract))
            for part in TURN_PARTS:
                link(dve.scalar_tensor_tensor(out=ang, in0=turns, scalar=-part, in1=ang, op0=ALU.mult, op1=ALU.add))
            link(dve.tensor_scalar(ang, ang, PI_LOW, -PI_LOW, ALU.min, ALU.max))
            link(dve.tensor_scalar(trig[:, 0:128], ang, TURN / 4, None, ALU.add))
            link(dve.tensor_scalar(turns, trig[:, 0:128], TURN / 2, -TURN, ALU.is_gt, ALU.mult))
            link(dve.tensor_tensor(trig[:, 0:128], trig[:, 0:128], turns, ALU.add))
            dve.tensor_scalar(trig[:, 0:128], trig[:, 0:128], PI_LOW, -PI_LOW, ALU.min, ALU.max).then_inc(angles, 1)
            dve.tensor_scalar(omka, vec[:, VEC_AT["k_a"]:VEC_AT["k_a"] + 4], -1.0, 1.0, ALU.mult, ALU.add)
            dve.tensor_scalar(omu, vec[:, VEC_AT["shift_mu"]:VEC_AT["shift_mu"] + NZ], -1.0, 1.0, ALU.mult, ALU.add)
            dve.wait_ge(sig_c, 1)
            dve.tensor_tensor(cond, sigc, vec[:, VEC_AT["c"]:VEC_AT["c"] + KD], ALU.mult).then_inc(cond_ready, 1)
            dve.wait_ge(cond_ready, 1)

            def ada(n):
                s = slot_of["ada", n]
                dve.wait_ge(slot_in[s], 16 * load_of["ada", n])
                if n >= 2:
                    dve.wait_ge(mod_mm, n - 1)
                w = ring[:, s * MAX_CHUNK:(s + 1) * MAX_CHUNK].rearrange("p (k n) -> p k n", k=KD)
                link(dve.tensor_scalar(acc[n % 2], w[:, 0, :], cond[:, 0:1], None, ALU.mult))
                for k in range(1, KD - 1):
                    link(dve.scalar_tensor_tensor(out=acc[n % 2], in0=w[:, k, :], scalar=cond[:, k:k + 1], in1=acc[n % 2],
                                                  op0=ALU.mult, op1=ALU.add))
                k = KD - 1
                dve.scalar_tensor_tensor(out=acc[n % 2], in0=w[:, k, :], scalar=cond[:, k:k + 1], in1=acc[n % 2],
                                         op0=ALU.mult, op1=ALU.add).then_inc(ada_used, 1)

            def modulation(lo, hi, chunks_done):
                dve.wait_ge(mod_mm, chunks_done)
                link(dve.tensor_tensor(mod[:, lo:hi], bank[5][:, lo:hi], vec[:, VEC_AT["ada_b"] + lo:VEC_AT["ada_b"] + hi], ALU.add))

            for n in range(4):
                ada(n)
            modulation(0, 16, 4)
            link(dve.scalar_tensor_tensor(out=gain[:, :], in0=mod[:, 8:16], scalar=1.0,
                                          in1=vec[:, VEC_AT["norm1_g"]:VEC_AT["norm1_g"] + KD], op0=ALU.add, op1=ALU.mult))
            norm_scale(0, lambda k: gain[:, k:k + 1], lambda k: mod[:, k:k + 1])
            later = 4
            for m in range(NZ):
                b = plan.bank(("z", m))
                dve.wait_ge(z_scaled, m + 1)
                dve.scalar_tensor_tensor(out=zs(m)[:, 1:T], in0=bank[b][:, 0:T - 1], scalar=col("shift_mu", m),
                                         in1=zs(m)[:, 1:T], op0=ALU.mult, op1=ALU.add).then_inc(evac[b], 1)
                if m % 2 == 1 and later < 12:
                    ada(later)
                    later += 1
            while later < 12:
                ada(later)
                later += 1
            modulation(16, 48, 12)

            dve.wait_ge(filled, plan.at["v", NT - 1] + 1)
            for c in range(4):
                dve.tensor_scalar(kkT[:, c, :], zs(4 + c), col("k_k", c), None, ALU.mult).then_inc(kk0_ready, 1)
            link(dve.memset(S1[:, :, :, 0:1], 0.0))
            for c in range(4):
                tile_evacuated(dve, ("wag", c, 0))
                for k in range(NT):
                    s = sigw[:, c, k * P:(k + 1) * P]
                    ins = dve.tensor_tensor_scan(S1[:, c, k, 1:129], ones, s, 0.0, ALU.mult, ALU.add)
            link(ins)
            dve.tensor_scalar(mids, S1[:, :, :, 64], DECAY_K, None, ALU.mult)
            dve.tensor_scalar(nmids, S1[:, :, :, 64], -DECAY_K, None, ALU.mult).then_inc(mid_ready, 1)
            for c in range(4):
                tile_evacuated(dve, ("wag", c, 1))
                t = KR[:, c, 0, :]
                link(dve.tensor_scalar(t, aT[:, c, :], col("k_a", c), omka[:, c:c + 1], ALU.mult, ALU.add))
                link(dve.tensor_tensor(zs(4 + c), zs(4 + c), t, ALU.mult))
                dve.scalar_tensor_tensor(out=KR[:, c, 1, :], in0=zs(c), scalar=col("r_k", c), in1=zs(4 + c),
                                         op0=ALU.mult, op1=ALU.mult).then_inc(rk_ready, 1)
            for c in range(4):
                b = plan.bank(("rk", c))
                dve.wait_ge(filled, plan.at["rk", c] + 1)
                dve.tensor_tensor(bonus[:, c, :], bank[b][:, :], zs(8 + c), ALU.mult).then_inc(evac[b], 1)
                tile_evacuated(dve, ("kk", c))
                link(dve.tensor_scalar(nrm[:, c, :], nrm[:, c, :], L2_EPS, None, ALU.max))
                link(dve.reciprocal(nrm[:, c, :], nrm[:, c, :]))
                link(dve.tensor_tensor(kkT[:, c, :], kkT[:, c, :], nrm[:, c, :], ALU.mult))
                dve.wait_ge(exp_ready, 4 * (c + 1))
                four = lambda x: x.rearrange("p (k t) -> p k t", k=NT)
                dve.tensor_tensor(four(KR[:, c, 0, :]), four(kkT[:, c, :]), E1[:, c, :, 0:128], ALU.mult)
                dve.tensor_tensor(four(KR[:, c, 1, :]), four(zs(c)), E1[:, c, :, 1:129], ALU.mult)
                dve.tensor_tensor(four(ktT[:, c, :]), four(zs(4 + c)), E2[:, c, :, :], ALU.mult)
                link(dve.tensor_tensor(aT[:, c, :], aT[:, c, :], kkT[:, c, :], ALU.mult))
                dve.tensor_tensor(four(btT[:, c, :]), four(aT[:, c, :]), E2[:, c, :, :], ALU.mult).then_inc(prep_done, 1)
            dve.wait_ge(exp_ready, 17)
            link(dve.tensor_tensor(dec[:, :, 0:3], E1[:, :, 0:3, 128], emid[:, :, 1:4], ALU.mult))
            link(dve.tensor_copy(dec[:, :, 3], E1[:, :, 3, 128]))
            tile_evacuated(dve, ("wag", 3, 2))
            dve.memset(S_sc, 0.0).then_inc(s_sb, 1)

            both = [const("strict"), const("incl")]
            mask2 = cst[:, CONST_AT["strict"]:CONST_AT["strict"] + 2 * P]
            q = 0
            for k in range(NT):
                for h in range(NH):
                    b = plan.bank(("am", k, h))
                    dve.wait_ge(filled, plan.at["am", k, h] + 1)
                    dve.tensor_tensor(AM[:, h, :].rearrange("p (j n) -> p j n", j=2),
                                      bank[b][:, :].rearrange("p (j n) -> p j n", j=2),
                                      mask2[:, None, :].to_broadcast([P, 2, 2 * P]), ALU.mult).then_inc(evac[b], 1)
                dve.tensor_copy(X[:, :, :], ident[:, None, :].to_broadcast([P, NH, P])).then_inc(x_sb, 1)
                dve.tensor_copy(XT[:, :, :], ident[:, None, :].to_broadcast([P, NH, P])).then_inc(xt_sb, 1)
                for lv in range(7):
                    mask = const("level")[:, lv * P:(lv + 1) * P]
                    for g in range(2):
                        hs = slice(4 * g, 4 * g + 4)
                        dve.wait_ge(t1_mm, (k * 7 + lv) * 2 + g + 1)
                        dve.tensor_tensor(T1[:, hs, :], bank[4 + g][:, :].rearrange("p (h n) -> p h n", h=4),
                                          mask[:, None, :].to_broadcast([P, 4, P]), ALU.mult).then_inc(t1_sb, 1)
                    for g in range(2):
                        hs = slice(4 * g, 4 * g + 4)
                        if lv < 6:
                            dve.wait_ge(xn_mm, (k * 6 + lv) * 2 + g + 1)
                            dve.tensor_tensor(X[:, hs, :], X[:, hs, :], bank[6 + g][:, :].rearrange("p (h n) -> p h n", h=4),
                                              ALU.subtract).then_inc(x_sb, 1)
                        dve.wait_ge(xt_mm, (k * 7 + lv) * 2 + g + 1)
                        dve.tensor_tensor(XT[:, hs, :], XT[:, hs, :], bank[4 + g][:, :].rearrange("p (h n) -> p h n", h=4),
                                          ALU.subtract).then_inc(xt_sb, 1)
                for i in (2 * k, 2 * k + 1):
                    tile_evacuated(dve, ("sbn", i))
                    link(dve.reciprocal(qk_sq(i), qk_sq(i)))
                    if i < 4:
                        link(dve.tensor_scalar(qk_sq(i), qk_sq(i), HD ** -0.5, None, ALU.mult))
                    dve.scalar_tensor_tensor(out=A(14 + i), in0=A(14 + i), scalar=col("q_norm_g") if i < 4 else col("k_norm_g"),
                                             in1=qk_sq(i), op0=ALU.mult, op1=ALU.mult).then_inc(qkn_ready, 1)
                dve.wait_ge(s_mm, k + 1)
                Sv = S_sc.rearrange("p (c n) -> p c n", c=4)
                Pv = bank[5][:, :].rearrange("p (c n) -> p c n", c=4)
                for half in range(2):
                    ps = slice(HD * half, HD * half + HD)
                    ins = dve.tensor_tensor(Sv[ps, :, ps], Sv[ps, :, ps], Pv[ps, :, ps], ALU.add)
                link(ins)
                for half in range(2):
                    ps = slice(HD * half, HD * half + HD)
                    ins = dve.tensor_tensor(Sv[ps, :, ps], Sv[ps, :, ps], dec[ps, :, k:k + 1].to_broadcast([HD, 4, HD]), ALU.mult)
                ins.then_inc(s_sb, 1)
                dve.wait_ge(y_mm, k + 1)
                heads = lambda x: x.rearrange("p (h d) -> p h d", h=NH)
                yv = heads(bank[4][:, :])
                link(dve.tensor_reduce(hsum, yv, AX.X, ALU.add))
                link(dve.tensor_scalar(hsum, hsum, 1.0 / HD, None, ALU.mult))
                if k:
                    tile_evacuated(dve, ("yT", k - 1))
                link(dve.tensor_tensor(heads(yn), yv, hsum[:, :, None].to_broadcast([P, NH, HD]), ALU.subtract))
                link(dve.tensor_tensor(ysq, yn, yn, ALU.mult))
                dve.tensor_reduce(hvar, heads(ysq), AX.X, ALU.add).then_inc(var_ready, 1)
                dve.wait_ge(std_ready, k + 1)
                link(dve.reciprocal(hrstd, hstd))
                dve.tensor_tensor(heads(yn), heads(yn), hrstd[:, :, None].to_broadcast([P, NH, HD]), ALU.mult).then_inc(yn_ready, 1)
            for k in range(NT):
                tile_evacuated(dve, ("yT", k))
            for c in range(4):
                link(dve.tensor_tensor(mixT(c), mixT(c), bonus[:, c, :], ALU.add))
                dve.tensor_tensor(mixT(c), mixT(c), gT[:, c, :], ALU.mult).then_inc(mix_ready, 1)

            def softplus(h):
                for kt in range(NT):
                    e = sb_e(h, kt)
                    dve.wait_ge(ln_ready, h * NT + kt + 1)
                    link(dve.scalar_tensor_tensor(out=e, in0=sb_logits(h, kt), scalar=0.0, in1=e, op0=ALU.max, op1=ALU.add))
                    dve.tensor_tensor(e[:, 0:P], e[:, 0:P], const("strict"), ALU.mult).then_inc(sp_ready, 1)

            def take_out(h):
                dve.wait_ge(o_mm, h + 1)
                dve.tensor_copy(o_tok[:, :, h * HD:(h + 1) * HD], sb_out(h).rearrange("p (t d) -> p t d", t=4)).then_inc(o_sb, 1)
            softplus(0)
            for h in range(NH):
                if h + 1 < NH:
                    softplus(h + 1)
                dve.wait_ge(r_mm, NT * (h + 1))
                for kt in range(NT):
                    diag = sb_logits(h, kt)[:, 0:P]
                    dve.tensor_tensor(diag, diag, const("sb_mask"), ALU.add).then_inc(r_masked, 1)
                if h:
                    take_out(h - 1)
            take_out(NH - 1)
            dve.wait_ge(o_sb, NH)
            for t in range(NT):
                heads = lambda x: x.rearrange("p (h d) -> p h d", h=NH)
                link(dve.tensor_tensor(ysq, o_tok[:, t, :], o_tok[:, t, :], ALU.mult))
                dve.tensor_reduce(hvar, heads(ysq), AX.X, ALU.add).then_inc(var_ready, 1)
                dve.wait_ge(std_ready, NT + t + 1)
                link(dve.reciprocal(hrstd, hstd))
                dve.tensor_tensor(heads(o_tok[:, t, :]), heads(o_tok[:, t, :]), hrstd[:, :, None].to_broadcast([P, NH, HD]), ALU.mult)\
                   .then_inc(on_ready, 1)
            for m in range(KD):
                b = plan.bank(("wo", m))
                dve.wait_ge(filled, plan.at["wo", m] + 1)
                dve.scalar_tensor_tensor(out=xT[:, m, :], in0=bank[b][:, :], scalar=mod[:, 16 + m:17 + m], in1=xT[:, m, :],
                                         op0=ALU.mult, op1=ALU.add).then_inc(evac[b], 1)

            link(dve.scalar_tensor_tensor(out=gain[:, :], in0=mod[:, 32:40], scalar=1.0,
                                          in1=vec[:, VEC_AT["norm2_g"]:VEC_AT["norm2_g"] + KD], op0=ALU.add, op1=ALU.mult))
            norm_scale(1, lambda k: gain[:, k:k + 1], lambda k: mod[:, 24 + k:25 + k])
            for t in range(NT):
                b = plan.bank(("lg", t))
                dve.wait_ge(filled, plan.at["lg", t] + 1)
                link_evac(dve.tensor_tensor(LG[:, t, :], bank[b][:, 0:EXPERTS], row("router_b"), ALU.add), ("lg", t))
            for t in range(NT):
                link(dve.max(TOPV[:, t, :], LG[:, t, :]))
                ins = dve.max_index(top_idx[:, t, :], TOPV[:, t, :], LG[:, t, :])
            link(ins)
            dve.tensor_copy(TOPF, top_idx[:, :, :])
            dve.tensor_tensor(TOPG, TOPV[:, :, 0:TOP_K], TOPV[:, :, 0:1].to_broadcast([P, NT, TOP_K]), ALU.subtract).then_inc(top_ready, 1)
            dve.wait_ge(eg_ready, 1)
            link(dve.tensor_reduce(GSUM, TOPG, AX.X, ALU.add))
            link(dve.reciprocal(GSUM, GSUM))
            link(dve.tensor_tensor(TOPG, TOPG, GSUM[:, :, None].to_broadcast([P, NT, TOP_K]), ALU.mult))
            for t in range(NT):
                link(dve.tensor_scalar(SEL[:, t, :], const("expert"), TOPF[:, t, 0:1], None, ALU.is_equal))
                link(dve.tensor_scalar(GATE[:, t, :], const("expert"), TOPF[:, t, 0:1], TOPG[:, t, 0:1], ALU.is_equal, ALU.mult))
                for r in range(1, TOP_K):
                    link(dve.scalar_tensor_tensor(out=SEL[:, t, :], in0=const("expert"), scalar=TOPF[:, t, r:r + 1], in1=SEL[:, t, :],
                                                  op0=ALU.is_equal, op1=ALU.add))
                    link(dve.tensor_scalar(GTMP, const("expert"), TOPF[:, t, r:r + 1], TOPG[:, t, r:r + 1], ALU.is_equal, ALU.mult))
                    link(dve.tensor_tensor(GATE[:, t, :], GATE[:, t, :], GTMP, ALU.add))
            link_to(dve.tensor_copy(token.rearrange("p t i -> p (t i)"), const("token")), route_ready)
            for t in range(NT):
                b = plan.bank(("pos", t))
                dve.wait_ge(filled, plan.at["pos", t] + 1)
                link_evac(dve.scalar_tensor_tensor(out=POS[:, t, 0:EXPERTS], in0=bank[b][:, 0:EXPERTS], scalar=1.0, in1=SEL[:, t, :],
                                                   op0=ALU.add, op1=ALU.mult), ("pos", t))
            link(dve.tensor_scalar(POS[:, :, 0:EXPERTS], POS[:, :, 0:EXPERTS], -1.0, None, ALU.add))
            link(dve.memset(POS[:, :, EXPERTS:EXPERTS + 2], -1.0))
            b = plan.bank(("cnt",))
            dve.wait_ge(filled, plan.at["cnt",] + 1)
            link_evac(dve.tensor_reduce(NPF[:, 0:1], bank[b][:, 0:EXPERTS], AX.X, ALU.max), ("cnt",))
            link(dve.tensor_scalar(NPF[:, 1:2], NPF[:, 0:1], 128.5, 1.0, ALU.is_gt, ALU.add))
            link(dve.scalar_tensor_tensor(out=NPF[:, 1:2], in0=NPF[:, 0:1], scalar=256.5, in1=NPF[:, 1:2], op0=ALU.is_gt, op1=ALU.add))
            link(dve.scalar_tensor_tensor(out=NPF[:, 1:2], in0=NPF[:, 0:1], scalar=384.5, in1=NPF[:, 1:2], op0=ALU.is_gt, op1=ALU.add))
            dve.tensor_copy(n_pass[:, :], NPF[:, 1:2]).then_inc(npass_ready, 1)
            dve.sem_inc(lin_ready, 1)
            dve.sem_inc(ye_sb, 1)
            for t in range(NT):
                for r in range(TOP_K):
                    ins = dve.scalar_tensor_tensor(out=picks[:, t * TOP_K + r, :], in0=const("expert"), scalar=TOPF[:, t, r:r + 1],
                                                   in1=POS[:, t, 0:EXPERTS], op0=ALU.is_equal, op1=ALU.mult)
            link(ins)
            link(dve.tensor_reduce(choice_at, picks, AX.X, ALU.add))
            dve.wait_ge(npass_ready, 1)
            passes = dve.value_load(n_pass[0:1, 0:1], min_val=1, max_val=4)
            LINKS = 3

            def look_up(j, n):
                i = j * LOOKS + n
                dve.wait_ge(idx_mm, i + 1)
                for t in range(NT):
                    ins = dve.tensor_scalar(OH[:, t, :], const("iota"), POS[:, t, bass.ds(n, 1)], None, ALU.is_equal)
                ins.then_inc(oh_ready, 1)
                dve.wait_ge(idx_mm, i + 2)
                dve.tensor_reduce(slot_f[:, 0:1], bank[4][:, 0:2], AX.X, ALU.add).then_inc(idx_f, 1)
                dve.wait_ge(idx_f, i + 1)
                dve.wait_ge(idx_used, i + 1)
                dve.tensor_copy(slot_token[:, :], slot_f[:, 0:1]).then_inc(idx_sb, 1)

            def activations(j, e):
                it = j * EXPERTS + e
                dve.wait_ge(w1_free, it * KD + 2 * KD)
                dve.wait_ge(b1_in, it * 16 + 16)
                dve.wait_ge(aT_mm, it + 1)
                for i in range(2):
                    ins = dve.tensor_tensor(G[:, i * T:(i + 1) * T], bank[i][:, :], B1[:, i * T:(i + 1) * T], ALU.add)
                ins.then_inc(moe_chain, 1)
                dve.wait_ge(moe_chain, it * LINKS + 1)
                dve.tensor_scalar(G, G, 7.0, None, ALU.min).then_inc(glu_ready, 1)
                for i in range(2):
                    ins = dve.tensor_tensor(LIN[:, i * T:(i + 1) * T], bank[2 + i][:, :], B1[:, (2 + i) * T:(3 + i) * T], ALU.add)
                ins.then_inc(lin_ready, 1)
                dve.wait_ge(lin_ready, it + 2)
                dve.tensor_scalar(LIN, LIN, 7.0, -7.0, ALU.min, ALU.max).then_inc(moe_chain, 1)
                dve.wait_ge(moe_chain, it * LINKS + 2)
                dve.scalar_tensor_tensor(out=LIN, in0=LIN, scalar=1.0, in1=G, op0=ALU.add, op1=ALU.mult).then_inc(moe_chain, 1)
                dve.wait_ge(moe_chain, it * LINKS + 3)
                dve.wait_ge(sig_ready, it + 1)
                dve.tensor_tensor(G, LIN, SG, ALU.mult).then_inc(act_ready, 1)

            def take_rows(j, e):
                it = j * EXPERTS + e
                dve.wait_ge(w2_free, it * KD + 2 * KD)
                dve.wait_ge(y_free, it + 1)
                for i in range(2):
                    ins = dve.tensor_copy(Y[:, i * T:(i + 1) * T], bank[6 + i][:, :])
                ins.then_inc(ye_sb, 1)
            by_tile = lambda x: x.rearrange("p (t r) -> p t r", t=NT)
            with dve.Fori(0, passes) as j:
                for n in range(3):
                    look_up(j, n)
                dve.tensor_scalar(choice_in, choice_at, 0.0, float(P - 1), ALU.max, ALU.min).then_inc(choice_chain, 1)
                dve.wait_ge(choice_chain, j * 3 + 1)
                dve.scalar_tensor_tensor(out=by_tile(GTMP[:, 0:NT * TOP_K]), in0=TOPF[:, :, 0:TOP_K], scalar=float(P),
                                         in1=by_tile(choice_in), op0=ALU.mult, op1=ALU.add)
                dve.tensor_tensor(choice_gate, choice_in, choice_at, ALU.is_equal).then_inc(choice_chain, 1)
                dve.wait_ge(choice_chain, j * 3 + 2)
                dve.tensor_copy(choice_row, GTMP[:, 0:NT * TOP_K])
                dve.tensor_tensor(by_tile(choice_gate), by_tile(choice_gate), TOPG, ALU.mult).then_inc(choice_chain, 1)
                dve.wait_ge(choice_chain, j * 3 + 3)
                dve.sem_inc(rows_ready, 1)
                activations(j, 0)
                with dve.Fori(0, EXPERTS - 1) as e:
                    look_up(j, e + 3)
                    activations(j, e + 1)
                    take_rows(j, e)
                take_rows(j, EXPERTS - 1)
                for t in range(NT):
                    dve.wait_ge(yr_in[t], j * (16 * TOP_K) + 16 * TOP_K)
                    total = YR[t * TOP_K]
                    for r in range(TOP_K):
                        gate = choice_gate[:, t * TOP_K + r:t * TOP_K + r + 1]
                        if r == 0:
                            ins = dve.tensor_scalar(total, total, gate, None, ALU.mult)
                        else:
                            dve.wait_ge(sum_chain, (j * NT + t) * (TOP_K - 1) + r)
                            ins = dve.scalar_tensor_tensor(out=total, in0=YR[t * TOP_K + r], scalar=gate, in1=total,
                                                           op0=ALU.mult, op1=ALU.add)
                        ins.then_inc(sum_chain if r < TOP_K - 1 else sum_ready, 1)
                for m in range(KD):
                    dve.wait_ge(mix_mm, j * (NT - 1 + KD) + (NT + m))
                    ins = dve.scalar_tensor_tensor(out=xT[:, m, :], in0=bank[m][:, :], scalar=mod[:, 40 + m:41 + m], in1=xT[:, m, :],
                                                   op0=ALU.mult, op1=ALU.add)
                dve.memset(GATE_T, 0.0)
                dve.tensor_scalar(choice_at, choice_at, -float(P), None, ALU.add)
                dve.tensor_scalar(POS, POS, -float(P), None, ALU.add).then_inc(passed, 1)
                dve.wait_ge(passed, j + 1)
            dve.sem_inc(x2_ready, 1)

            norm_plain(2, "norm1_g_2")
            for t in range(NT):
                tile_evacuated(dve, ("q2", t))
                tile_evacuated(dve, ("kv2", t))
                link(dve.tensor_tensor(scr, q_tok[:, t, :], q_tok[:, t, :], ALU.mult))
                dve.tensor_reduce(stats[:, t, 0:8], scr.rearrange("p (h d) -> p h d", h=8), AX.X, ALU.add)
                link(dve.tensor_tensor(four_k(scr2[:, 0:256]), kk_tok(t), kk_tok(t), ALU.mult))
                ins = dve.tensor_reduce(stats[:, t, 8:12], scr2[:, 0:256].rearrange("p (h d) -> p h d", h=4), AX.X, ALU.add)
            ins.then_inc(qn_sq, 1)
            dve.wait_ge(qn_rt, 1)
            link(dve.reciprocal(nmax[:, 0:48], nmax[:, 0:48]))
            link(dve.tensor_scalar(stats[:, :, 0:8], stats[:, :, 0:8], HD ** -0.5, None, ALU.mult))

            def rotate(n, x1, x2, o1, o2, t):
                shape = list(x1.shape)
                cos = cos_sin[:, 0, t, :]
                sin = cos_sin[:, 1, t, :]
                if len(shape) == 4:
                    cs = [c[:, None, None, :].to_broadcast(shape) for c in (cos, sin)]
                else:
                    cs = [c[:, None, :].to_broadcast(shape) for c in (cos, sin)]
                w = n * 32
                tmp = [scr[:, 0:w], scr[:, 256:256 + w], scr2[:, 0:w], scr2[:, 256:256 + w]]
                if len(shape) == 4:
                    tmp = [x.rearrange("p (a b d) -> p a b d", a=shape[1], b=shape[2]) for x in tmp]
                else:
                    tmp = [x.rearrange("p (a d) -> p a d", a=shape[1]) for x in tmp]
                dve.tensor_tensor(tmp[0], x1, cs[0], ALU.mult)
                dve.tensor_tensor(tmp[1], x2, cs[1], ALU.mult)
                dve.tensor_tensor(tmp[2], x2, cs[0], ALU.mult)
                link(dve.tensor_tensor(tmp[3], x1, cs[1], ALU.mult))
                dve.tensor_tensor(o1, tmp[0], tmp[1], ALU.subtract)
                return dve.tensor_tensor(o2, tmp[2], tmp[3], ALU.add)
            for t in range(NT):
                q = q_tok[:, t, :].rearrange("p (h d) -> p h d", h=8)
                link(dve.tensor_tensor(q, q, stats[:, t, 0:8, None].to_broadcast([P, 8, HD]), ALU.mult))
                link(dve.tensor_tensor(q, q, row("q_norm_g_2")[:, None, :].to_broadcast([P, 8, HD]), ALU.mult))
                src = q_tok[:, t, :].rearrange("p (j c d) -> p j c d", j=2, c=4)
                dst = q_tok[:, t, :].rearrange("p (c j d) -> p j c d", j=2, c=4)
                link_to(rotate(8, src[:, :, :, 0:32], src[:, :, :, 32:64], dst[:, :, :, 0:32], dst[:, :, :, 32:64], t), q_ready)
                k = kk_tok(t)
                link(dve.tensor_tensor(k, k, stats[:, t, 8:12].rearrange("p (b g) -> p b g", b=2)[:, :, :, None].to_broadcast([P, 2, 2, HD]), ALU.mult))
                g = row("k_norm_g_2")[:, HD:3 * HD].rearrange("p (b d) -> p b d", b=2)[:, :, None, :].to_broadcast([P, 2, 2, HD])
                link(dve.tensor_tensor(k, k, g, ALU.mult))
                link_to(rotate(4, k[:, :, :, 0:32], k[:, :, :, 32:64], k[:, :, :, 0:32], k[:, :, :, 32:64], t), k_ready)
            for c in range(4):
                tile_evacuated(dve, ("ac", c))
                dve.wait_ge(filled, plan.at["ax", c] + 1)
                link_evac(dve.tensor_tensor(yaT[:, c, :], bank[plan.bank(("ax", c))][:, :], yaT[:, c, :], ALU.mult), ("ax", c))
            for c in range(4):
                conv(scr, yaT[:, c, :], [col("conv_a_w_2", 4 * j + c) for j in range(3)], None)
                dve.wait_ge(filled, plan.at["ab", c] + 1)
                link_evac(dve.tensor_tensor(yaT[:, c, :], bank[plan.bank(("ab", c))][:, :], scr, ALU.mult), ("ab", c))
            b = plan.bank(("kvc",))
            dve.wait_ge(filled, plan.at["kvc",] + 1)
            dve.tensor_copy(v_cmp, bank[b][0:N_CMP, 128:256])
            link_evac(dve.tensor_copy(kcn, bank[b][0:N_CMP, 0:128]), ("kvc",))
            pair = lambda x: x.rearrange("p (g d) -> p g d", g=2)
            link(dve.tensor_tensor(scr[0:N_CMP, 0:P], kcn, kcn, ALU.mult))
            dve.tensor_reduce(cstat[0:N_CMP, 0:2], pair(scr[0:N_CMP, 0:P]), AX.X, ALU.add).then_inc(kc_sq, 1)
            dve.wait_ge(kc_rt, 1)
            link(dve.reciprocal(cstat[0:N_CMP, 0:2], cstat[0:N_CMP, 0:2]))
            link(dve.tensor_tensor(pair(kcn), pair(kcn), cstat[0:N_CMP, 0:2, None].to_broadcast([N_CMP, 2, HD]), ALU.mult))
            dve.tensor_tensor(pair(kcn), pair(kcn), row("k_norm_g_2")[0:N_CMP, None, 0:HD].to_broadcast([N_CMP, 2, HD]), ALU.mult)\
               .then_inc(kc_ready, 1)
            hk = lambda x: x.rearrange("p (h n) -> p h n", h=NH)
            sc = crow[:, 0:248]
            gate3 = lambda t, j: nsa_gate[:, t, :].rearrange("p (h j) -> p h j", j=3)[:, :, j]
            for t in range(NT):
                bias = const("cmp_bias")[:, t * 32:t * 32 + N_CMP]
                ok = const("cmp_mask")[:, t * 32:t * 32 + N_CMP]
                if t:
                    dve.wait_ge(filled, plan.at["cT", t - 1, 1] + 1)
                for g in range(2):
                    b = plan.bank(("cs", t, g))
                    dve.wait_ge(filled, plan.at["cs", t, g] + 1)
                    src = bank[b][:, 0:128].rearrange("p (h n) -> p h n", h=4)[:, :, 0:N_CMP]
                    link_evac(dve.tensor_tensor(hk(sc)[:, 4 * g:4 * g + 4, :], src, bias[:, None, :].to_broadcast([P, 4, N_CMP]), ALU.add), ("cs", t, g))
                link(dve.tensor_reduce(cmx, hk(sc), AX.X, ALU.max))
                dve.tensor_tensor(hk(sc), hk(sc), cmx[:, :, None].to_broadcast([P, NH, N_CMP]), ALU.subtract).then_inc(cs_ready, 1)
                dve.wait_ge(cp_exp, t + 1)
                link(dve.tensor_reduce(csum, hk(sc), AX.X, ALU.add))
                link(dve.reciprocal(csum, csum))
                link(dve.tensor_tensor(gs, csum, gate3(t, 0), ALU.mult))
                link(dve.tensor_tensor(hk(sc), hk(sc), gs[:, :, None].to_broadcast([P, NH, N_CMP]), ALU.mult))
                dve.tensor_tensor(hk(sc), hk(sc), ok[:, None, :].to_broadcast([P, NH, N_CMP]), ALU.mult).then_inc(cp_ready, 1)
            def combine(t):
                dve.wait_ge(p_ready, 16 * (t + 1))
                sums = psum_[:, 16 * t:16 * t + 16]
                link(dve.reciprocal(sums, sums))
                dve.wait_ge(o2_mm, 16 * (t + 1))
                dve.wait_ge(co_sb, t + 1)
                for j in range(2):
                    link(dve.tensor_tensor(gs, sums.rearrange("p (h j) -> p h j", j=2)[:, :, j], gate3(t, 1 + j), ALU.mult))
                    link(dve.tensor_tensor(hk(yb_tmp), hk(bank[j][:, :]), gs[:, :, None].to_broadcast([P, NH, HD]), ALU.mult))
                    ins = dve.tensor_tensor(yb_tok[:, t, :], yb_tok[:, t, :], yb_tmp, ALU.add)
                    if j == 0:
                        link(ins)
                link_to(ins, yb_ready)

            for u in range(64):
                t = u // 16
                s = s_bank(u)
                dve.wait_ge(s2_mm, u + 1)
                link(dve.tensor_tensor(s[:, t * P:(t + 1) * P], s[:, t * P:(t + 1) * P], const("causal"), ALU.add))
                dve.tensor_reduce(nmax[:, u:u + 1], s[:, 0:(t + 1) * P], AX.X, ALU.max, negate=True).then_inc(mx_ready, 1)
                if t and u % 16 == 1:
                    combine(t - 1)
            combine(NT - 1)
            for m in range(KD):
                for i in range(2):
                    tile_evacuated(dve, ("mg", m, i))
                for i in range(2):
                    g = A(24 + 2 * (m % 2) + i)
                    dve.wait_ge(filled, plan.at["mg", m, 2 + i] + 1)
                    link_evac(dve.tensor_tensor(g, g, bank[plan.bank(("mg", m, 2 + i))][:, :], ALU.mult), ("mg", m, 2 + i))
                dve.tensor_tensor(mix2(m), A(24 + 2 * (m % 2)), A(25 + 2 * (m % 2)), ALU.add).then_inc(mg_ready, 1)
            for m in range(KD):
                b = plan.bank(("w_o", m))
                dve.wait_ge(filled, plan.at["w_o", m] + 1)
                dve.tensor_tensor(xT[:, m, :], xT[:, m, :], bank[b][:, :], ALU.add).then_inc(evac[b], 1)
            norm_plain(3, "norm2_g_2")
            for m in range(KF):
                tile_evacuated(dve, ("gu", m, 0))
                if m >= 2:
                    dve.wait_ge(silu_ready, m - 1)
                conv(A(24 + m % 2), A(22 + m % 2), [col("ffn_conv_w_2", KF * j + m) for j in range(3)], col("ffn_conv_b_2", m), conv_ready)
                if m:
                    gated(m - 1)
            gated(KF - 1)
            for m in range(KD):
                dve.wait_ge(fo_mm, m + 1)
                dve.tensor_tensor(xT[:, m, :], xT[:, m, :], bank[m][:, :], ALU.add).then_inc(fo_sb, 1)

        @block.tensor
        def _(pe):
            mm = pe.matmul

            def turn(key, parts, rows=P):
                b = plan.bank(key)
                pe.wait_ge(evac[b], plan.turn(key))
                for c, x in enumerate(parts):
                    ins = pe.transpose(bank[b][0:rows, c * P:(c + 1) * P], x, ident)
                ins.then_inc(filled, 1)

            def fill(key, parts, cols=T):
                b = plan.bank(key)
                if plan.turn(key):
                    pe.wait_ge(evac[b], plan.turn(key))
                dst = bank[b][:, 0:cols]
                for i, (l, r) in enumerate(parts):
                    ins = mm(dst, l, r, start=(i == 0), stop=(i == len(parts) - 1))
                ins.then_inc(filled, 1)

            def mean_square(stage):
                for k in range(KD):
                    pe.wait_ge(sq_ready, stage * KD + k + 1)
                    ins = mm(bank[4][:, :], ones, hT[:, k, :], start=(k == 0), stop=(k == KD - 1))
                ins.then_inc(ss_done, 1)

            def sum_mod(n):
                pe.wait_ge(ada_used, n + 1)
                for j in range(4):
                    ins = mm(bank[5][:, 4 * n + j:4 * n + j + 1], acc[n % 2][:, j * P:(j + 1) * P], ones[:, 0:1], start=True, stop=True)
                ins.then_inc(mod_mm, 1)

            pe.wait_ge(cst_in, 16)
            mean_square(0)
            for n in range(4):
                sum_mod(n)
            later = 4
            for i in range(7):
                s = slot_of["win", i]
                width = WIN_CUTS[i + 1] - WIN_CUTS[i]
                w = ring[:, s * MAX_CHUNK:s * MAX_CHUNK + KD * width].rearrange("p (k n) -> p k n", k=KD)
                pe.wait_ge(slot_in[s], 16 * load_of["win", i])
                pe.wait_ge(h_ready, KD)
                if i < 6:
                    for j, m in enumerate(WIN_TILES[i]):
                        fill(("z", m), [(w[:, k, j * P:(j + 1) * P], hT[:, k, :]) for k in range(KD)])
                        if m >= 2 and m % 2 == 0 and later < 12 and m < NZ:
                            sum_mod(later)
                            later += 1
                else:
                    for t in range(NT):
                        fill(("v", t), [(hT[:, k, t * P:(t + 1) * P], w[:, k, :]) for k in range(KD)])
            while later < 12:
                sum_mod(later)
                later += 1

            pe.wait_ge(up_in, 48)
            pe.wait_ge(gates_lo, 2)
            for c in range(4):
                cs = slice(c * P, (c + 1) * P)
                fill(("wag", c, 0), [(up_wa[0:64, cs], zs(12)[0:64, :])])
                fill(("wag", c, 1), [(up_wa[64:128, cs], zs(12)[64:128, :])])
                fill(("wag", c, 2), [(up_g[:, cs], zs(13))])
            for c in range(4):
                pe.wait_ge(kk2_ready, c + 1)
                fill(("kk", c), [(head_ones, nrm[:, c, :])])
            for c in range(4):
                pe.wait_ge(rk_ready, c + 1)
                fill(("rk", c), [(head_ones, KR[:, c, 1, :])])
            pe.wait_ge(prep_done, 4)
            for k in range(NT):
                ks = slice(k * P, (k + 1) * P)
                for j, src in enumerate((lambda c: zs(8 + c)[:, ks], lambda c: ktT[:, c, ks], lambda c: btT[:, c, ks])):
                    key = ("tok", k, j)
                    b = plan.bank(key)
                    pe.wait_ge(evac[b], plan.turn(key))
                    for c in range(4):
                        ins = pe.transpose(bank[b][:, c * P:(c + 1) * P], src(c), ident)
                    ins.then_inc(filled, 1)

            def turn_y(k):
                pe.wait_ge(yn_ready, k + 1)
                turn(("yT", k), [yn[:, c * P:(c + 1) * P] for c in range(4)])
            for k in range(NT):
                ks = slice(k * P, (k + 1) * P)
                for h in range(NH):
                    hp, c = slice(HD * (h % 2), HD * (h % 2) + HD), h // 2
                    key = ("am", k, h)
                    b = plan.bank(key)
                    pe.wait_ge(evac[b], plan.turn(key))
                    rhs = KR[hp, c, :, ks]
                    mm(bank[b][:, 0:256], ktT[hp, c, ks], rhs, start=True, stop=True)
                    mm(bank[b][:, 256:512], btT[hp, c, ks], rhs, start=True, stop=True).then_inc(filled, 1)
                if k:
                    turn_y(k - 1)
                for i in (2 * k, 2 * k + 1):
                    pe.wait_ge(qk2_ready, i + 1)
                    fill(("sbn", i), [(head_ones, qk_sq(i))])
                for h in range(NH):
                    tile_evacuated(pe, ("am", k, h))
                for lv in range(7):
                    for g in range(2):
                        done = 1 if lv == 0 else 1 + (lv - 1) * 2 + g + 1
                        pe.wait_ge(x_sb, k * 13 + done)
                        pe.wait_ge(xt_sb, k * 15 + done)
                        for h in range(4 * g, 4 * g + 4):
                            ins = mm(bank[4 + g][:, (h % 4) * P:(h % 4 + 1) * P], AM[:, h, 2 * P:3 * P], X[:, h, :], start=True, stop=True)
                        ins.then_inc(t1_mm, 1)
                    for g in range(2):
                        pe.wait_ge(t1_sb, (k * 7 + lv) * 2 + g + 1)
                        if lv < 6:
                            for h in range(4 * g, 4 * g + 4):
                                ins = mm(bank[6 + g][:, (h % 4) * P:(h % 4 + 1) * P], XT[:, h, :], T1[:, h, :], start=True, stop=True)
                            ins.then_inc(xn_mm, 1)
                        for h in range(4 * g, 4 * g + 4):
                            ins = mm(bank[4 + g][:, (h % 4) * P:(h % 4 + 1) * P], T1[:, h, :], XT[:, h, :], start=True, stop=True)
                        ins.then_inc(xt_mm, 1)
                pe.wait_ge(s_sb, k + 1)
                tile_evacuated(pe, ("tok", k, 2))
                for c in range(4):
                    cs = slice(c * P, (c + 1) * P)
                    mm(bank[6][:, cs], KR[:, c, 0, ks], S_sc[:, cs], start=True, stop=True)
                    for h in (2 * c, 2 * c + 1):
                        hs = slice(h * HD, (h + 1) * HD)
                        ins = mm(bank[6][:, hs], AM[:, h, 0:P], v_tok[:, k, hs], start=False, stop=True, skip_group_check=True)
                ins.then_inc(w_mm, 1)
                pe.wait_ge(w_sb, k + 1)
                pe.wait_ge(xt_sb, (k + 1) * 15)
                for h in range(NH):
                    hs = slice(h * HD, (h + 1) * HD)
                    ins = mm(bank[7][:, hs], XT[:, h, :], W_sb[:, hs], start=True, stop=True)
                ins.then_inc(u_mm, 1)
                pe.wait_ge(u_sb, k + 1)
                for c in range(4):
                    cs = slice(c * P, (c + 1) * P)
                    mm(bank[4][:, cs], KR[:, c, 1, ks], S_sc[:, cs], start=True, stop=True)
                    for h in (2 * c, 2 * c + 1):
                        hs = slice(h * HD, (h + 1) * HD)
                        mm(bank[4][:, hs], AM[:, h, P:2 * P], v_tok[:, k, hs], start=False, stop=True, skip_group_check=True)
                        ins = mm(bank[4][:, hs], AM[:, h, 3 * P:4 * P], U_sb[:, hs], start=False, stop=True, skip_group_check=True)
                ins.then_inc(y_mm, 1)
                for c in range(4):
                    cs = slice(c * P, (c + 1) * P)
                    mm(bank[5][:, cs], kt_tok[:, k, cs], v_tok[:, k, cs], start=True, stop=False)
                    ins = mm(bank[5][:, cs], bt_tok[:, k, cs], U_sb[:, cs], start=False, stop=True)
                ins.then_inc(s_mm, 1)
            turn_y(NT - 1)
            pe.wait_ge(qkn_ready, 8)

            def logits(h):
                hp, c = slice(HD * (h % 2), HD * (h % 2) + HD), h // 2
                if h >= 2:
                    pe.wait_ge(wt_ready, NT * (h - 1))
                for kt in (0, 1, 3, 2):
                    ins = mm(sb_logits(h, kt), k_sb[hp, c, kt * P:(kt + 1) * P], q_sb[hp, c, kt * P:T], start=(kt != 3), stop=True,
                       skip_group_check=True)
                ins.then_inc(l_mm, 1)

            def sums(h):
                for kt in range(NT - 1, -1, -1):
                    pe.wait_ge(sp_ready, h * NT + NT)
                    dst = sb_logits(h, kt)
                    ins = mm(dst, const("neg_tri"), sb_e(h, kt), start=False, stop=True, skip_group_check=True)
                    for k2 in range(kt + 1, NT):
                        ins = mm(dst[:, (k2 - kt) * P:], const("neg_ones"), sb_e(h, k2), start=False, stop=True, skip_group_check=True)
                    ins.then_inc(r_mm, 1)

            def values(h):
                hs = slice(h * HD, (h + 1) * HD)
                pe.wait_ge(wt_ready, NT * (h + 1))
                if h >= 2:
                    pe.wait_ge(o_sb, h - 1)
                for t in range(NT):
                    for kt in range(t + 1):
                        ins = mm(sb_out(h)[:, t * HD:(t + 1) * HD], sb_w(h, kt)[:, (t - kt) * P:(t - kt + 1) * P], v_sb[:, kt, hs],
                                 start=(kt == 0), stop=(kt == t), skip_group_check=True)
                ins.then_inc(o_mm, 1)

            for i in range(8):
                tile_evacuated(pe, ("sbn", i))
            pe.wait_ge(s_sb, NT + 1)
            tile_evacuated(pe, ("yT", NT - 1))
            logits(0)
            for h in range(NH):
                if h + 1 < NH:
                    logits(h + 1)
                sums(h)
                if h:
                    values(h - 1)
            values(NH - 1)
            for t in range(NT):
                key = ("oT", t)
                b = plan.bank(key)
                pe.wait_ge(on_ready, t + 1)
                pe.wait_ge(evac[b], plan.turn(key))
                for c in range(4):
                    ins = pe.transpose(bank[b][:, c * P:(c + 1) * P], o_tok[:, t, c * P:(c + 1) * P], ident)
                ins.then_inc(filled, 1)
            pe.wait_ge(wo_in, 16)
            pe.wait_ge(mix_ready, 4)
            for t in range(NT):
                tile_evacuated(pe, ("oT", t))
            w = ring[:, 0:KD * D].rearrange("p (k n) -> p k n", k=KD)
            for m in range(KD):
                fill(("wo", m), [(w[:, k, m * P:(m + 1) * P], mixT(k)) for k in range(KD)])

            mean_square(1)
            pe.wait_ge(h_ready, 2 * KD)
            for t in range(NT):
                ts = slice(t * P, (t + 1) * P)
                for i in range(2):
                    turn(("ht", t, i), [hT[:, 4 * i + c, ts] for c in range(4)])
            pe.wait_ge(rw_in, 16)
            for t in range(NT):
                ts = slice(t * P, (t + 1) * P)
                fill(("lg", t), [(hT[:, k, ts], router_w[:, k, :]) for k in range(KD)], cols=EXPERTS)
            pe.wait_ge(route_ready, 1)
            for t in range(NT):
                fill(("pos", t), [(ones, SEL[:, i, :]) for i in range(t)] + [(const("strict"), SEL[:, t, :])], cols=EXPERTS)
            fill(("cnt",), [(ones, SEL[:, t, :]) for t in range(NT)], cols=EXPERTS)
            b = plan.bank(("gateT",))
            pe.wait_ge(evac[b], plan.turn(("gateT",)))
            for t in range(NT):
                ins = pe.transpose(bank[b][0:EXPERTS, t * P:(t + 1) * P], GATE[:, t, :], ident)
            ins.then_inc(filled, 1)
            for t in range(NT):
                tile_evacuated(pe, ("pos", t))
            tile_evacuated(pe, ("cnt",))
            tile_evacuated(pe, ("gateT",))
            pe.sem_inc(idx_mm, 1)
            pe.sem_inc(gx_mm, 1)
            pe.sem_inc(aT_mm, 1)
            pe.wait_ge(npass_ready, 1)
            passes = pe.value_load(n_pass[0:1, 0:1], min_val=1, max_val=4)

            def number_slots(j, n):
                pe.wait_ge(oh_ready, j * LOOKS + (n + 1))
                for t in range(NT):
                    ins = mm(bank[4][:, 0:2], OH[:, t, :], token[:, t, :], start=(t == 0), stop=(t == NT - 1))
                ins.then_inc(idx_mm, 1)

            def turn_rows(j, n, looks):
                pe.wait_ge(rows_in, j * (16 * LOOKS) + n * 16 + 16)
                pe.wait_ge(idx_sb, j * LOOKS + looks)
                for c in range(KD):
                    ins = pe.transpose(bank[4 + c // 4][:, (c % 4) * P:(c % 4 + 1) * P], XR[:, c * P:(c + 1) * P], ident)
                ins.then_inc(gx_mm, 1)

            def hidden(j, e):
                it = j * EXPERTS + e
                pe.wait_ge(gx_sb, j * TURNS + (e + 1))
                pe.wait_ge(lin_ready, it + 1)
                for k in range(KD):
                    pe.wait_ge(w1_in[k], it * 16 + 16)
                    for n in range(4):
                        ins = mm(bank[n][:, :], XG[:, k, :], w1_slot(k)[:, n * T:(n + 1) * T], start=(k == 0), stop=(k == KD - 1))
                    ins.then_inc(w1_free, 1)
                    if k == 3:
                        pe.wait_ge(aT_sb, it + 1)
                        number_slots(j, e + 2)
                turn_rows(j, e + 1, e + 3)

            def turn_activations(j, e):
                pe.wait_ge(act_ready, j * EXPERTS + (e + 1))
                pe.wait_ge(gx_sb, j * TURNS + (e + 2))
                for c in range(KD):
                    ins = pe.transpose(bank[4 + c // 4][:, (c % 4) * P:(c % 4 + 1) * P], G[:, c * P:(c + 1) * P], ident)
                ins.then_inc(aT_mm, 1)

            def rows(j, e):
                it = j * EXPERTS + e
                pe.wait_ge(aT_sb, it + 2)
                pe.wait_ge(ye_sb, it + 1)
                for k in range(KD):
                    pe.wait_ge(w2_in[k], it * 16 + 16)
                    for n in range(2):
                        ins = mm(bank[6 + n][:, :], aT2k[:, k, :], w2_slot(k)[:, n * T:(n + 1) * T], start=(k == 0), stop=(k == KD - 1))
                    ins.then_inc(w2_free, 1)
            with pe.Fori(0, passes) as j:
                pe.wait_ge(aT_sb, j * EXPERTS + 1)
                number_slots(j, 0)
                turn_rows(j, 0, 1)
                pe.wait_ge(gx_sb, j * TURNS + 1)
                number_slots(j, 1)
                hidden(j, 0)
                turn_activations(j, 0)
                with pe.Fori(0, EXPERTS - 1) as e:
                    hidden(j, e + 1)
                    rows(j, e)
                    turn_activations(j, e + 1)
                rows(j, EXPERTS - 1)
                pe.wait_ge(b2_in, 16)
                pe.wait_ge(ye_sb, j * EXPERTS + (EXPERTS + 1))
                for m in range(KD):
                    mm(bank[m][:, :], B2[:, m * P:(m + 1) * P], GATE_T, start=True, stop=True)
                for t in range(NT):
                    pe.wait_ge(sum_ready, j * NT + (t + 1))
                    total = YR[t * TOP_K]
                    for m in range(KD):
                        ins = mm(bank[m][:, t * P:(t + 1) * P], total[:, m * P:(m + 1) * P], ident, start=False, stop=True,
                                 skip_group_check=True)
                        if m == KD - 1 or t == NT - 1:
                            ins.then_inc(mix_mm, 1)

            pe.wait_ge(x2_ready, 1)
            mean_square(2)
            pe.wait_ge(h_ready, 3 * KD)
            loaded2(pe, "q2")
            w = slot2("q2", KD, 512)
            for t in range(NT):
                fill(("q2", t), [(hT[:, k, t * P:(t + 1) * P], w[:, k, :]) for k in range(KD)])
            loaded2(pe, "kv2")
            w = slot2("kv2", KD, 512)
            for t in range(NT):
                fill(("kv2", t), [(hT[:, k, t * P:(t + 1) * P], w[:, k, :]) for k in range(KD)])
            loaded2(pe, "kc")
            w = slot2("kc", KD, 280)
            fill(("kc",), [(w[:, k, 0:P], hT[:, k, :]) for k in range(KD)])
            fill(("vc",), [(w[:, k, P:2 * P], hT[:, k, :]) for k in range(KD)])
            for t in range(NT):
                fill(("g2", t), [(hT[:, k, t * P:(t + 1) * P], w[:, k, 256:280]) for k in range(KD)], cols=24)
            for name in ("ac", "ax", "ab"):
                loaded2(pe, name)
                w = slot2(name, KD, 512)
                for c in range(4):
                    fill((name, c), [(w[:, k, c * P:(c + 1) * P], hT[:, k, :]) for k in range(KD)])
            pe.wait_ge(cw_in, 16 * 6)
            tile_evacuated(pe, ("kc",))
            tile_evacuated(pe, ("vc",))
            for j, (src, pe_name) in enumerate(((kcT, "cmp_k_pe_2"), (vcT, "cmp_v_pe_2"))):
                for g in range(2):
                    key = ("hid", j, g)
                    b = plan.bank(key)
                    pe.wait_ge(evac[b], plan.turn(key))
                    gp = slice(g * HD, (g + 1) * HD)
                    for i in range(CMP_BLOCK):
                        ins = mm(bank[b][0:HD, 0:N_CMP], cmp_w1[j][gp, i, :], src[gp, i:i + CMP_STRIDE * (N_CMP - 1) + 1:CMP_STRIDE],
                                 start=(i == 0), stop=(i == CMP_BLOCK - 1))
                    if g == 0:
                        for i in range(CMP_BLOCK):
                            at = VEC_AT[pe_name] + i
                            ins = mm(bank[b][0:HD, 64:65], cmp_w1[j][0:HD, i, :], vec[0:HD, at:at + 1], start=(i == 0), stop=(i == CMP_BLOCK - 1))
                    ins.then_inc(filled, 1)
            key = ("kvc",)
            b = plan.bank(key)
            pe.wait_ge(evac[b], plan.turn(key))
            for j in range(2):
                for g in range(2):
                    tile_evacuated(pe, ("hid", j, g))
                    ins = mm(bank[b][0:N_CMP, j * P + g * HD:j * P + (g + 1) * HD], hid[j][:, g, 0:N_CMP], cmp_w2[0:HD, j * HD:(j + 1) * HD],
                             start=True, stop=True)
            ins.then_inc(filled, 1)
            key = ("kcT",)
            b = plan.bank(key)
            pe.wait_ge(evac[b], plan.turn(key))
            pe.wait_ge(kc_ready, 1)
            pe.transpose(bank[b][:, 0:N_CMP], kcn, ident[0:N_CMP, 0:N_CMP]).then_inc(filled, 1)
            for t in range(NT):
                pe.wait_ge(q_ready, t + 1)
                turn(("qkT", t), [q_tok[:, t, c * P:(c + 1) * P] for c in range(4)])
            for t in range(NT):
                pe.wait_ge(k_ready, t + 1)
                turn(("kkT", t), [kv_tok[:, t, 2 * b * P:(2 * b + 1) * P] for b in range(2)])
            tile_evacuated(pe, ("kcT",))
            for t in range(NT):
                tile_evacuated(pe, ("qkT", t))
                tile_evacuated(pe, ("kkT", t))

            def head(h):
                return h % 4, slice(HD * (h // 4), HD * (h // 4) + HD)
            for t in range(NT):
                ts = slice(t * P, (t + 1) * P)
                for g in range(2):
                    key = ("cs", t, g)
                    b = plan.bank(key)
                    pe.wait_ge(evac[b], plan.turn(key))
                    for h in range(4 * g, 4 * g + 4):
                        c, hp = head(h)
                        ins = mm(bank[b][:, c * 32:c * 32 + N_CMP], QT[hp, c, ts], KcT[hp, :], start=True, stop=True)
                    ins.then_inc(filled, 1)
                pe.wait_ge(cp_ready, t + 1)
                for i in range(2):
                    turn(("cT", t, i), [crow[:, (4 * i + c) * N_CMP:(4 * i + c + 1) * N_CMP] for c in range(4)], rows=N_CMP)
                for i in range(2):
                    tile_evacuated(pe, ("cT", t, i))
                if t >= 2:
                    pe.wait_ge(co_sb, t - 1)
                for h in range(NH):
                    ins = mm(bank[4 + t % 2][:, h * HD:(h + 1) * HD], cPT[0:N_CMP, h, :], v_cmp[:, (h // 4) * HD:(h // 4 + 1) * HD],
                             start=True, stop=True)
                ins.then_inc(co_mm, 1)
            pe.wait_ge(co_sb, NT)

            def scores(u):
                t, h, j = u // 16, u % 16 // 2, u % 2
                c, hp = head(h)
                if u >= 4:
                    pe.wait_ge(p_ready, u - 3)
                mm(s_bank(u)[:, 0:(t + 1) * P], QT[hp, c, t * P:(t + 1) * P], (KselT, KwinT)[j][hp, 0:(t + 1) * P], start=True, stop=True)\
                    .then_inc(s2_mm, 1)

            def turn_weights(u):
                t = u // 16
                pe.wait_ge(p_ready, u + 1)
                if u >= 2:
                    pe.wait_ge(pt_sb, u - 1)
                for k in range(t + 1):
                    ins = pe.transpose(bank[4 + u % 2][:, k * P:(k + 1) * P], Pb[u % 2][:, k * P:(k + 1) * P], ident)
                ins.then_inc(pt_mm, 1)

            def weigh(u):
                t, h, j = u // 16, u % 16 // 2, u % 2
                if u % 16 < 2 and t:
                    pe.wait_ge(yb_ready, t)
                pe.wait_ge(pt_sb, u + 1)
                v = (2 * j + 1) * P + (h // 4) * HD
                for k in range(t + 1):
                    ins = mm(bank[j][:, h * HD:(h + 1) * HD], PTb[u % 2][:, k * P:(k + 1) * P], kv_tok[:, k, v:v + HD],
                             start=(k == 0), stop=(k == t))
                ins.then_inc(o2_mm, 1)
            scores(0)
            scores(1)
            for u in range(64):
                if u + 2 < 64:
                    scores(u + 2)
                if u:
                    weigh(u - 1)
                turn_weights(u)
            weigh(63)
            pe.wait_ge(yb_ready, NT)
            for t in range(NT):
                turn(("ybT", t), [yb_tok[:, t, c * P:(c + 1) * P] for c in range(4)])
            for t in range(NT):
                tile_evacuated(pe, ("ybT", t))
            for name in ("wa", "wb"):
                loaded2(pe, name)
            wa, wb = slot2("wa", 4, D), slot2("wb", 4, D)
            for m in range(KD):
                if m % 2 == 0:
                    loaded2(pe, ("mg", m // 2))
                w = slot2(("mg", m // 2), KD, 512)
                at = (m % 2) * P
                fill(("mg", m, 0), [(w[:, k, at:at + P], hT[:, k, :]) for k in range(KD)])
                fill(("mg", m, 1), [(w[:, k, 256 + at:256 + at + P], hT[:, k, :]) for k in range(KD)])
                fill(("mg", m, 2), [(wa[:, k, m * P:(m + 1) * P], yaT[:, k, :]) for k in range(4)])
                fill(("mg", m, 3), [(wb[:, k, m * P:(m + 1) * P], ybT[:, k, :]) for k in range(4)])
            for j in range(2):
                loaded2(pe, ("w_o", j))
            pe.wait_ge(mg_ready, KD)
            for m in range(KD):
                fill(("w_o", m), [(slot2(("w_o", k // 4), 4, D)[:, k % 4, m * P:(m + 1) * P], mix2(k)) for k in range(KD)])
            mean_square(3)
            for m in range(KF):
                if m % 2 == 0:
                    loaded2(pe, ("fi", m // 2))
                pe.wait_ge(h_ready, 4 * KD)
                w = slot2(("fi", m // 2), KD, 512)
                at = (m % 2) * P
                for i in range(2):
                    fill(("gu", m, i), [(w[:, k, 256 * i + at:256 * i + at + P], hT[:, k, :]) for k in range(KD)])
            for m in range(KF):
                tile_evacuated(pe, ("gu", m, 1))
            for k in range(KF):
                if k % 4 == 0:
                    loaded2(pe, ("fo", k // 4))
                w = slot2(("fo", k // 4), min(4, KF - 4 * (k // 4)), D)
                for m in range(KD):
                    ins = mm(bank[m][:, :], w[:, k % 4, m * P:(m + 1) * P], actT(k), start=(k == 0), stop=(k == KF - 1))
                    if k == KF - 1:
                        ins.then_inc(fo_mm, 1)


def kernel(**inputs):
    import concourse.bacc as _bacc
    from concourse.bass_utils import run_bass_kernel_spmd as _run

    def cols(x):
        return np.asarray(x).reshape(-1, P).T

    def twice(x):
        return np.concatenate([x, x], 0)

    i = inputs
    v = dict(c=cols(i["c"]), norm1_g=cols(i["norm1_g"]), norm2_g=cols(i["norm2_g"]), ada_b=cols(i["ada_b"]),
             shift_mu=cols(i["shift_mu"]), decay_w0=cols(i["decay_w0"]), iclr_a0=cols(i["iclr_a0"]), k_k=cols(i["k_k"]),
             k_a=cols(i["k_a"]), r_k=cols(i["r_k"]), lnx_w=cols(i["lnx_w"]), lnx_b=cols(i["lnx_b"]),
             sb_out_g=cols(i["sb_out_g"]), q_norm_g=twice(i["q_norm_g"].T), k_norm_g=twice(i["k_norm_g"].T),
             norm1_g_2=cols(i["norm1_g_2"]), norm2_g_2=cols(i["norm2_g_2"]), conv_a_w_2=cols(i["conv_a_w_2"]),
             ffn_conv_w_2=cols(i["ffn_conv_w_2"]), ffn_conv_b_2=cols(i["ffn_conv_b_2"]),
             cmp_k_pe_2=twice(i["cmp_k_pe_2"][0].T), cmp_v_pe_2=twice(i["cmp_v_pe_2"][0].T))
    for name in ROW_COLS:
        v[name] = np.tile(np.asarray(i[name]).reshape(1, -1), (P, 1))
    vecs = np.ascontiguousarray(np.concatenate([v[n] for n in VEC_AT], 1))
    arrays = dict(vecs=vecs, consts=constants(),
                  xT=np.ascontiguousarray(i["x"][0].T.reshape(KD, P, T).transpose(1, 0, 2)))
    arrays["positions"] = np.ascontiguousarray(np.asarray(i["positions_2"]).reshape(NT, P).T)
    for name in ("decay_up", "iclr_up", "gate_up", "ada_w", "w_in", "w_out", "router_w", "exp_w1", "exp_b1", "exp_w2", "exp_b2",
                 "w_in_2", "w_a_out_2", "w_b_out_2", "w_o_2", "w_ffn_in_2", "w_ffn_out_2", "cmp_k_w1_2", "cmp_k_w2_2",
                 "cmp_v_w1_2", "cmp_v_w2_2"):
        arrays[name] = np.ascontiguousarray(i[name])
    nc = _bacc.Bacc("TRN2", target_bir_lowering=False, num_devices=1)
    a = {n: nc.dram_tensor(f"in_{n}", x.shape, mybir.dt.from_np(x.dtype), kind="ExternalInput").ap() for n, x in arrays.items()}
    out = nc.dram_tensor("out_0_dram", (D, T), F32, kind="ExternalOutput").ap()
    program(nc, a, out)
    r = _run(nc, [{f"in_{n}": x for n, x in arrays.items()}], core_ids=[0])
    return np.ascontiguousarray(r.results[0]["out_0_dram"].T)[None]
```
